# Optimizing a Trainium2 kernel written in Bass

```python
import math
import jax, jax.numpy as jnp
from jax import lax
import numpy as np

D_MODEL = 1024
BATCH = 1
SEQ = 256
DEPTH = 2

N_MIXERS = 2
N_POOL_LAYERS = (DEPTH + 1) // 2
N_DN_LAYERS = DEPTH // 2

RMS_EPS = 1e-6

POOL_WINDOWS = (2, 4, 8, 16)
POOL_GROUPS = len(POOL_WINDOWS)
POOL_GROUP_DIM = D_MODEL // POOL_GROUPS

DN_HEAD_DIM = 128
DN_HEADS = D_MODEL // DN_HEAD_DIM
DN_KEY_DIM = DN_HEADS * DN_HEAD_DIM
DN_CONV = 4
DN_CHUNK = 64
DN_IN_DIM = 4 * DN_KEY_DIM + 2 * DN_HEADS

DENSE_FF = 2816
N_EXPERTS = 8
TOP_K = 2
EXPERT_FF = 3584


def rmsnorm(x, g):
    x32 = x.astype(jnp.float32)
    y = x32 * lax.rsqrt(jnp.mean(x32 * x32, axis=-1, keepdims=True) + RMS_EPS)
    return (y * g.astype(jnp.float32)).astype(x.dtype)

def l2norm(x):
    return x * lax.rsqrt(jnp.sum(x * x, axis=-1, keepdims=True) + RMS_EPS)

def swiglu(x, w_gate, w_up, w_down):
    return (jax.nn.silu(x @ w_gate) * (x @ w_up)) @ w_down

def pool_mixer(h, w_in, w_group, scale):
    b, s, d = h.shape
    u = (h @ w_in).reshape(b, s, POOL_GROUPS, POOL_GROUP_DIM).astype(jnp.float32)
    csum = jnp.cumsum(u, axis=1)
    pos = jnp.arange(1, s + 1, dtype=jnp.float32)[:, None]
    outs = []
    for gi, w in enumerate(POOL_WINDOWS):
        c = csum[:, :, gi]
        c_prev = jnp.pad(c, ((0, 0), (w, 0), (0, 0)))[:, :s]
        cnt = jnp.minimum(pos, float(w))
        outs.append((c - c_prev) / cnt - u[:, :, gi])
    m = jnp.stack(outs, axis=2).astype(h.dtype)
    y = jnp.einsum('bsgc,gce->bsge', m, w_group).reshape(b, s, d)
    return y * scale

def causal_depthwise_conv(x, w):
    k, c = w.shape
    return lax.conv_general_dilated(
        x, w[:, None, :], window_strides=(1,), padding=[(k - 1, 0)],
        dimension_numbers=('NWC', 'WIO', 'NWC'), feature_group_count=c)

def gated_delta_rule_chunked(q, k, v, beta, g):
    b, s, h, dk = q.shape
    dv = v.shape[-1]
    c = DN_CHUNK
    n = s // c

    def to_chunks(t):
        t = t.reshape((b, n, c, h) + t.shape[3:])
        return jnp.moveaxis(t, 3, 1)

    q, k, v, beta, g = (to_chunks(t) for t in (q, k, v, beta, g))
    gc = jnp.cumsum(g, axis=-1)
    causal = jnp.tril(jnp.ones((c, c), dtype=bool))
    strict = jnp.tril(jnp.ones((c, c), dtype=bool), -1)
    decay = jnp.exp(jnp.where(causal, gc[..., :, None] - gc[..., None, :], -jnp.inf))

    k_beta = k * beta[..., None]
    v_beta = v * beta[..., None]
    a = jnp.einsum('bhnid,bhnjd->bhnij', k_beta, k) * decay
    a = jnp.where(strict, a, 0.0) + jnp.eye(c, dtype=a.dtype)
    u = lax.linalg.triangular_solve(a, v_beta, left_side=True, lower=True, unit_diagonal=True)
    w = lax.linalg.triangular_solve(a, k_beta * jnp.exp(gc)[..., None],
                                    left_side=True, lower=True, unit_diagonal=True)
    qk = jnp.einsum('bhnid,bhnjd->bhnij', q, k) * decay

    xs = tuple(jnp.moveaxis(t, 2, 0) for t in (q, k, u, w, qk, gc))

    def step(state, inp):
        q_c, k_c, u_c, w_c, qk_c, gc_c = inp
        v_new = u_c - jnp.einsum('bhck,bhkv->bhcv', w_c, state)
        o = (jnp.einsum('bhck,bhkv->bhcv', q_c * jnp.exp(gc_c)[..., None], state)
             + jnp.einsum('bhij,bhjv->bhiv', qk_c, v_new))
        g_last = gc_c[..., -1]
        k_dec = k_c * jnp.exp(g_last[..., None] - gc_c)[..., None]
        state = state * jnp.exp(g_last)[..., None, None] + jnp.einsum('bhck,bhcv->bhkv', k_dec, v_new)
        return state, o

    s0 = jnp.zeros((b, h, dk, dv), jnp.float32)
    _, o = lax.scan(step, s0, xs)
    return jnp.transpose(o, (1, 0, 3, 2, 4)).reshape(b, s, h, dv)

def deltanet_mixer(h, w_in, conv_w, a_log, dt_bias, norm_g, w_out):
    b, s, _ = h.shape
    kd = DN_KEY_DIM
    proj = h @ w_in
    qkv = proj[..., :3 * kd]
    z = proj[..., 3 * kd:4 * kd]
    b_logit = proj[..., 4 * kd:4 * kd + DN_HEADS].astype(jnp.float32)
    a_in = proj[..., 4 * kd + DN_HEADS:].astype(jnp.float32)
    qkv = jax.nn.silu(causal_depthwise_conv(qkv, conv_w)).astype(jnp.float32)
    q, k, v = jnp.split(qkv, 3, axis=-1)
    q = l2norm(q.reshape(b, s, DN_HEADS, DN_HEAD_DIM)) * (DN_HEAD_DIM ** -0.5)
    k = l2norm(k.reshape(b, s, DN_HEADS, DN_HEAD_DIM))
    v = v.reshape(b, s, DN_HEADS, DN_HEAD_DIM)
    beta = jax.nn.sigmoid(b_logit)
    g = -jnp.exp(a_log.astype(jnp.float32)) * jax.nn.softplus(a_in + dt_bias.astype(jnp.float32))
    o = gated_delta_rule_chunked(q, k, v, beta, g)
    o = o * lax.rsqrt(jnp.mean(o * o, axis=-1, keepdims=True) + RMS_EPS) * norm_g.astype(jnp.float32)
    o = o * jax.nn.silu(z.astype(jnp.float32)).reshape(b, s, DN_HEADS, DN_HEAD_DIM)
    return o.reshape(b, s, kd).astype(h.dtype) @ w_out

def moe_ffn(h, router_w, router_b, w_gate, w_up, w_down):
    b, s, d = h.shape
    t = h.reshape(b * s, d)
    logits = (t @ router_w).astype(jnp.float32) + router_b.astype(jnp.float32)
    top_vals, top_idx = lax.top_k(logits, TOP_K)
    top_w = jax.nn.softmax(top_vals, axis=-1)
    gates = jnp.sum(jax.nn.one_hot(top_idx, N_EXPERTS, dtype=jnp.float32) * top_w[..., None], axis=1)
    out = jnp.zeros((b * s, d), jnp.float32)
    for e in range(N_EXPERTS):
        y = swiglu(t, w_gate[e], w_up[e], w_down[e]).astype(jnp.float32)
        out = out + gates[:, e:e + 1] * y
    return out.astype(h.dtype).reshape(b, s, d)

def first_inputs(seed: int = 0) -> dict:
    key = jax.random.key(seed)
    ks = jax.random.split(key, 24)
    f32 = jnp.float32
    D = D_MODEL
    NP, ND = N_POOL_LAYERS, N_DN_LAYERS

    def nrm(k, shape, fan_in):
        return jax.random.normal(k, shape, f32) * (fan_in ** -0.5)

    def gain(k, shape):
        return 1.0 + 0.05 * jax.random.normal(k, shape, f32)

    dt = jnp.exp(jax.random.uniform(ks[10], (ND, DN_HEADS), f32,
                                    minval=math.log(1e-3), maxval=math.log(1e-1)))
    return {
        "x": jax.random.normal(ks[0], (BATCH, SEQ, D), f32),
        "norm_mix_g": gain(ks[1], (DEPTH, D)),
        "norm_ffn_g": gain(ks[2], (DEPTH, D)),
        "pool_w_in": nrm(ks[3], (NP, D, D), D),
        "pool_w_group": nrm(ks[4], (NP, POOL_GROUPS, POOL_GROUP_DIM, POOL_GROUP_DIM), POOL_GROUP_DIM),
        "pool_scale": gain(ks[5], (NP, D)),
        "dn_w_in": nrm(ks[6], (ND, D, DN_IN_DIM), D),
        "dn_conv_w": nrm(ks[7], (ND, DN_CONV, 3 * DN_KEY_DIM), DN_CONV),
        "dn_a_log": jnp.log(jax.random.uniform(ks[8], (ND, DN_HEADS), f32, minval=1.0, maxval=16.0)),
        "dn_dt_bias": dt + jnp.log(-jnp.expm1(-dt)),
        "dn_norm_g": gain(ks[9], (ND, DN_HEAD_DIM)),
        "dn_w_out": nrm(ks[11], (ND, DN_KEY_DIM, D), DN_KEY_DIM),
        "ffn_w_gate": nrm(ks[12], (NP, D, DENSE_FF), D),
        "ffn_w_up": nrm(ks[13], (NP, D, DENSE_FF), D),
        "ffn_w_down": nrm(ks[14], (NP, DENSE_FF, D), DENSE_FF),
        "moe_router_w": nrm(ks[15], (ND, D, N_EXPERTS), D),
        "moe_router_b": 0.01 * jax.random.normal(ks[16], (ND, N_EXPERTS), f32),
        "moe_w_gate": nrm(ks[17], (ND, N_EXPERTS, D, EXPERT_FF), D),
        "moe_w_up": nrm(ks[18], (ND, N_EXPERTS, D, EXPERT_FF), D),
        "moe_w_down": nrm(ks[19], (ND, N_EXPERTS, EXPERT_FF, D), EXPERT_FF),
        "final_norm_g": gain(ks[20], (D,)),
    }

def first_block(x, norm_mix_g, norm_ffn_g, pool_w_in, pool_w_group, pool_scale,
              dn_w_in, dn_conv_w, dn_a_log, dn_dt_bias, dn_norm_g, dn_w_out,
              ffn_w_gate, ffn_w_up, ffn_w_down,
              moe_router_w, moe_router_b, moe_w_gate, moe_w_up, moe_w_down,
              final_norm_g):
    h = x
    for i in range(DEPTH):
        j = i // N_MIXERS
        hn = rmsnorm(h, norm_mix_g[i])
        if i % N_MIXERS == 0:
            h = h + pool_mixer(hn, pool_w_in[j], pool_w_group[j], pool_scale[j])
        else:
            h = h + deltanet_mixer(hn, dn_w_in[j], dn_conv_w[j], dn_a_log[j], dn_dt_bias[j],
                                   dn_norm_g[j], dn_w_out[j])
        hn = rmsnorm(h, norm_ffn_g[i])
        if i % 2 == 0:
            h = h + swiglu(hn, ffn_w_gate[j], ffn_w_up[j], ffn_w_down[j])
        else:
            h = h + moe_ffn(hn, moe_router_w[j], moe_router_b[j], moe_w_gate[j], moe_w_up[j], moe_w_down[j])
    return rmsnorm(h, final_norm_g)


DEPTH_2 = 1

MEM_LEN = 256
HD = 64
SB_HEADS = 8
FOX_HEADS = 8
MEM_HEADS = 4
MEM_HD = 128
D_SB = SB_HEADS * HD
D_FOX = FOX_HEADS * HD
D_MEM = MEM_HEADS * MEM_HD
N_BRANCH = 3
D_FF = 4 * D_MODEL
BLOCK_Q = 128
EPS = 1e-6
NEG_INF = -1e30
SPLITS = (D_SB, D_SB, D_SB, D_FOX, D_FOX, D_FOX, FOX_HEADS, D_MEM, N_BRANCH * D_MODEL)
D_IN = sum(SPLITS)


def split_columns(t, sizes):
    pieces = []
    start = 0
    for n in sizes:
        pieces.append(t[..., start:start + n])
        start += n
    return pieces

def rmsnorm_2(x, g):
    xf = x.astype(jnp.float32)
    y = xf * lax.rsqrt(jnp.mean(xf * xf, axis=-1, keepdims=True) + EPS)
    return (y * g.astype(jnp.float32)).astype(x.dtype)

def to_heads(t, n, d):
    b, s, _ = t.shape
    return t.reshape(b, s, n, d).transpose(0, 2, 1, 3)

def from_heads(t):
    b, h, s, d = t.shape
    return t.transpose(0, 2, 1, 3).reshape(b, s, h * d)

def stick_breaking_attention(q, k, v):
    s_len = q.shape[2]
    scale = HD ** -0.5
    outs = []
    for i in range(s_len // BLOCK_Q):
        q0 = i * BLOCK_Q
        kend = q0 + BLOCK_Q
        z = jnp.einsum('bhtd,bhsd->bhts', q[:, :, q0:kend], k[:, :, :kend]).astype(jnp.float32) * scale
        t_idx = q0 + jnp.arange(BLOCK_Q)[:, None]
        s_idx = jnp.arange(kend)[None, :]
        strict = s_idx < t_idx
        log_rem = jnp.where(strict, jax.nn.log_sigmoid(-z), 0.0)
        after = lax.cumsum(log_rem, axis=3, reverse=True) - log_rem
        w = jnp.where(strict, jnp.exp(jax.nn.log_sigmoid(z) + after), 0.0)
        outs.append(jnp.einsum('bhts,bhsd->bhtd', w.astype(v.dtype), v[:, :, :kend]))
    return jnp.concatenate(outs, axis=2)

def forgetting_attention(q, k, v, log_f):
    s_len = q.shape[2]
    scale = HD ** -0.5
    F = lax.cumsum(log_f.astype(jnp.float32), axis=2)
    outs = []
    for i in range(s_len // BLOCK_Q):
        q0 = i * BLOCK_Q
        kend = q0 + BLOCK_Q
        z = jnp.einsum('bhtd,bhsd->bhts', q[:, :, q0:kend], k[:, :, :kend]).astype(jnp.float32) * scale
        z = z + F[:, :, q0:kend, None] - F[:, :, None, :kend]
        causal = jnp.arange(kend)[None, :] <= (q0 + jnp.arange(BLOCK_Q)[:, None])
        p = jax.nn.softmax(jnp.where(causal, z, NEG_INF), axis=-1)
        outs.append(jnp.einsum('bhts,bhsd->bhtd', p.astype(v.dtype), v[:, :, :kend]))
    return jnp.concatenate(outs, axis=2)

def memory_attention(q, k, v):
    z = jnp.einsum('bhtd,bhmd->bhtm', q, k).astype(jnp.float32) * (MEM_HD ** -0.5)
    p = jax.nn.softmax(z, axis=-1)
    return jnp.einsum('bhtm,bhmd->bhtd', p.astype(v.dtype), v)

def second_inputs(seed: int = 0) -> dict:
    key = jax.random.key(seed)
    ks = jax.random.split(key, 20)

    def w(k, shape, fan_in):
        return jax.random.normal(k, shape, jnp.float32) * fan_in ** -0.5

    def gain(k, shape):
        return 1.0 + 0.02 * jax.random.normal(k, shape, jnp.float32)

    L = DEPTH_2
    return {
        "x": jax.random.normal(ks[0], (BATCH, SEQ, D_MODEL), jnp.float32),
        "mem": jax.random.normal(ks[1], (BATCH, MEM_LEN, D_MODEL), jnp.float32),
        "g_mix_norm": gain(ks[2], (L, D_MODEL)),
        "g_mem_norm": gain(ks[3], (L, D_MODEL)),
        "w_in": w(ks[4], (L, D_MODEL, D_IN), D_MODEL),
        "b_forget": 3.0 + 0.5 * jax.random.normal(ks[5], (L, FOX_HEADS), jnp.float32),
        "g_fox_q": gain(ks[6], (L, HD)),
        "g_fox_k": gain(ks[7], (L, HD)),
        "g_mem_q": gain(ks[8], (L, MEM_HD)),
        "g_mem_k": gain(ks[9], (L, MEM_HD)),
        "w_mem_kv": w(ks[10], (L, D_MODEL, 2 * D_MEM), D_MODEL),
        "w_branch_sb": w(ks[11], (L, D_SB, D_MODEL), D_SB),
        "w_branch_fox": w(ks[12], (L, D_FOX, D_MODEL), D_FOX),
        "w_branch_mem": w(ks[13], (L, D_MEM, D_MODEL), D_MEM),
        "w_out": w(ks[14], (L, D_MODEL, D_MODEL), D_MODEL),
        "g_mlp_norm": gain(ks[15], (L, D_MODEL)),
        "w_ff_up": w(ks[16], (L, D_MODEL, D_FF), D_MODEL),
        "w_ff_down": w(ks[17], (L, D_FF, D_MODEL), D_FF),
    }

def second_block(x, mem, g_mix_norm, g_mem_norm, w_in, b_forget, g_fox_q, g_fox_k, g_mem_q, g_mem_k,
              w_mem_kv, w_branch_sb, w_branch_fox, w_branch_mem, w_out, g_mlp_norm, w_ff_up, w_ff_down):
    b, s, _ = x.shape
    for l in range(DEPTH_2):
        h = rmsnorm_2(x, g_mix_norm[l])
        proj = jnp.einsum('bsd,de->bse', h, w_in[l])
        sb_q, sb_k, sb_v, fx_q, fx_k, fx_v, f_logit, m_q, gate_logit = split_columns(proj, SPLITS)

        o_sb = stick_breaking_attention(to_heads(sb_q, SB_HEADS, HD), to_heads(sb_k, SB_HEADS, HD),
                                        to_heads(sb_v, SB_HEADS, HD))

        fq = rmsnorm_2(to_heads(fx_q, FOX_HEADS, HD), g_fox_q[l])
        fk = rmsnorm_2(to_heads(fx_k, FOX_HEADS, HD), g_fox_k[l])
        log_f = jax.nn.log_sigmoid((f_logit + b_forget[l]).astype(jnp.float32)).transpose(0, 2, 1)
        o_fox = forgetting_attention(fq, fk, to_heads(fx_v, FOX_HEADS, HD), log_f)

        mh = rmsnorm_2(mem, g_mem_norm[l])
        mkv = jnp.einsum('bmd,de->bme', mh, w_mem_kv[l])
        mk, mv = split_columns(mkv, (D_MEM, D_MEM))
        mq = rmsnorm_2(to_heads(m_q, MEM_HEADS, MEM_HD), g_mem_q[l])
        mk = rmsnorm_2(to_heads(mk, MEM_HEADS, MEM_HD), g_mem_k[l])
        o_mem = memory_attention(mq, mk, to_heads(mv, MEM_HEADS, MEM_HD))

        gates = jax.nn.sigmoid(gate_logit.reshape(b, s, N_BRANCH, D_MODEL))
        br_sb = jnp.einsum('bse,ed->bsd', from_heads(o_sb), w_branch_sb[l])
        br_fox = jnp.einsum('bse,ed->bsd', from_heads(o_fox), w_branch_fox[l])
        br_mem = jnp.einsum('bse,ed->bsd', from_heads(o_mem), w_branch_mem[l])
        merged = gates[:, :, 0] * br_sb + gates[:, :, 1] * br_fox + gates[:, :, 2] * br_mem
        x = x + jnp.einsum('bsd,de->bse', merged, w_out[l])

        h2 = rmsnorm_2(x, g_mlp_norm[l])
        u = jax.nn.relu(jnp.einsum('bsd,df->bsf', h2, w_ff_up[l]))
        x = x + jnp.einsum('bsf,fd->bsd', u * u, w_ff_down[l])
    return x


def setup_inputs(seed=0):
    out = dict(first_inputs(seed))
    for name, value in second_inputs(seed + 1).items():
        if name != "x":
            out[name + "_2"] = value
    return out


def reference(
    x, norm_mix_g, norm_ffn_g, pool_w_in, pool_w_group, pool_scale, dn_w_in, dn_conv_w,
    dn_a_log, dn_dt_bias, dn_norm_g, dn_w_out, ffn_w_gate, ffn_w_up, ffn_w_down, moe_router_w,
    moe_router_b, moe_w_gate, moe_w_up, moe_w_down, final_norm_g, mem_2, g_mix_norm_2,
    g_mem_norm_2, w_in_2, b_forget_2, g_fox_q_2, g_fox_k_2, g_mem_q_2, g_mem_k_2, w_mem_kv_2,
    w_branch_sb_2, w_branch_fox_2, w_branch_mem_2, w_out_2, g_mlp_norm_2, w_ff_up_2,
    w_ff_down_2,
):
    x = first_block(
        x, norm_mix_g, norm_ffn_g, pool_w_in, pool_w_group, pool_scale, dn_w_in, dn_conv_w,
        dn_a_log, dn_dt_bias, dn_norm_g, dn_w_out, ffn_w_gate, ffn_w_up, ffn_w_down,
        moe_router_w, moe_router_b, moe_w_gate, moe_w_up, moe_w_down, final_norm_g,
    )
    return second_block(
        x, mem_2, g_mix_norm_2, g_mem_norm_2, w_in_2, b_forget_2, g_fox_q_2, g_fox_k_2,
        g_mem_q_2, g_mem_k_2, w_mem_kv_2, w_branch_sb_2, w_branch_fox_2, w_branch_mem_2,
        w_out_2, g_mlp_norm_2, w_ff_up_2, w_ff_down_2,
    )


_drawn_inputs = setup_inputs


def setup_inputs(seed=0):
    import zlib

    import numpy as np

    out = dict(_drawn_inputs(seed))
    spreads = {}
    factors = {'g_mix_norm_2': 5.423,
     'g_mem_norm_2': 8.0,
     'g_fox_q_2': 8.0,
     'g_fox_k_2': 8.0,
     'g_mem_q_2': 8.0,
     'g_mem_k_2': 8.0,
     'g_mlp_norm_2': 9.36}
    for name, (base, spread) in spreads.items():
        noise = np.random.default_rng([zlib.crc32(name.encode()), seed]).standard_normal(out[name].shape)
        drawn = base * np.exp(spread * noise) if base else spread * noise
        out[name] = __import__('jax').numpy.asarray(drawn.astype(out[name].dtype))
    for name, factor in factors.items():
        out[name] = (out[name] * factor).astype(out[name].dtype)
    return out
```

```python
from contextlib import ExitStack

import numpy as np

import concourse.bass as bass
from concourse import mybir

F32 = mybir.dt.float32
FR = mybir.dt.float32r
I32 = mybir.dt.int32
ALU = mybir.AluOpType
ACT = mybir.ActivationFunctionType
AX = mybir.AxisListType.X

P = 128
D = 1024
S = 256
NT = S // P
KD = D // P
CB = 512
KC = 4
EPS = 1e-6
RAW = 7
SPL = 3
TOP_K = 2
NEG = -1e30

POOL_WINDOWS = (2, 4, 8, 16)
DENSE_FF = 2816
NE = 8
EXPERT_FF = 3584
HEADS = 8
CONV = 4
SB_HD = 64
MEM_HD = 128
FF2 = 4096
MAX_ITEMS = NE + 3

LEVELS = (1, 2, 4, 8, 16, 32, 64)
CONST_AT = {}
_at = 0
for _name, _n in (("ident", P), ("ones", P), ("upto", P), ("before", P), ("from_", P), ("future", P),
                  ("iota", P), ("levels", P * len(LEVELS)), ("jlt", NE * NE)):
    CONST_AT[_name] = (_at, _at + _n)
    _at += _n
N_CONST = _at
COL_AT = {}
_at = 0
for _name, _n in (("mix0", 8), ("ffn0", 8), ("mix1", 8), ("ffn1", 8), ("mix2", 8), ("mem2", 8), ("mlp2", 8),
                  ("conv", 96), ("dn_norm", 1), ("mem_q", 1), ("mem_k", 1), ("fox_q", 1), ("fox_k", 1)):
    COL_AT[_name] = (_at, _at + _n)
    _at += _n
N_COL = _at
ROW_AT = {}
_at = 0
for _name, _n in (("scale", D), ("final", D), ("dt", 8), ("alog", 8), ("router_b", 8), ("forget", 8)):
    ROW_AT[_name] = (_at, _at + _n)
    _at += _n
N_ROW = _at


def shape_constants():
    c = np.zeros((P, N_CONST), np.float32)
    i, j = np.arange(P)[:, None], np.arange(P)[None, :]

    def put(name, a):
        c[:, CONST_AT[name][0]:CONST_AT[name][1]] = a

    put("ident", i == j)
    put("ones", np.ones((P, P)))
    put("upto", i <= j)
    put("before", i < j)
    put("from_", i >= j)
    put("future", np.where(j > i, NEG, 0.0))
    put("iota", np.broadcast_to(j, (P, P)))
    put("levels", np.concatenate([(i // (2 * s) == j // (2 * s)) & (i // s % 2 == 0) & (j // s % 2 == 1)
                                  for s in LEVELS], axis=1))
    put("jlt", np.broadcast_to((np.arange(NE)[None, :] < np.arange(NE)[:, None]).reshape(1, -1), (P, NE * NE)))
    pool = np.zeros((P, 2, len(POOL_WINDOWS), S), np.float32)
    t, s = np.arange(S)[None, :], np.arange(S)[:, None]
    for g, w in enumerate(POOL_WINDOWS):
        a = ((s <= t) & (s > t - w)) / np.minimum(t + 1, w) - (s == t)
        pool[:, :, g, :] = a.reshape(2, P, S).transpose(1, 0, 2)
    return c, pool.reshape(P, -1)


def build(nc, t, out):
    with ExitStack() as ctx:
        def sb(name, shape, dt=F32):
            return ctx.enter_context(nc.sbuf_tensor(name, shape, dt))

        def sem(name):
            return ctx.enter_context(nc.semaphore(name))

        raw = sb("raw", [P, RAW, KC * CB])
        w_hi = sb("w_hi", [P, SPL, KC * CB], FR)
        w_lo = sb("w_lo", [P, SPL, KC * CB], FR)
        cst = sb("cst", [P, N_CONST])
        col = sb("col", [P, N_COL])
        row = sb("row", [P, N_ROW])
        w_ba = sb("w_ba", [P, KD, 16])
        w_router = sb("w_router", [P, KD, NE])
        w_forget = sb("w_forget", [P, KD, 8])
        h = sb("h", [P, NT, D])
        xn = sb("xn", [P, NT, D])
        small = sb("small", [P, 512])
        xT1 = sb("xT1", [P, KD, S], FR)
        xT2 = sb("xT2", [P, KD, S], FR)
        area = nc.sbuf_base
        sb("room", [P, 13312])

        def at(name, shape, off, dt=F32):
            return nc.alloc_sbuf_tensor_at(name, shape, dt, offset=area + int(off * 1024))

        hid1 = at("hid1", [P, 16, S], 0, FR)
        hid2 = at("hid2", [P, 16, S], 16, FR)
        gate_s = at("gate_s", [P, NT, CB], 32)
        hnat = at("hnat", [P, NT, CB], 36)
        pool_m = at("pool_m", [P, 2, 4, S], 0)
        pool_u = at("pool_u", [P, NT, D], 8)
        pool_t = at("pool_t", [P, NT, CB], 16)

        qkvT = [at(n, [P, HEADS, S], o) for n, o in (("qT", 0), ("kT", 8), ("vT", 16))]
        qT, kT, vT = qkvT
        z_s = at("z_s", [P, NT, D], 24)
        kn = at("kn", [P, NT, HEADS, P], 32)
        vn = at("vn", [P, NT, HEADS, P], 40)
        memory_s = at("memory_s", [P, HEADS, P], 48)
        squares = at("squares", [P, 16, S], -16)
        o_sq = at("o_sq", [P, NT, D], 0)
        buf = {}
        for _h, offs in enumerate(((-16, -14, -12, -10, -8, -6), (-4, -2, 16, 18, 20, 22))):
            for _n, _o in zip(("dec", "A", "T", "TT", "X", "qk"), offs):
                buf[_n, _h] = at(f"{_n}{_h}", [P, 4, P], _o)
        hidden1 = hid1[:, :, :].rearrange("p a b -> p (a b)")
        hidden2 = hid2[:, :, :].rearrange("p a b -> p (a b)")
        y_s = at("y_s", [P, 2, CB], 40)
        pick = at("pick", [P, NT, P], 44)
        pick_gate = at("pick_gate", [P, NT, P], 45)
        spread = at("spread", [P, NT, P], 46)
        rt = at("rt", [P, 40, 8], 48)
        item_pos = at("item_pos", [P, NT, 12], 50)
        item_gate = at("item_gate", [P, NT, 12], 50.25)
        item_f = at("item_f", [P, 16], 50.5)
        item_i = at("item_i", [P, 16], 50.75, I32)
        mem_in = at("mem_in", [P, NT, D], 0)
        o_sb = at("o_sb", [P, NT, CB], 0)
        o_fox = at("o_fox", [P, NT, CB], 4)
        o_mem = at("o_mem", [P, NT, CB], 44)
        v_mem = at("v_mem", [P, NT, CB], 8)
        k_memT = at("k_memT", [P, 4, S], 12)
        q_sbT = at("q_sbT", [P, 4, S], 16)
        k_sbT = at("k_sbT", [P, 4, S], 20)
        v_sb = at("v_sb", [P, NT, CB], 24)
        q_foxT = at("q_foxT", [P, 4, S], 28)
        k_foxT = at("k_foxT", [P, 4, S], 32)
        v_fox = at("v_fox", [P, NT, CB], 36)
        q_memT = at("q_memT", [P, 4, S], 40)
        head_sq = at("head_sq", [P, NT, CB], 44)
        third = at("third", [P, 2, 3 * P], 48)
        oT1 = [at(f"oT1_{b}", [P, 4, S], 16 + 8 * b, FR) for b in range(3)]
        oT2 = [at(f"oT2_{b}", [P, 4, S], 20 + 8 * b, FR) for b in range(3)]
        gate2 = at("gate2", [P, NT, CB], 8)
        fx = small[:, 16:80].rearrange("p (a b) -> p a b", a=4)
        (F_NLF, F_M, F_E, F_CUM) = range(4)
        hs = small[:, 80:144].rearrange("p (a b) -> p a b", a=4)
        st = small[:, 144:176].rearrange("p (a b) -> p a b", a=8)
        dnv = small[:, 256:512].rearrange("p (a b) -> p a b", a=16)
        (V_BETA, V_X, V_M, V_E, V_G, V_GC, V_GL, V_EGC, V_EKD, V_SS, _, V_R, _, V_TMP, _, V_EA) = range(16)

        bank = [ctx.enter_context(nc.psum_tensor(f"bank{i}", [P, CB], F32)) for i in range(8)]
        acc, tp = bank[:4], bank[4:]

        def C(name):
            return cst[:, CONST_AT[name][0]:CONST_AT[name][1]]

        def G(name, k=0):
            a = COL_AT[name][0] + k
            return col[:, a:a + 1]

        def R(name):
            return row[:, ROW_AT[name][0]:ROW_AT[name][1]]

        ident = C("ident")

        stream = []
        cbs = {}

        def add_cb(name, w, c0, n, rows=None, k0=0):
            rows = w.shape[0] - k0 if rows is None else rows
            first = len(stream)
            for r in range(k0, k0 + rows, KC * P):
                kc = min(KC, (k0 + rows - r) // P)
                stream.append((w[r:r + kc * P, c0:c0 + n].rearrange("(k p) n -> p k n", p=P), kc, n))
            cbs[name] = (first, len(stream), n)

        for c in range(2):
            add_cb(("pool_in", c), t["pool_w_in"][0], c * CB, CB)
        for c in range(2):
            first = len(stream)
            stream.append((t["pool_w_group"][0, 2 * c:2 * c + 2].rearrange("g (k p) e -> p (g k) e", p=P), 4, 256))
            cbs["pool_out", c] = (first, first + 1, CB)
        FF_HALVES = ((0, (512, 512, 512)), (1536, (512, 512, 256)))
        for hf, (f0, blocks) in enumerate(FF_HALVES):
            f = f0
            for b, n in enumerate(blocks):
                if f + n > DENSE_FF:
                    n = DENSE_FF - f
                add_cb(("gate", hf, b), t["ffn_w_gate"][0], f, n)
                add_cb(("up", hf, b), t["ffn_w_up"][0], f, n)
                f += n
            for c in range(2):
                add_cb(("down", hf, c), t["ffn_w_down"][0], c * CB, CB, f - f0, f0)
        for c in range(8):
            add_cb(("dn_in", c), t["dn_w_in"][0], c * CB, CB)
        for c in range(2):
            add_cb(("dn_out", c), t["dn_w_out"][0], c * CB, CB)
        NA = len(stream)

        add_cb(("b_in", "mk"), t["w_mem_kv_2"][0], 0, CB)
        add_cb(("b_in", "mv"), t["w_mem_kv_2"][0], CB, CB)
        B_IN = (("sbq", 0), ("sbk", 512), ("sbv", 1024), ("fxq", 1536), ("fxk", 2048), ("fxv", 2560), ("mq", 3080))
        for name, c0 in B_IN:
            add_cb(("b_in", name), t["w_in_2"][0], c0, CB)
        for c in range(2):
            for b, w in enumerate(("sb", "fox", "mem")):
                add_cb(("b_gate", b, c), t["w_in_2"][0], 3592 + b * D + c * CB, CB)
                add_cb(("branch", b, c), t[f"w_branch_{w}_2"][0], c * CB, CB)
        for c in range(2):
            add_cb(("b_out", c), t["w_out_2"][0], c * CB, CB)
        for hf in range(2):
            for b in range(4):
                add_cb(("f_up", hf, b), t["w_ff_up_2"][0], (4 * hf + b) * CB, CB)
            for c in range(2):
                add_cb(("f_down", hf, c), t["w_ff_down_2"][0], c * CB, CB, 4 * CB, 4 * hf * CB)

        HEADED = {"mk": (k_memT, 128, "mem_k"), "sbq": (q_sbT, 0, None), "sbk": (k_sbT, 0, None),
                  "fxq": (q_foxT, 64, "fox_q"), "fxk": (k_foxT, 64, "fox_k"), "mq": (q_memT, 128, "mem_q")}
        KEPT = {"mv": v_mem, "sbv": v_sb, "fxv": v_fox}
        NORMED = [n for n in ("mk", "fxq", "fxk", "mq")]
        STAGE = {"mk": 0, **{n: c % 2 for c, (n, _) in enumerate(B_IN)}}

        FB = EXPERT_FF // CB
        MT = 4 * FB + 2 * FB
        m_tiles = []
        for f in range(FB):
            for w in ("moe_w_gate", "moe_w_up"):
                for k in range(2):
                    m_tiles.append((w, k * CB, f * CB))
        for c in range(2):
            for f in range(FB):
                m_tiles.append(("moe_w_down", f * CB, c * CB))
        assert len(m_tiles) == MT and MT % RAW == 0 and MT % SPL == 0

        setup = sem("setup")
        x_in = sem("x_in")
        landed = [sem(f"landed{i}") for i in range(RAW)]
        split_hi = sem("split_hi")
        split_lo = sem("split_lo")
        used = sem("used")
        tp_done = sem("tp_done")
        tp_free = {"A": sem("tp_free_act"), "D": sem("tp_free_dve")}
        acc_free = {"A": sem("acc_free_act"), "D": sem("acc_free_dve")}
        a_own = sem("a_own")
        d_own = sem("d_own")
        sq_done = sem("sq_done")
        rs_done = sem("rs_done")
        xn_done = sem("xn_done")
        hi_out = sem("hi_out")
        gate_done = sem("gate_done")
        out_done = sem("out_done")
        v_done = sem("v_done")
        h_done = sem("h_done")
        silu_done = sem("silu_done")
        gain_in = sem("gain_in")
        route_act = sem("route_act")
        route_dve = sem("route_dve")
        items_ready = sem("items_ready")
        picked0 = sem("picked0")
        m_landed = [sem(f"m_landed{i}") for i in range(RAW)]
        m_hi = sem("m_hi")
        m_lo = sem("m_lo")
        m_used = sem("m_used")
        m_tp = sem("m_tp")
        m_read = sem("m_read")
        m_spread = sem("m_spread")
        m_turned = sem("m_turned")
        m_gate = sem("m_gate")
        m_up = sem("m_up")
        m_y = sem("m_y")
        m_pick = sem("m_pick")
        moe_done = sem("moe_done")
        mem_loaded = sem("mem_loaded")
        h_square = sem("h_square")
        h_sq_v = sem("h_sq_v")
        h_rs = sem("h_rs")
        h_scaled = sem("h_scaled")
        fox_dve = sem("fox_dve")
        fox_act = sem("fox_act")
        sb_e = sem("sb_e")
        sb_z = sem("sb_z")
        sb_l = sem("sb_l")
        sb_sp = sem("sb_sp")
        sb_a = sem("sb_a")
        sb_wx = sem("sb_wx")
        sb_w = sem("sb_w")
        sm_z = sem("sm_z")
        sm_p = sem("sm_p")
        relu_sq = sem("relu_sq")
        merged = sem("merged")
        small_act = sem("small_act")
        small_dve = sem("small_dve")
        dec_min = sem("dec_min")
        dec_exp = sem("dec_exp")
        inv_first = sem("inv_first")
        inv_level = sem("inv_level")
        rhs_done = sem("rhs_done")
        kdec_done = sem("kdec_done")
        o_done = sem("o_done")
        o_squared = sem("o_squared")
        rs_ready = sem("rs_ready")
        block = ctx.enter_context(nc.Block())

        def before(hf, b):
            return (hf, b - 1) if b else (hf - 1, len(FF_HALVES[hf - 1][1]) - 1)

        (R_LG, R_EXP, R_SEL, R_RANK, R_CNT, R_MAX, R_IND, R_TMP, R_BIG, R_TIE) = (0, 2, 4, 6, 8, 9, 10, 11, 16, 24)
        SC1, SPREAD, TURN, GATHER, TURN6, SC0, M_BANKS, M_READS = 0, 2, 3, 9, 11, 12, 14, 13

        def n_items(eng):
            return eng.value_load(item_i[0:1, 12:13], min_val=NE, max_val=MAX_ITEMS)

        batches, batch_of = [], {}
        groups, group_of = [], {}
        SETUP = 7 * 16

        @block.tensor
        def _(pe):
            def tp_bank(name, owner):
                b = len(batches)
                if b >= 4:
                    o = batches[b - 4]
                    pe.wait_ge(tp_free[o], batches[:b - 3].count(o))
                batches.append(owner)
                batch_of[name] = (tp[b % 4], b + 1, owner, batches.count(owner))
                return tp[b % 4]

            def result(name):
                _, _, owner, n = batch_of[name]
                pe.wait_ge(tp_free[owner], n)

            def gemm(name, owner, a1, a2, chunks=None, between=None):
                first, end, n = cbs[name]
                g = len(groups)
                if g >= 2:
                    o = groups[g - 2]
                    pe.wait_ge(acc_free[o], groups[:g - 1].count(o))
                groups.append(owner)
                banks = acc[2 * (g % 2):2 * (g % 2) + 2]
                group_of[name] = (banks, end, owner, groups.count(owner))
                k0 = 0
                for i in range(first, end):
                    _, kc, _ = stream[i]
                    pe.wait_ge(split_lo, i + 1)
                    s = i % SPL
                    for tt in range(NT):
                        for k in range(kc):
                            ch = k0 + k if chunks is None else chunks[k0 + k]
                            b1 = w_hi[:, s, k * n:k * n + n]
                            b2 = w_lo[:, s, k * n:k * n + n]
                            o = banks[tt][:, 0:n]
                            x1 = a1[:, ch, tt * P:tt * P + P]
                            x2 = a2[:, ch, tt * P:tt * P + P]
                            begin, end_ = i == first and k == 0, i == end - 1 and k == kc - 1
                            nc.tensor.matmul(o, x1, b2, start=begin, stop=False)
                            nc.tensor.matmul(o, x2, b1, start=False, stop=False)
                            last = nc.tensor.matmul(o, x1, b1, start=False, stop=end_)
                    last.then_inc(used, 1)
                    k0 += kc
                    if between and i == first:
                        between()

            def turn_norm(tag, n_norm):
                pe.wait_ge(xn_done, 2 * n_norm)
                for p in range(KD // 2):
                    b = tp_bank((tag, p), "D")
                    for j in range(2):
                        for tt in range(NT):
                            ch = 2 * p + j
                            last = nc.tensor.transpose(b[:, (2 * j + tt) * P:(2 * j + tt + 1) * P],
                                                       xn[:, tt, ch * P:ch * P + P], ident)
                    last.then_inc(tp_done, 1)
                result((tag, KD // 2 - 1))

            def turn_hidden(tag, up):
                pe.wait_ge(acc_free["D"], group_of[up][3])
                n = cbs[up][2]
                for tt in range(NT):
                    b = tp_bank((tag, tt), "D")
                    for k in range(n // P):
                        last = nc.tensor.transpose(b[:, k * P:k * P + P], hnat[:, tt, k * P:k * P + P], ident)
                    last.then_inc(tp_done, 1)

            def small_products(name, owner, products):
                b = tp_bank(name, owner)
                for o, l, r in products(b):
                    last = nc.tensor.matmul(o, l, r, start=True, stop=True)
                last.then_inc(tp_done, 1)

            def four(b):
                return [b[:, k * P:k * P + P] for k in range(4)]

            def across(v):
                return v.broadcast_to((P, P))

            def deltanet():
                b = tp_bank("ba", "D")
                for tt in range(NT):
                    for k in range(KD):
                        for x in (xT2, xT1):
                            last = nc.tensor.matmul(b[:, tt * 16:tt * 16 + 16], x[:, k, tt * P:tt * P + P].bitcast(F32),
                                                    w_ba[:, k, :], start=k == 0 and x is xT2, stop=k == KD - 1 and x is xT1)
                last.then_inc(tp_done, 1)

                def turn_conv(c):
                    pe.wait_ge(acc_free["A"], group_of["dn_in", c][3])
                    for j in range(2):
                        b = tp_bank(("conv", c, j), "D")
                        for k in range(2):
                            for tt in range(NT):
                                col0 = tt * CB + (2 * j + k) * P
                                last = nc.tensor.transpose(b[:, (2 * k + tt) * P:(2 * k + tt + 1) * P],
                                                           xn[:, c % 2, col0:col0 + P], ident)
                        last.then_inc(tp_done, 1)

                for c in range(8):
                    gemm(("dn_in", c), "A", xT1, xT2)
                    if 1 <= c <= 6:
                        turn_conv(c - 1)
                    if c == 2:
                        pe.wait_ge(small_dve, 2)
                        small_products("gc", "D", lambda b: [
                            (b[:, 0:16], C("upto"), dnv[:, V_G, :]), (b[:, 16:32], C("ones"), dnv[:, V_G, :])])
                pe.wait_ge(o_squared, 2)
                small_products("ssq", "D", lambda b: [
                    (b[:, (2 * m + tt) * 8 + hh:(2 * m + tt) * 8 + hh + 1], squares[:, 8 * m + hh, tt * P:tt * P + P],
                     C("ones")[:, 0:1]) for m in range(2) for tt in range(NT) for hh in range(HEADS)])
                pe.wait_ge(rs_ready, 1)
                for m in range(2):
                    for p in range(4):
                        small_products(("unit", m, p), "D", lambda b: [
                            (b[:, (2 * k + tt) * P:(2 * k + tt + 1) * P],
                             across(dnv[:, V_R + m, tt * 8 + 2 * p + k:tt * 8 + 2 * p + k + 1]), ident)
                            for k in range(2) for tt in range(NT)])
                pe.wait_ge(silu_done, 12)
                result(("unit", 1, 3))
                for n, src in (("vn", vT), ("kn", kT)):
                    for tt in range(NT):
                        for hg in range(2):
                            b = tp_bank((n, tt, hg), "A")
                            for k in range(4):
                                last = nc.tensor.transpose(b[:, k * P:k * P + P],
                                                           src[:, 4 * hg + k, tt * P:tt * P + P], ident)
                            last.then_inc(tp_done, 1)
                result(("kn", 1, 1))
                for tt in range(NT):
                    now = slice(tt * P, tt * P + P)

                    def heads(hg):
                        return [4 * hg + k for k in range(4)]

                    for hg in range(2):
                        small_products(("decay", tt, hg), "D", lambda b: [
                            (o, across(dnv[:, V_G, tt * 8 + hh:tt * 8 + hh + 1]), C("upto"))
                            for o, hh in zip(four(b), heads(hg))])
                    for hg in range(2):
                        small_products(("kk", tt, hg), "D", lambda b: [
                            (o, kT[:, hh, now], kT[:, hh, now]) for o, hh in zip(four(b), heads(hg))])
                        small_products(("beta", tt, hg), "D", lambda b: [
                            (o, across(dnv[:, V_BETA, tt * 8 + hh:tt * 8 + hh + 1]), ident)
                            for o, hh in zip(four(b), heads(hg))])
                        small_products(("qk", tt, hg), "D", lambda b: [
                            (o, kT[:, hh, now], qT[:, hh, now]) for o, hh in zip(four(b), heads(hg))])
                    for hg in range(2):
                        pe.wait_ge(inv_first, 2 * tt + hg + 1)
                        b = tp_bank(("T", tt, hg), "A")
                        for k in range(4):
                            last = nc.tensor.transpose(b[:, k * P:k * P + P], buf["TT", hg][:, k, :], ident)
                        last.then_inc(tp_done, 1)
                    for l in range(1, len(LEVELS)):
                        for hg in range(2):
                            pe.wait_ge(inv_level, (tt * (len(LEVELS) - 1) + l - 1) * 2 + hg + 1)
                            result(("T", tt, hg) if l == 1 else ("inv_T", tt, hg, l - 1))
                            small_products(("X", tt, hg, l), "A", lambda b: [
                                (o, buf["dec", hg][:, k, :], buf["T", hg][:, k, :]) for k, o in enumerate(four(b))])
                        for hg in range(2):
                            result(("X", tt, hg, l))
                            if l > 1:
                                result(("inv_TT", tt, hg, l - 1))
                            if l < len(LEVELS) - 1:
                                small_products(("inv_T", tt, hg, l), "D", lambda b: [
                                    (o, buf["TT", hg][:, k, :], buf["X", hg][:, k, :]) for k, o in enumerate(four(b))])
                            small_products(("inv_TT", tt, hg, l), "D", lambda b: [
                                (o, buf["X", hg][:, k, :], buf["TT", hg][:, k, :]) for k, o in enumerate(four(b))])
                    for hg in range(2):
                        if tt:
                            result(("state", 0, hg))
                            small_products(("kS", tt, hg), "D", lambda b: [
                                (o, kT[:, hh, now], memory_s[:, hh, :]) for o, hh in zip(four(b), heads(hg))])
                            small_products(("qS", tt, hg), "D", lambda b: [
                                (o, qT[:, hh, now], memory_s[:, hh, :]) for o, hh in zip(four(b), heads(hg))])
                    for hg in range(2):
                        pe.wait_ge(rhs_done, 2 * tt + hg + 1)
                        result(("inv_TT", tt, hg, len(LEVELS) - 1))
                        small_products(("vnew", tt, hg), "A", lambda b: [
                            (o, buf["TT", hg][:, k, :], buf["A", hg][:, k, :]) for k, o in enumerate(four(b))])
                    for hg in range(2):
                        result(("vnew", tt, hg))
                        small_products(("o", tt, hg), "D", lambda b: [
                            (o, buf["qk", hg][:, k, :], buf["X", hg][:, k, :]) for k, o in enumerate(four(b))])
                        if tt == 0:
                            pe.wait_ge(kdec_done, hg + 1)
                            small_products(("state", 0, hg), "A", lambda b: [
                                (o, buf["T", hg][:, k, :], buf["X", hg][:, k, :]) for k, o in enumerate(four(b))])
                turn_norm("o", 4)
                for c in range(2):
                    gemm(("dn_out", c), "D", xT1, xT2)

            def experts():
                turn_norm("n3", 5)
                b = tp_bank("router", "D")
                for tt in range(NT):
                    for k in range(KD):
                        for x in (xT2, xT1):
                            last = nc.tensor.matmul(b[:, tt * 8:tt * 8 + 8], x[:, k, tt * P:tt * P + P].bitcast(F32),
                                                    w_router[:, k, :], start=k == 0 and x is xT2,
                                                    stop=k == KD - 1 and x is xT1)
                last.then_inc(tp_done, 1)
                pe.wait_ge(route_dve, 2)
                b = tp_bank("places", "D")
                sel = [rt[:, R_SEL + tt, :] for tt in range(NT)]
                nc.tensor.matmul(b[:, 0:8], C("before"), sel[0], start=True, stop=True)
                nc.tensor.matmul(b[:, 8:16], C("ones"), sel[0], start=True, stop=False)
                nc.tensor.matmul(b[:, 8:16], C("before"), sel[1], start=False, stop=True)
                nc.tensor.matmul(b[:, 16:24], C("ones"), sel[0], start=True, stop=False)
                nc.tensor.matmul(b[:, 16:24], C("ones"), sel[1], start=False, stop=True).then_inc(tp_done, 1)

                def gather(b, half):
                    for k in range(4):
                        ch = 4 * half + k
                        for tt in range(NT):
                            last = nc.tensor.matmul(b[:, k * P:k * P + P], xn[:, tt, ch * P:ch * P + P], pick[:, tt, :],
                                                    start=tt == 0, stop=tt == NT - 1)
                    return last

                pe.wait_ge(picked0, 4)
                for half in range(2):
                    gather(tp_bank(("gather", half), "D"), half).then_inc(tp_done, 1)
                result(("gather", 1))
                for o in "AD":
                    pe.wait_ge(tp_free[o], batches.count(o))
                    pe.wait_ge(acc_free[o], groups.count(o))
                n = n_items(pe)
                with pe.Fori(0, n) as i:
                    def product(j, lhs, out, begin, end):
                        pe.wait_ge(m_lo, i * MT + (j + 2))
                        s = j % SPL
                        for k in range(KC):
                            a1, a2 = lhs(k)
                            b1, b2 = w_hi[:, s, k * CB:k * CB + CB], w_lo[:, s, k * CB:k * CB + CB]
                            nc.tensor.matmul(out, a1, b2, start=begin and k == 0, stop=False)
                            nc.tensor.matmul(out, a2, b1, start=False, stop=False)
                            last = nc.tensor.matmul(out, a1, b1, start=False, stop=end and k == KC - 1)
                        last.then_inc(m_used, 1)

                    def tokens(j):
                        return lambda k: (xT1[:, 4 * (j % 2) + k, 0:P], xT2[:, 4 * (j % 2) + k, 0:P])

                    def hidden(f):
                        return lambda k: (hidden1[:, (4 * f + k) * P:(4 * f + k + 1) * P],
                                          hidden2[:, (4 * f + k) * P:(4 * f + k + 1) * P])

                    def turn(f):
                        pe.wait_ge(m_up, i * FB + (f + 1))
                        bi = TURN + f if f < 6 else TURN6
                        if f < 6:
                            if f == 3:
                                pe.wait_ge(m_spread, i + 1)
                            pe.wait_ge(m_read, i * M_READS + (3 if f < 4 else f))
                        else:
                            pe.wait_ge(m_read, i * M_READS + 8)
                        b = tp[bi % 4]
                        for k in range(4):
                            last = nc.tensor.transpose(b[:, k * P:k * P + P], hnat[:, f % 2, k * P:k * P + P], ident)
                        last.then_inc(m_tp, 1)

                    def scatter(bi, c):
                        for tt in range(NT):
                            nc.tensor.matmul(tp[(bi + tt) % 4][:, :], spread[:, tt, :], y_s[:, c, :],
                                             start=True, stop=True).then_inc(m_tp, 1)

                    for f in range(FB):
                        g = acc[2 * (f % 2)][:, :]
                        u = acc[2 * (f % 2) + 1][:, :]
                        if f == 1:
                            pe.wait_ge(m_y, i * 2 + 1)
                        elif f > 1:
                            pe.wait_ge(m_gate, i * FB + (f - 1))
                        for j in (4 * f, 4 * f + 1):
                            product(j, tokens(j), g, j % 2 == 0, j % 2 == 1)
                        if f == 0:
                            pe.wait_ge(m_y, i * 2 + 1)
                            pe.wait_ge(m_read, i * M_READS + 1)
                            scatter(SC1, 1)
                        if f >= 1:
                            turn(f - 1)
                        if f >= 2:
                            pe.wait_ge(m_up, i * FB + (f - 1))
                        for j in (4 * f + 2, 4 * f + 3):
                            product(j, tokens(j), u, j % 2 == 0, j % 2 == 1)
                        if f == 0:
                            for tt in range(NT):
                                last = nc.tensor.transpose(tp[SPREAD % 4][:, tt * P:tt * P + P], pick_gate[:, tt, :], ident)
                            last.then_inc(m_tp, 1)
                    pe.wait_ge(m_pick, i * 4 + 4)
                    for half in range(2):
                        pe.wait_ge(m_read, i * M_READS + (6 + half))
                        gather(tp[(GATHER + half) % 4], half).then_inc(m_tp, 1)
                    pe.wait_ge(m_gate, i * FB + 6)
                    for j in range(4 * FB, 5 * FB):
                        if j == 4 * FB + 1:
                            turn(FB - 1)
                        f = j - 4 * FB
                        if f in (1, FB - 1):
                            pe.wait_ge(m_read, i * M_READS + (9 if f == 1 else 12))
                        product(j, hidden(f), acc[2][:, :], f == 0, f == FB - 1)
                    pe.wait_ge(m_up, i * FB + 6)
                    for j in range(5 * FB, 6 * FB):
                        f = j - 5 * FB
                        product(j, hidden(f), acc[3][:, :], f == 0, f == FB - 1)
                        if f == 1:
                            pe.wait_ge(m_y, i * 2 + 2)
                            pe.wait_ge(m_read, i * M_READS + 12)
                            scatter(SC0, 0)
                pe.wait_ge(m_y, n * 2 + 1)
                pe.wait_ge(m_read, n * M_READS + 1)
                for tt in range(NT):
                    nc.tensor.matmul(tp[tt][:, :], spread[:, tt, :], y_s[:, 1, :], start=True, stop=True)\
                        .then_inc(m_tp, 1)
                pe.wait_ge(moe_done, 1)

            def second_block():
                def turn_heads(name):
                    if HEADED[name][1]:
                        pe.wait_ge(h_scaled, NORMED.index(name) + 1)
                    else:
                        pe.wait_ge(acc_free["A"], group_of["b_in", name][3])
                    for j in range(2):
                        b = tp_bank(("heads", name, j), "D")
                        for k in range(2):
                            for tt in range(NT):
                                c0 = tt * CB + (2 * j + k) * P
                                last = nc.tensor.transpose(b[:, (2 * k + tt) * P:(2 * k + tt + 1) * P],
                                                           xn[:, STAGE[name], c0:c0 + P], ident)
                        last.then_inc(tp_done, 1)

                turn_norm("mm", 6)
                gemm(("b_in", "mk"), "A", xT1, xT2)
                gemm(("b_in", "mv"), "A", xT1, xT2)
                turn_heads("mk")
                turn_norm("m2", 7)
                b = tp_bank("forget", "D")
                for tt in range(NT):
                    for k in range(KD):
                        for x in (xT2, xT1):
                            last = nc.tensor.matmul(b[:, tt * 8:tt * 8 + 8], x[:, k, tt * P:tt * P + P].bitcast(F32),
                                                    w_forget[:, k, :], start=k == 0 and x is xT2,
                                                    stop=k == KD - 1 and x is xT1)
                last.then_inc(tp_done, 1)
                for c, (name, _) in enumerate(B_IN):
                    gemm(("b_in", name), "A", xT1, xT2)
                    if c == 1:
                        pe.wait_ge(fox_dve, 2)
                        b = tp_bank("cumf", "D")
                        nc.tensor.matmul(b[:, 0:8], C("upto"), fx[:, F_NLF, 0:8], start=True, stop=True)
                        nc.tensor.matmul(b[:, 8:16], C("ones"), fx[:, F_NLF, 0:8], start=True, stop=False)
                        nc.tensor.matmul(b[:, 8:16], C("upto"), fx[:, F_NLF, 8:16], start=False, stop=True)\
                            .then_inc(tp_done, 1)
                    if c and B_IN[c - 1][0] in HEADED:
                        turn_heads(B_IN[c - 1][0])
                turn_heads("mq")
                result(("heads", "mq", 1))
                pe.wait_ge(acc_free["A"], group_of["b_in", "fxv"][3])

                def half(x, hh, cols):
                    r = 64 * (hh % 2)
                    return x[r:r + 64, hh // 2, cols]

                t0, t1, both = slice(0, P), slice(P, S), slice(0, S)
                for pair in range(4):
                    hd = (2 * pair, 2 * pair + 1)
                    for hh in hd:
                        b = tp_bank(("sb_z", hh), "A")
                        nc.tensor.matmul(b[:, 0:S], half(k_sbT, hh, t0), half(q_sbT, hh, both), start=True, stop=True)
                        nc.tensor.matmul(b[:, S:S + P], half(k_sbT, hh, t1), half(q_sbT, hh, t1), start=True, stop=True)\
                            .then_inc(tp_done, 1)
                    for hh in hd:
                        pe.wait_ge(sb_sp, hh + 1)
                        sp_ = xn[:, hh % 2, 3 * P:6 * P]
                        b = tp_bank(("sb_cum", hh), "D")
                        nc.tensor.matmul(b[:, 0:S], C("from_"), sp_[:, 0:S], start=True, stop=False)
                        nc.tensor.matmul(b[:, P:S], C("ones"), sp_[:, S:S + P], start=False, stop=True)
                        nc.tensor.matmul(b[:, S:S + P], C("from_"), sp_[:, S:S + P], start=True, stop=True)\
                            .then_inc(tp_done, 1)
                    b = tp_bank(("sb_o", pair), "D")
                    for k, hh in enumerate(hd):
                        pe.wait_ge(sb_w, hh + 1)
                        w = xn[:, hh % 2, 0:3 * P]
                        v = [v_sb[:, tt, hh * 64:hh * 64 + 64] for tt in range(NT)]
                        nc.tensor.matmul(b[:, k * 64:k * 64 + 64], w[:, 0:P], v[0], start=True, stop=True)
                        nc.tensor.matmul(b[:, P + k * 64:P + k * 64 + 64], w[:, P:S], v[0], start=True, stop=False)
                        last = nc.tensor.matmul(b[:, P + k * 64:P + k * 64 + 64], w[:, S:S + P], v[1],
                                                start=False, stop=True)
                    last.then_inc(tp_done, 1)
                for pair in range(4):
                    hd = (2 * pair, 2 * pair + 1)
                    for hh in hd:
                        b = tp_bank(("fx_z", hh), "D")
                        f0 = across(fx[:, F_NLF, hh:hh + 1])
                        f1 = across(fx[:, F_NLF, 8 + hh:9 + hh])
                        nc.tensor.matmul(b[:, 0:P], half(q_foxT, hh, t0), half(k_foxT, hh, t0), start=True, stop=False)
                        nc.tensor.matmul(b[:, 0:P], f0, C("upto"), start=False, stop=True)
                        nc.tensor.matmul(b[:, P:3 * P], half(q_foxT, hh, t1), half(k_foxT, hh, both), start=True, stop=False)
                        nc.tensor.matmul(b[:, P:S], f0, C("upto"), start=False, stop=False)
                        nc.tensor.matmul(b[:, S:3 * P], f0, C("ones"), start=False, stop=False)
                        nc.tensor.matmul(b[:, S:3 * P], f1, C("upto"), start=False, stop=True).then_inc(tp_done, 1)
                    for hh in hd:
                        pe.wait_ge(sm_p, hh + 1)
                        b = tp_bank(("fx_t", hh), "A")
                        for k in range(3):
                            last = nc.tensor.transpose(b[:, k * P:k * P + P], xn[:, hh % 2, k * P:k * P + P], ident)
                        last.then_inc(tp_done, 1)
                    b = tp_bank(("fx_o", pair), "D")
                    for k, hh in enumerate(hd):
                        result(("fx_t", hh))
                        pT = xn[:, hh % 2, 3 * P:6 * P]
                        v = [v_fox[:, tt, hh * 64:hh * 64 + 64] for tt in range(NT)]
                        nc.tensor.matmul(b[:, k * 64:k * 64 + 64], pT[:, 0:P], v[0], start=True, stop=True)
                        nc.tensor.matmul(b[:, P + k * 64:P + k * 64 + 64], pT[:, P:S], v[0], start=True, stop=False)
                        last = nc.tensor.matmul(b[:, P + k * 64:P + k * 64 + 64], pT[:, S:3 * P], v[1],
                                                start=False, stop=True)
                    last.then_inc(tp_done, 1)
                for pair in range(2):
                    hd = (2 * pair, 2 * pair + 1)
                    for hh in hd:
                        b = tp_bank(("mm_z", hh), "D")
                        for tt in range(NT):
                            last = nc.tensor.matmul(b[:, tt * S:tt * S + S], q_memT[:, hh, tt * P:tt * P + P],
                                                    k_memT[:, hh, :], start=True, stop=True)
                        last.then_inc(tp_done, 1)
                    for hh in hd:
                        pe.wait_ge(sm_p, 8 + hh + 1)
                        b = tp_bank(("mm_t", hh), "A")
                        for k in range(4):
                            last = nc.tensor.transpose(b[:, k * P:k * P + P], xn[:, hh % 2, k * P:k * P + P], ident)
                        last.then_inc(tp_done, 1)
                    b = tp_bank(("mm_o", pair), "D")
                    for k, hh in enumerate(hd):
                        result(("mm_t", hh))
                        pT = xn[:, hh % 2, 4 * P:8 * P]
                        for tt in range(NT):
                            for m in range(2):
                                last = nc.tensor.matmul(b[:, tt * S + k * P:tt * S + k * P + P],
                                                        pT[:, (2 * tt + m) * P:(2 * tt + m + 1) * P],
                                                        v_mem[:, m, hh * P:hh * P + P], start=m == 0, stop=m == 1)
                    last.then_inc(tp_done, 1)
                for br, (o, done) in enumerate(((o_sb, ("sb_o", 3)), (o_fox, ("fx_o", 3)), (o_mem, ("mm_o", 1)))):
                    result(done)
                    for j in range(2):
                        b = tp_bank(("oT", br, j), "D")
                        for k in range(2):
                            for tt in range(NT):
                                ch = 2 * j + k
                                last = nc.tensor.transpose(b[:, (2 * k + tt) * P:(2 * k + tt + 1) * P],
                                                           o[:, tt, ch * P:ch * P + P], ident)
                        last.then_inc(tp_done, 1)
                for c in range(2):
                    for br in range(3):
                        gemm(("b_gate", br, c), "A", xT1, xT2)
                        result(("oT", br, 1))
                        gemm(("branch", br, c), "D", oT1[br], oT2[br])
                turn_norm("mg", 8)
                for c in range(2):
                    gemm(("b_out", c), "D", xT1, xT2)
                turn_norm("m3", 9)
                for hf in range(2):
                    def turn(b):
                        pe.wait_ge(relu_sq, 2 * (4 * hf + b + 1))
                        for tt in range(NT):
                            bk = tp_bank((("fhid", hf, b), tt), "D")
                            for k in range(4):
                                last = nc.tensor.transpose(bk[:, k * P:k * P + P], hnat[:, tt, k * P:k * P + P], ident)
                            last.then_inc(tp_done, 1)

                    for b in range(4):
                        gemm(("f_up", hf, b), "A", xT1, xT2)
                        if b:
                            turn(b - 1)
                    result((("fhid", hf, 2), 1))
                    gemm(("f_down", hf, 0), "D", hid1, hid2,
                         between=lambda: (turn(3), result((("fhid", hf, 3), 1))))
                    gemm(("f_down", hf, 1), "D", hid1, hid2)

            pe.wait_ge(setup, SETUP)
            turn_norm("n0", 1)
            for c in range(2):
                gemm(("pool_in", c), "A", xT1, xT2)
            pe.wait_ge(acc_free["A"], 2)
            for g in range(4):
                b = tp_bank(("pool", g), "D")
                for j in range(2):
                    ch = 2 * g + j
                    nc.tensor.matmul(b[:, j * S:j * S + S], pool_u[:, 0, ch * P:ch * P + P], pool_m[:, 0, g, :],
                                     start=True, stop=False)
                    last = nc.tensor.matmul(b[:, j * S + P:j * S + S], pool_u[:, 1, ch * P:ch * P + P],
                                            pool_m[:, 1, g, P:S], start=False, stop=True)
                last.then_inc(tp_done, 1)
            result(("pool", 3))
            for c in range(2):
                first = cbs["pool_out", c][0]
                g = len(groups)
                o = groups[g - 2]
                pe.wait_ge(acc_free[o], groups[:g - 1].count(o))
                groups.append("D")
                banks = acc[2 * (g % 2):2 * (g % 2) + 2]
                group_of["pool_out", c] = (banks, first + 1, "D", groups.count("D"))
                pe.wait_ge(split_lo, first + 1)
                s = first % SPL
                for tt in range(NT):
                    for w in range(2):
                        for k in range(2):
                            ch = 4 * c + 2 * w + k
                            o = banks[tt][:, w * 256:w * 256 + 256]
                            b1 = w_hi[:, s, (2 * w + k) * 256:(2 * w + k + 1) * 256]
                            b2 = w_lo[:, s, (2 * w + k) * 256:(2 * w + k + 1) * 256]
                            x1, x2 = xT1[:, ch, tt * P:tt * P + P], xT2[:, ch, tt * P:tt * P + P]
                            nc.tensor.matmul(o, x1, b2, start=k == 0, stop=False)
                            nc.tensor.matmul(o, x2, b1, start=False, stop=False)
                            last = nc.tensor.matmul(o, x1, b1, start=False, stop=k == 1)
                last.then_inc(used, 1)
            turn_norm("n1", 2)
            for hf, (f0, blocks) in enumerate(FF_HALVES):
                nb = len(blocks)
                for b in range(nb):
                    gemm(("gate", hf, b), "A", xT1, xT2)
                    if b:
                        turn_hidden(("hid", hf, b - 1), ("up", hf, b - 1))
                    gemm(("up", hf, b), "D", xT1, xT2)
                result((("hid", hf, nb - 2), 1))
                gemm(("down", hf, 0), "D", hid1, hid2,
                     between=lambda: (turn_hidden(("hid", hf, nb - 1), ("up", hf, nb - 1)),
                                      result((("hid", hf, nb - 1), 1))))
                gemm(("down", hf, 1), "D", hid1, hid2)

            turn_norm("n2", 3)
            deltanet()
            experts()
            second_block()

        @block.sync
        def _(sp):
            sp.dma_start(h[:], t["x"][0].rearrange("(t p) d -> p t d", p=P)).then_inc(x_in, 16)

            def load(tiles):
                for i in tiles:
                    src, kc, n = stream[i]
                    if i >= RAW:
                        sp.wait_ge(split_lo, i - RAW + 1)
                    dst = raw[:, i % RAW, 0:kc * n].rearrange("p (k n) -> p k n", k=kc)
                    sp.dma_start(dst, src).then_inc(landed[i % RAW], 16)

            def load_expert(j, e):
                w, r, c = m_tiles[j % MT]
                sp.dma_start(raw[:, j % RAW, :].rearrange("p (k n) -> p k n", k=KC),
                             t[w][0, bass.ds(e, 1), r:r + KC * P, c:c + CB].rearrange("e (k p) n -> p (e k) n", p=P))\
                  .then_inc(m_landed[j % RAW], 16)

            load(range(NA))
            for j in range(SPL):
                sp.wait_ge(split_lo, max(i for i in range(NA) if i % RAW == j) + 1)
                load_expert(j, 0)
            sp.wait_ge(split_lo, NA)
            sp.wait_ge(items_ready, 1)
            n = n_items(sp)
            with sp.Fori(0, n) as i:
                now = sp.value_load(item_i[0:1, bass.ds(i, 1)], min_val=0, max_val=NE - 1)
                after = sp.value_load(item_i[0:1, bass.ds(i + 1, 1)], min_val=0, max_val=NE - 1)
                for j in range(SPL, MT + SPL):
                    if j == 4 * FB:
                        now = sp.value_load(item_i[0:1, bass.ds(i, 1)], min_val=0, max_val=NE - 1)
                    sp.wait_ge(m_lo, i * MT + (1 + max(0, j - RAW + 1)))
                    sp.wait_ge(items_ready, 1)
                    load_expert(j, now if j < MT else after)
            sp.wait_ge(m_lo, n * MT + (SPL + 1))
            sp.wait_ge(moe_done, 1)
            sp.dma_start(mem_in[:], t["mem_2"][0].rearrange("(t p) d -> p t d", p=P)).then_inc(mem_loaded, 16)
            load(range(NA, len(stream)))
            sp.wait_ge(out_done, 1)
            sp.dma_start(out[0].rearrange("(t p) d -> p t d", p=P), h[:]).then_inc(x_in, 16)
            sp.wait_ge(x_in, 32)

        @block.scalar
        def _(act):
            act.dma_start(cst[:], t["consts"]).then_inc(setup, 16)
            act.dma_start(pool_m[:].rearrange("p a b c -> p (a b c)"), t["pool_mix"]).then_inc(setup, 16)
            act.dma_start(col[:], t["cols"]).then_inc(setup, 16)
            act.dma_start(row[:], t["rows"].broadcast_to((P, N_ROW))).then_inc(setup, 16)
            act.dma_start(w_ba[:], t["dn_w_in"][0, :, 4 * D:4 * D + 16].rearrange("(k p) n -> p k n", p=P))\
               .then_inc(setup, 16)
            act.dma_start(w_router[:], t["moe_router_w"][0].rearrange("(k p) n -> p k n", p=P)).then_inc(setup, 16)
            act.dma_start(w_forget[:], t["w_in_2"][0, :, 3072:3080].rearrange("(k p) n -> p k n", p=P))\
               .then_inc(setup, 16)
            act.wait_ge(setup, SETUP)
            told = {}
            state = {"split": 0, "limit": NA, "own": 0, "hi": 0}

            def tell(ins, signal):
                told[signal] = told.get(signal, 0) + 1
                ins.then_inc(signal, 1)
                act.wait_ge(signal, told[signal])

            def own(ins):
                tell(ins, a_own)

            def split_to(n):
                n = min(n, state["limit"])
                for i in range(state["split"], n):
                    _, kc, w = stream[i]
                    act.wait_ge(landed[i % RAW], 16 * (i // RAW + 1))
                    if i >= SPL:
                        act.wait_ge(used, i - SPL + 1)
                    nc.scalar.activation(w_hi[:, i % SPL, 0:kc * w], raw[:, i % RAW, 0:kc * w], ACT.Copy)\
                        .then_inc(split_hi, 1)
                state["split"] = max(n, state["split"])

            def after(name):
                banks, end = group_of[name][:2]
                split_to(end + SPL - 1)
                act.wait_ge(used, end)
                return banks

            def batch(name):
                b, n, _, _ = batch_of[name]
                act.wait_ge(tp_done, n)
                return b

            def whole(name):
                split_to(group_of[name][1] + SPL)
                act.wait_ge(acc_free["D"], group_of[name][3])

            def square_sum(src, k):
                for tt in range(NT):
                    tell(nc.scalar.activation(xn[:, tt, :], src[:, tt, :], ACT.Square,
                                              accum_out=small[:, k + tt:k + tt + 1]), sq_done)

            def rsqrt_seed(o, v):
                own(nc.scalar.activation(o, v, ACT.Ln))
                tell(nc.scalar.activation(o, o, ACT.Exp, scale=-0.5), rs_done)

            def norm_turn(tag, gain, step=1):
                for p in range(KD // 2):
                    b = batch((tag, p))
                    if gain is None:
                        tell(nc.scalar.activation(xT1[:, 2 * p:2 * p + 2, :],
                                                  b[:, :].rearrange("p (a b) -> p a b", a=2), ACT.Copy), hi_out)
                        continue
                    for j in range(2):
                        tell(nc.scalar.activation(xT1[:, 2 * p + j, :], b[:, j * S:j * S + S], ACT.Copy,
                                                  scale=G(gain, step * (2 * p + j))), hi_out)

            def result(name):
                _, _, owner, n = batch_of[name]
                act.wait_ge(tp_free[owner], n)

            def keep(name, dst):
                tell(nc.scalar.activation(dst, batch(name)[:, :].rearrange("p (a b) -> p a b", a=4), ACT.Copy),
                     tp_free["A"])

            def deltanet():
                result("ba")
                own(nc.scalar.activation(dnv[:, V_BETA, :], dnv[:, V_BETA, :], ACT.Exp, scale=-1.0))
                own(nc.scalar.activation(dnv[:, V_EA, 0:8], R("alog"), ACT.Exp))
                act.wait_ge(small_dve, 1)
                own(nc.scalar.activation(dnv[:, V_E, :], dnv[:, V_E, :], ACT.Exp))
                tell(nc.scalar.activation(dnv[:, V_E, :], dnv[:, V_E, :], ACT.Ln, bias=1.0), small_act)

                def conv(c):
                    for j in range(2):
                        b = batch(("conv", c, j))
                        for k in range(2):
                            ch = 4 * c + 2 * j + k
                            tell(nc.scalar.activation(qkvT[ch // 8][:, ch % 8, :], b[:, k * S:k * S + S], ACT.Copy,
                                                      scale=G("conv", 4 * ch + 3)), hi_out)
                    for j in range(2):
                        result(("conv", c, j))
                        ch = 4 * c + 2 * j
                        x = qkvT[ch // 8][:, ch % 8:ch % 8 + 2, :]
                        tell(nc.scalar.activation(x, x, ACT.Silu), silu_done)

                for c in range(8):
                    banks = after(("dn_in", c))
                    if c < 6:
                        if c >= 2:
                            result(("conv", c - 2, 1))
                        else:
                            result(("n2", KD // 2 - 1))
                        for tt in range(NT):
                            tell(nc.scalar.activation(xn[:, c % 2, tt * CB:tt * CB + CB], banks[tt][:, :], ACT.Copy),
                                 acc_free["A"] if tt else a_own)
                    else:
                        for tt in range(NT):
                            tell(nc.scalar.activation(z_s[:, tt, (c - 6) * CB:(c - 5) * CB], banks[tt][:, :], ACT.Silu),
                                 acc_free["A"] if tt else a_own)
                    if 1 <= c <= 6:
                        conv(c - 1)
                for m in range(2):
                    tell(nc.scalar.activation(squares[:, 8 * m:8 * m + 8, :], qkvT[m][:, :, :], ACT.Square), o_squared)
                act.wait_ge(small_dve, 4)
                own(nc.scalar.activation(dnv[:, V_R:V_R + 2, :], dnv[:, V_SS:V_SS + 2, :], ACT.Ln))
                tell(nc.scalar.activation(dnv[:, V_R:V_R + 2, :], dnv[:, V_R:V_R + 2, :], ACT.Exp, scale=-0.5), small_act)
                own(nc.scalar.activation(dnv[:, V_EGC, :], dnv[:, V_GC, :], ACT.Exp))
                tell(nc.scalar.activation(dnv[:, V_EKD, :], dnv[:, V_EKD, :], ACT.Exp), small_act)
                for n, dst in (("vn", vn), ("kn", kn)):
                    for tt in range(NT):
                        for hg in range(2):
                            keep((n, tt, hg), dst[:, tt, 4 * hg:4 * hg + 4, :])
                for tt in range(NT):
                    for hg in range(2):
                        act.wait_ge(dec_min, 2 * tt + hg + 1)
                        x = buf["dec", hg][:, :, :]
                        tell(nc.scalar.activation(x, x, ACT.Exp), dec_exp)
                    for hg in range(2):
                        keep(("T", tt, hg), buf["T", hg][:, :, :])
                    for l in range(1, len(LEVELS)):
                        for hg in range(2):
                            keep(("X", tt, hg, l), buf["X", hg][:, :, :])
                    for hg in range(2):
                        keep(("vnew", tt, hg), buf["X", hg][:, :, :])
                    if tt == 0:
                        for hg in range(2):
                            keep(("state", 0, hg), memory_s[:, 4 * hg:4 * hg + 4, :])
                for tt in range(NT):
                    act.wait_ge(o_done, 2 * tt + 2)
                    tell(nc.scalar.activation(o_sq[:, tt, :], xn[:, tt, :], ACT.Square), o_squared)
                act.wait_ge(small_dve, 5)
                own(nc.scalar.activation(dnv[:, V_R, :], dnv[:, V_SS, :], ACT.Ln))
                tell(nc.scalar.activation(dnv[:, V_R, :], dnv[:, V_R, :], ACT.Exp, scale=-0.5), small_act)
                norm_turn("o", "dn_norm", 0)

            def experts():
                act.dma_start(R("scale"), t["rows2"].broadcast_to((P, D))).then_inc(gain_in, 16)
                whole(("dn_out", 1))
                square_sum(h, 0)
                act.wait_ge(v_done, 4)
                rsqrt_seed(small[:, 4:6], small[:, 2:4])
                norm_turn("n3", None)
                act.wait_ge(route_dve, 1)
                tell(nc.scalar.activation(rt[:, R_EXP:R_EXP + 2, :], rt[:, R_EXP:R_EXP + 2, :], ACT.Exp), route_act)
                for half in range(2):
                    b = batch(("gather", half))
                    tell(nc.scalar.activation(xT1[:, 4 * half:4 * half + 4, 0:P],
                                              b[:, :].rearrange("p (a b) -> p a b", a=4), ACT.Copy), hi_out)
                act.wait_ge(used, NA)

                def split(j, i):
                    act.wait_ge(m_landed[j % RAW], i * (16 * MT // RAW) + 16 * (j // RAW + 1))
                    if j >= SPL:
                        act.wait_ge(m_used, i * MT + (j - SPL + 1))
                    nc.scalar.activation(w_hi[:, j % SPL, :], raw[:, j % RAW, :], ACT.Copy).then_inc(m_hi, 1)

                for j in range(SPL):
                    split(j, 0)
                n = n_items(act)
                with act.Fori(0, n) as i:
                    at_ = [SPL]

                    def split_until(j):
                        for k in range(at_[0], j):
                            split(k, i)
                        at_[0] = max(at_[0], j)

                    def turned(f):
                        bi = TURN + f if f < 6 else TURN6
                        act.wait_ge(m_tp, i * M_BANKS + (bi + 1))
                        nc.scalar.activation(hidden1[:, 4 * f * P:4 * (f + 1) * P], tp[bi % 4][:, :], ACT.Copy)\
                            .then_inc(m_turned, 1)

                    for f in range(FB):
                        split_until(4 * f + 2 + SPL - 1)
                        act.wait_ge(m_used, i * MT + (4 * f + 2))
                        if f > 1:
                            act.wait_ge(m_up, i * FB + (f - 1))
                        nc.scalar.activation(gate_s[:, f % 2, :], acc[2 * (f % 2)][:, :], ACT.Silu).then_inc(m_gate, 1)
                        if f:
                            turned(f - 1)
                        else:
                            split_until(4 + SPL - 1)
                            act.wait_ge(m_tp, i * M_BANKS + (SPREAD + 1))
                            nc.scalar.activation(spread[:, :, :],
                                                 tp[SPREAD % 4][:, 0:NT * P].rearrange("p (a b) -> p a b", a=NT),
                                                 ACT.Copy).then_inc(m_spread, 1)
                    split_until(4 * FB + SPL - 1)
                    for half in range(2):
                        bi = GATHER + half
                        act.wait_ge(m_tp, i * M_BANKS + (bi + 1))
                        nc.scalar.activation(xT1[:, 4 * half:4 * half + 4, 0:P],
                                             tp[bi % 4][:, :].rearrange("p (a b) -> p a b", a=4), ACT.Copy)\
                            .then_inc(m_turned, 1)
                    split_until(4 * FB + 1 + SPL - 1)
                    turned(FB - 1)
                    for c in range(2):
                        split_until((5 + c) * FB + SPL - 1)
                        act.wait_ge(m_used, i * MT + (5 + c) * FB)
                        nc.scalar.activation(y_s[:, c, :], acc[2 + c][:, :], ACT.Copy).then_inc(m_y, 1)
                    split_until(MT + SPL)
                act.wait_ge(moe_done, 1)

            def second_block():
                state["limit"] = len(stream)
                act.wait_ge(mem_loaded, 16)
                square_sum(mem_in, 0)
                act.wait_ge(v_done, 5)
                rsqrt_seed(small[:, 4:6], small[:, 2:4])
                norm_turn("mm", "mem2")

                def headed(name):
                    banks = after(("b_in", name))
                    if name in KEPT:
                        for tt in range(NT):
                            tell(nc.scalar.activation(KEPT[name][:, tt, :], banks[tt][:, :], ACT.Copy),
                                 acc_free["A"] if tt else a_own)
                        return
                    x = xn[:, STAGE[name], :]
                    for tt in range(NT):
                        tell(nc.scalar.activation(x[:, tt * CB:tt * CB + CB], banks[tt][:, :], ACT.Copy),
                             acc_free["A"] if tt else a_own)
                    if name in NORMED:
                        q = NORMED.index(name)
                        if q:
                            act.wait_ge(h_sq_v, q)
                        for tt in range(NT):
                            tell(nc.scalar.activation(head_sq[:, tt, :], x[:, tt * CB:tt * CB + CB], ACT.Square), h_square)
                        act.wait_ge(h_sq_v, q + 1)
                        n = NT * CB // HEADED[name][1]
                        own(nc.scalar.activation(hs[:, 1, 0:n], hs[:, 0, 0:n], ACT.Ln))
                        tell(nc.scalar.activation(hs[:, 1, 0:n], hs[:, 1, 0:n], ACT.Exp, scale=-0.5), h_rs)

                headed("mk")
                headed("mv")
                square_sum_after(("heads", "mk", 1), 6)
                act.wait_ge(h_done, 6)
                square_sum(h, 0)
                act.wait_ge(v_done, 7)
                rsqrt_seed(small[:, 4:6], small[:, 2:4])
                norm_turn("m2", "mix2")
                act.wait_ge(fox_dve, 1)
                own(nc.scalar.activation(fx[:, F_E, :], fx[:, F_E, :], ACT.Exp))
                tell(nc.scalar.activation(fx[:, F_E, :], fx[:, F_E, :], ACT.Ln, bias=1.0), fox_act)
                prev = {0: None, 1: None}
                for c, (name, _) in enumerate(B_IN):
                    if name in HEADED and prev[c % 2]:
                        split_to(group_of["b_in", name][1] + SPL - 1)
                        result(("heads", prev[c % 2], 1))
                    if name in HEADED:
                        prev[c % 2] = name
                    headed(name)
                for pair in range(4):
                    hd = (2 * pair, 2 * pair + 1)
                    for hh in hd:
                        if pair == 0:
                            result(("heads", "mq", 1))
                        else:
                            result(("sb_o", pair - 1))
                        b = batch(("sb_z", hh))
                        own(nc.scalar.activation(xn[:, hh % 2, 0:3 * P], b[:, 0:3 * P], ACT.Copy, scale=SB_HD ** -0.5))
                        tell(nc.scalar.activation(third[:, hh % 2, :], b[:, 0:3 * P], ACT.Abs, scale=SB_HD ** -0.5),
                             tp_free["A"])
                        own(nc.scalar.activation(third[:, hh % 2, :], third[:, hh % 2, :], ACT.Exp, scale=-1.0))
                        tell(nc.scalar.activation(third[:, hh % 2, :], third[:, hh % 2, :], ACT.Ln, bias=1.0), sb_l)
                    for hh in hd:
                        act.wait_ge(sb_a, hh + 1)
                        x = xn[:, hh % 2, 0:3 * P]
                        tell(nc.scalar.activation(x, x, ACT.Exp), sb_wx)

                def softmax_exp(n, hh, parts):
                    act.wait_ge(sm_z, n + 1)
                    for tt, cols in enumerate(parts):
                        x = xn[:, hh % 2, cols]
                        tell(nc.scalar.activation(x, x, ACT.Exp, bias=st[:, hh % 2 * 2 + tt, 0:1],
                                                  accum_out=st[:, hh % 2 * 2 + tt, 1:2]), sm_p if tt else a_own)

                for pair in range(4):
                    hd = (2 * pair, 2 * pair + 1)
                    for hh in hd:
                        softmax_exp(hh, hh, (slice(0, P), slice(P, 3 * P)))
                    for hh in hd:
                        b = batch(("fx_t", hh))
                        tell(nc.scalar.activation(xn[:, hh % 2, 3 * P:6 * P], b[:, 0:3 * P], ACT.Copy), tp_free["A"])
                for pair in range(2):
                    hd = (2 * pair, 2 * pair + 1)
                    for hh in hd:
                        softmax_exp(8 + hh, hh, (slice(0, S), slice(S, 2 * S)))
                    for hh in hd:
                        b = batch(("mm_t", hh))
                        tell(nc.scalar.activation(xn[:, hh % 2, 4 * P:8 * P], b[:, :], ACT.Copy), tp_free["A"])
                for br in range(3):
                    for j in range(2):
                        b = batch(("oT", br, j))
                        tell(nc.scalar.activation(oT1[br][:, 2 * j:2 * j + 2, :],
                                                  b[:, :].rearrange("p (a b) -> p a b", a=2), ACT.Copy), hi_out)
                last_branch = None
                for c in range(2):
                    for br in range(3):
                        banks = after(("b_gate", br, c))
                        if last_branch:
                            act.wait_ge(acc_free["D"], group_of[last_branch][3])
                            act.wait_ge(merged, last_branch[1] + 3 * last_branch[2] + 1)
                        last_branch = ("branch", br, c)
                        for tt in range(NT):
                            tell(nc.scalar.activation(gate2[:, tt, :], banks[tt][:, :], ACT.Sigmoid),
                                 acc_free["A"] if tt else a_own)
                split_to(group_of["branch", 2, 1][1] + SPL)
                norm_turn("mg", None)
                whole(("b_out", 1))
                square_sum(h, 0)
                act.wait_ge(v_done, 8)
                rsqrt_seed(small[:, 4:6], small[:, 2:4])
                norm_turn("m3", "mlp2")
                for hf in range(2):
                    def turned(b):
                        for tt in range(NT):
                            bk = batch((("fhid", hf, b), tt))
                            tell(nc.scalar.activation(hid1[:, 4 * b:4 * b + 4, tt * P:tt * P + P],
                                                      bk[:, :].rearrange("p (k c) -> p k c", k=4), ACT.Copy), hi_out)

                    for b in range(4):
                        banks = after(("f_up", hf, b))
                        if hf or b:
                            act.wait_ge(relu_sq, 2 * (4 * hf + b))
                        for tt in range(NT):
                            tell(nc.scalar.activation(gate_s[:, tt, :], banks[tt][:, :], ACT.Relu),
                                 acc_free["A"] if tt else a_own)
                        if b:
                            turned(b - 1)
                    split_to(cbs["f_down", hf, 0][0] + 1 + SPL)
                    turned(3)
                split_to(len(stream))

            def square_sum_after(name, v):
                result(name)
                square_sum(h, 0)
                act.wait_ge(v_done, v)
                rsqrt_seed(small[:, 4:6], small[:, 2:4])

            act.wait_ge(x_in, 16)
            square_sum(h, 0)
            act.wait_ge(v_done, 1)
            rsqrt_seed(small[:, 4:6], small[:, 2:4])
            split_to(SPL)
            norm_turn("n0", "mix0")
            for c in range(2):
                banks = after(("pool_in", c))
                own(nc.scalar.activation(pool_u[:, 0, c * CB:c * CB + CB], banks[0][:, :], ACT.Copy))
                tell(nc.scalar.activation(pool_u[:, 1, c * CB:c * CB + CB], banks[1][:, :], ACT.Copy), acc_free["A"])
            for g in range(4):
                b = batch(("pool", g))
                tell(nc.scalar.activation(xT1[:, 2 * g:2 * g + 2, :], b[:, :].rearrange("p (a b) -> p a b", a=2),
                                          ACT.Copy), hi_out)
            split_to(cbs["pool_out", 1][1] + SPL)
            act.wait_ge(h_done, 4)
            square_sum(h, 0)
            act.wait_ge(v_done, 2)
            rsqrt_seed(small[:, 4:6], small[:, 2:4])
            norm_turn("n1", "ffn0")
            last_up = None
            for hf, (f0, blocks) in enumerate(FF_HALVES):
                nb = len(blocks)

                def hidden(b):
                    for tt in range(NT):
                        bk = batch((("hid", hf, b), tt))
                        n = cbs["up", hf, b][2] // P
                        tell(nc.scalar.activation(hid1[:, 4 * b:4 * b + n, tt * P:tt * P + P],
                                                  bk[:, 0:n * P].rearrange("p (k c) -> p k c", k=n), ACT.Copy), hi_out)

                for b in range(nb):
                    banks = after(("gate", hf, b))
                    n = cbs["gate", hf, b][2]
                    if last_up:
                        act.wait_ge(acc_free["D"], group_of[last_up][3])
                    last_up = ("up", hf, b)
                    own(nc.scalar.activation(gate_s[:, 0, 0:n], banks[0][:, 0:n], ACT.Silu))
                    tell(nc.scalar.activation(gate_s[:, 1, 0:n], banks[1][:, 0:n], ACT.Silu), acc_free["A"])
                    if b:
                        hidden(b - 1)
                split_to(cbs["down", hf, 0][0] + 1 + SPL)
                hidden(nb - 1)
            whole(("down", 1, 1))
            square_sum(h, 0)
            act.wait_ge(v_done, 3)
            rsqrt_seed(small[:, 4:6], small[:, 2:4])
            norm_turn("n2", "mix1")
            deltanet()
            experts()
            second_block()

        @block.vector
        def _(dve):
            dve.wait_ge(setup, SETUP)
            told = {}
            state = {"split": 0, "limit": NA, "own": 0, "hi": 0, "sq": 0, "rs": 0, "acc": 0}

            def tell(ins, signal):
                told[signal] = told.get(signal, 0) + 1
                ins.then_inc(signal, 1)
                dve.wait_ge(signal, told[signal])

            def own(ins):
                tell(ins, d_own)

            def split_to(n):
                n = min(n, state["limit"])
                for i in range(state["split"], n):
                    _, kc, w = stream[i]
                    dve.wait_ge(split_hi, i + 1)
                    nc.vector.tensor_tensor(w_lo[:, i % SPL, 0:kc * w], raw[:, i % RAW, 0:kc * w],
                                            w_hi[:, i % SPL, 0:kc * w], ALU.subtract).then_inc(split_lo, 1)
                state["split"] = max(n, state["split"])

            def after(name):
                banks, end = group_of[name][:2]
                split_to(end + SPL - 1)
                dve.wait_ge(used, end)
                return banks

            def high(n=1):
                state["hi"] += n
                dve.wait_ge(hi_out, state["hi"])

            def rstd(k, scale):
                ss, v, y, u = (small[:, k + 2 * j:k + 2 * j + 2] for j in range(4))
                state["sq"] += 2
                dve.wait_ge(sq_done, state["sq"])
                tell(nc.vector.tensor_scalar(v, ss, scale, EPS, ALU.mult, ALU.add), v_done)
                state["rs"] += 1
                dve.wait_ge(rs_done, state["rs"])
                own(nc.vector.tensor_tensor(u, y, y, ALU.mult))
                own(nc.vector.tensor_tensor(u, u, v, ALU.mult))
                own(nc.vector.tensor_scalar(u, u, -0.5, 1.5, ALU.mult, ALU.add))
                own(nc.vector.tensor_tensor(y, y, u, ALU.mult))
                return y

            def normed(src, k=0):
                y = rstd(k, 1.0 / D)
                for tt in range(NT):
                    tell(nc.vector.tensor_scalar(xn[:, tt, :], src[:, tt, :], y[:, tt:tt + 1], None, ALU.mult), xn_done)

            def norm_turn(tag, gain, step=1):
                for p in range(KD // 2):
                    b = batch_of[tag, p][0]
                    if gain is None:
                        high()
                        tell(nc.vector.tensor_tensor(xT2[:, 2 * p:2 * p + 2, :],
                                                     b[:, :].rearrange("p (a b) -> p a b", a=2),
                                                     xT1[:, 2 * p:2 * p + 2, :].bitcast(F32), ALU.subtract),
                             tp_free["D"])
                        continue
                    high(2)
                    for j in range(2):
                        tell(nc.vector.scalar_tensor_tensor(
                            out=xT2[:, 2 * p + j, :], in0=b[:, j * S:j * S + S], scalar=G(gain, step * (2 * p + j)),
                            in1=xT1[:, 2 * p + j, :].bitcast(F32), op0=ALU.mult, op1=ALU.subtract),
                            tp_free["D"] if j else d_own)

            def result(name):
                _, _, owner, n = batch_of[name]
                dve.wait_ge(tp_free[owner], n)

            def batch(name):
                b, n, owner, m = batch_of[name]
                assert owner == "D" and m == told.get(tp_free["D"], 0) + 1, name
                dve.wait_ge(tp_done, n)
                return b

            def bank4(name):
                return batch(name)[:, :].rearrange("p (a b) -> p a b", a=4)

            def newton(y, v, u):
                own(nc.vector.tensor_tensor(u, y, y, ALU.mult))
                own(nc.vector.tensor_tensor(u, u, v, ALU.mult))
                own(nc.vector.tensor_scalar(u, u, -0.5, 1.5, ALU.mult, ALU.add))
                own(nc.vector.tensor_tensor(y, y, u, ALU.mult))

            def deltanet():
                b = batch("ba")
                ba = b[:, 0:32].rearrange("p (t a h) -> p t a h", t=NT, a=2)
                wide = lambda v: dnv[:, v, :].rearrange("p (t h) -> p t h", t=NT)
                own(nc.vector.tensor_copy(wide(V_X), ba[:, :, 1, :]))
                tell(nc.vector.tensor_copy(wide(V_BETA), ba[:, :, 0, :]), tp_free["D"])
                own(nc.vector.tensor_tensor(wide(V_X), wide(V_X), R("dt").unsqueeze(1).broadcast_to((P, NT, 8)), ALU.add))
                own(nc.vector.tensor_scalar(dnv[:, V_M, :], dnv[:, V_X, :], 0.0, None, ALU.max))
                tell(nc.vector.scalar_tensor_tensor(out=dnv[:, V_E, :], in0=dnv[:, V_M, :], scalar=-2.0,
                                                    in1=dnv[:, V_X, :], op0=ALU.mult, op1=ALU.add), small_dve)
                dve.wait_ge(small_act, 1)
                own(nc.vector.tensor_scalar(dnv[:, V_BETA, :], dnv[:, V_BETA, :], 1.0, None, ALU.add))
                own(nc.vector.reciprocal(dnv[:, V_BETA, :], dnv[:, V_BETA, :]))
                own(nc.vector.tensor_tensor(dnv[:, V_M, :], dnv[:, V_M, :], dnv[:, V_E, :], ALU.add))
                tell(nc.vector.scalar_tensor_tensor(out=wide(V_G), in0=wide(V_M), scalar=-1.0,
                                                    in1=dnv[:, V_EA, 0:8].unsqueeze(1).broadcast_to((P, NT, 8)),
                                                    op0=ALU.mult, op1=ALU.mult), small_dve)

                def conv(c):
                    for j in range(2):
                        b = batch(("conv", c, j))
                        high(2)
                        for k in range(2):
                            ch = 4 * c + 2 * j + k
                            for back in range(1, CONV):
                                o = qkvT[ch // 8][:, ch % 8, back:S]
                                tell(nc.vector.scalar_tensor_tensor(
                                    out=o, in0=b[:, k * S:k * S + S - back], scalar=G("conv", 4 * ch + 3 - back),
                                    in1=o, op0=ALU.mult, op1=ALU.add),
                                    tp_free["D"] if k == 1 and back == CONV - 1 else d_own)

                for c in range(8):
                    split_to(group_of["dn_in", c][1] + SPL - 1)
                    if 1 <= c <= 6:
                        conv(c - 1)
                    if c == 2:
                        b = batch("gc")
                        own(nc.vector.tensor_copy(dnv[:, V_GC:V_GC + 2, :], b[:, 0:32].rearrange("p (a b) -> p a b", a=2)))
                        tell(nc.vector.tensor_tensor(dnv[:, V_EKD, :], b[:, 16:32], dnv[:, V_GC, :], ALU.subtract),
                             tp_free["D"])
                        tell(nc.vector.memset(small[:, 250:251], 0.0), small_dve)
                b = batch("ssq")
                tell(nc.vector.tensor_scalar(dnv[:, V_SS:V_SS + 2, :], b[:, 0:32].rearrange("p (a b) -> p a b", a=2),
                                             EPS, None, ALU.add), tp_free["D"])
                tell(nc.vector.memset(small[:, 250:251], 0.0), small_dve)
                dve.wait_ge(small_act, 2)
                newton(dnv[:, V_R:V_R + 2, :], dnv[:, V_SS:V_SS + 2, :], dnv[:, V_TMP:V_TMP + 2, :])
                tell(nc.vector.tensor_scalar(dnv[:, V_R, :], dnv[:, V_R, :], float(P) ** -0.5, None, ALU.mult), rs_ready)
                for m in range(2):
                    for p in range(4):
                        b = batch(("unit", m, p))
                        x = qkvT[m][:, 2 * p:2 * p + 2, :]
                        tell(nc.vector.tensor_tensor(x, b[:, :].rearrange("p (a b) -> p a b", a=2), x, ALU.mult),
                             tp_free["D"])
                dve.wait_ge(small_act, 3)

                def by_token(v, tt, hg):
                    return dnv[:, v, tt * 8 + 4 * hg:tt * 8 + 4 * hg + 4].unsqueeze(2).broadcast_to((P, 4, P))

                def by_head(m):
                    return m.unsqueeze(1).broadcast_to((P, 4, P))

                def level(l, hg):
                    tell(nc.vector.tensor_tensor(buf["dec", hg][:, :, :], buf["A", hg][:, :, :],
                                                 by_head(C("levels")[:, l * P:l * P + P]), ALU.mult), inv_level)

                for tt in range(NT):
                    for hg in range(2):
                        dec = buf["dec", hg][:, :, :]
                        tell(nc.vector.tensor_tensor(dec, bank4(("decay", tt, hg)), by_token(V_GC, tt, hg), ALU.subtract),
                             tp_free["D"])
                        tell(nc.vector.tensor_scalar(dec, dec, 0.0, None, ALU.min), dec_min)
                    for hg in range(2):
                        dec = buf["dec", hg][:, :, :]
                        dve.wait_ge(dec_exp, 2 * tt + hg + 1)
                        own(nc.vector.tensor_tensor(dec, dec, by_head(C("upto")), ALU.mult))
                        a = buf["A", hg][:, :, :]
                        tell(nc.vector.tensor_tensor(a, bank4(("kk", tt, hg)), dec, ALU.mult), tp_free["D"])
                        tell(nc.vector.tensor_tensor(a, bank4(("beta", tt, hg)), a, ALU.mult), tp_free["D"])
                        tell(nc.vector.tensor_tensor(buf["qk", hg][:, :, :], bank4(("qk", tt, hg)), dec, ALU.mult),
                             tp_free["D"])
                        TT = buf["TT", hg][:, :, :]
                        own(nc.vector.tensor_tensor(TT, a, by_head(C("levels")[:, 0:P]), ALU.mult))
                        tell(nc.vector.tensor_tensor(TT, by_head(ident), TT, ALU.subtract), inv_first)
                        level(1, hg)
                    for l in range(1, len(LEVELS)):
                        for hg in range(2):
                            T, TT = buf["T", hg][:, :, :], buf["TT", hg][:, :, :]
                            if l < len(LEVELS) - 1:
                                tell(nc.vector.tensor_tensor(T, T, bank4(("inv_T", tt, hg, l)), ALU.subtract), tp_free["D"])
                            tell(nc.vector.tensor_tensor(TT, TT, bank4(("inv_TT", tt, hg, l)), ALU.subtract), tp_free["D"])
                            if l < len(LEVELS) - 1:
                                level(l + 1, hg)
                    for hg in range(2):
                        r = buf["A", hg][:, :, :]
                        v = vn[:, tt, 4 * hg:4 * hg + 4, :]
                        if tt:
                            tell(nc.vector.tensor_tensor(r, bank4(("kS", tt, hg)), by_token(V_EGC, tt, hg), ALU.mult),
                                 tp_free["D"])
                            own(nc.vector.tensor_tensor(r, v, r, ALU.subtract))
                            v = r
                            o = xn[:, tt, hg * CB:hg * CB + CB].rearrange("p (a b) -> p a b", a=4)
                            tell(nc.vector.tensor_tensor(o, bank4(("qS", tt, hg)), by_token(V_EGC, tt, hg), ALU.mult),
                                 tp_free["D"])
                        tell(nc.vector.tensor_tensor(r, v, by_token(V_BETA, tt, hg), ALU.mult), rhs_done)
                        if tt == 0:
                            tell(nc.vector.tensor_tensor(buf["T", hg][:, :, :], kn[:, tt, 4 * hg:4 * hg + 4, :],
                                                         by_token(V_EKD, tt, hg), ALU.mult), kdec_done)
                    for hg in range(2):
                        o = xn[:, tt, hg * CB:hg * CB + CB].rearrange("p (a b) -> p a b", a=4)
                        if tt:
                            tell(nc.vector.tensor_tensor(o, bank4(("o", tt, hg)), o, ALU.add), tp_free["D"])
                        else:
                            tell(nc.vector.tensor_copy(o, bank4(("o", tt, hg))), tp_free["D"])
                        tell(nc.vector.memset(small[:, 250:251], 0.0), o_done)
                for tt in range(NT):
                    dve.wait_ge(o_squared, 3 + tt)
                    own(nc.vector.tensor_reduce(dnv[:, V_SS, 8 * tt:8 * tt + 8],
                                                o_sq[:, tt, :].rearrange("p (a b) -> p a b", a=HEADS), AX, ALU.add))
                tell(nc.vector.tensor_scalar(dnv[:, V_SS, :], dnv[:, V_SS, :], 1.0 / P, EPS, ALU.mult, ALU.add), small_dve)
                dve.wait_ge(small_act, 4)
                newton(dnv[:, V_R, :], dnv[:, V_SS, :], dnv[:, V_TMP, :])
                for tt in range(NT):
                    o = xn[:, tt, :].rearrange("p (a b) -> p a b", a=HEADS)
                    own(nc.vector.tensor_tensor(o, o, dnv[:, V_R, 8 * tt:8 * tt + 8].unsqueeze(2).broadcast_to(
                        (P, HEADS, P)), ALU.mult))
                    tell(nc.vector.tensor_tensor(xn[:, tt, :], xn[:, tt, :], z_s[:, tt, :], ALU.mult), xn_done)
                norm_turn("o", "dn_norm", 0)
                for c in range(2):
                    add_to_h(("dn_out", c), c)

            def experts():
                y = rstd(0, 1.0 / D)
                dve.wait_ge(gain_in, 16)
                for tt in range(NT):
                    tell(nc.vector.scalar_tensor_tensor(out=xn[:, tt, :], in0=h[:, tt, :], scalar=y[:, tt:tt + 1],
                                                        in1=R("scale"), op0=ALU.mult, op1=ALU.mult), xn_done)
                norm_turn("n3", None)
                b = batch("router")
                lg = rt[:, R_LG:R_LG + 2, :]
                tell(nc.vector.tensor_tensor(lg, b[:, 0:16].rearrange("p (a b) -> p a b", a=2),
                                             R("router_b").unsqueeze(1).broadcast_to((P, NT, NE)), ALU.add), tp_free["D"])
                own(nc.vector.tensor_reduce(rt[:, R_MAX, 0:2], lg, AX, ALU.max))
                tell(nc.vector.tensor_tensor(rt[:, R_EXP:R_EXP + 2, :], lg,
                                             rt[:, R_MAX, 0:2].unsqueeze(2).broadcast_to((P, NT, NE)), ALU.subtract),
                     route_dve)
                jlt = C("jlt").rearrange("p (a b) -> p a b", a=NE)
                big, tie = rt[:, R_BIG:R_BIG + 8, :], rt[:, R_TIE:R_TIE + 8, :]
                for tt in range(NT):
                    other = rt[:, R_LG + tt, :].unsqueeze(1).broadcast_to((P, NE, NE))
                    this = rt[:, R_LG + tt, :].unsqueeze(2).broadcast_to((P, NE, NE))
                    own(nc.vector.tensor_tensor(big, other, this, ALU.is_gt))
                    own(nc.vector.tensor_tensor(tie, other, this, ALU.is_equal))
                    own(nc.vector.tensor_tensor(tie, tie, jlt, ALU.mult))
                    own(nc.vector.tensor_tensor(big, big, tie, ALU.add))
                    own(nc.vector.tensor_reduce(rt[:, R_RANK + tt, :], big, AX, ALU.add))
                sel = rt[:, R_SEL:R_SEL + 2, :]
                tell(nc.vector.tensor_scalar(sel, rt[:, R_RANK:R_RANK + 2, :], TOP_K - 0.5, None, ALU.is_lt), route_dve)
                dve.wait_ge(route_act, 1)
                gate = rt[:, R_EXP:R_EXP + 2, :]
                own(nc.vector.tensor_tensor(gate, gate, sel, ALU.mult))
                own(nc.vector.tensor_reduce(rt[:, R_MAX, 2:4], gate, AX, ALU.add))
                own(nc.vector.reciprocal(rt[:, R_MAX, 2:4], rt[:, R_MAX, 2:4]))
                own(nc.vector.tensor_tensor(item_gate[:, :, 0:NE], gate,
                                            rt[:, R_MAX, 2:4].unsqueeze(2).broadcast_to((P, NT, NE)), ALU.mult))
                b = batch("places")
                place = item_pos[:, :, 0:NE]
                cnt = rt[:, R_CNT, :]
                own(nc.vector.tensor_scalar(cnt, b[:, 16:24], P + 0.5, None, ALU.is_gt))
                tell(nc.vector.scalar_tensor_tensor(out=rt[:, R_LG:R_LG + 2, :],
                                                    in0=b[:, 0:16].rearrange("p (a b) -> p a b", a=2), scalar=1.0,
                                                    in1=sel, op0=ALU.add, op1=ALU.mult), tp_free["D"])
                own(nc.vector.tensor_scalar(place, lg, 1.0, None, ALU.subtract))
                own(nc.vector.tensor_tensor(tie, cnt.unsqueeze(1).broadcast_to((P, NE, NE)), jlt, ALU.mult))
                own(nc.vector.tensor_reduce(rt[:, R_RANK, :], tie, AX, ALU.add))
                own(nc.vector.memset(item_f[:, :], 0.0))
                own(nc.vector.tensor_copy(item_f[:, 0:NE], C("iota")[:, 0:NE]))
                own(nc.vector.tensor_reduce(item_f[:, 12:13], cnt, AX, ALU.add))
                own(nc.vector.tensor_scalar(item_f[:, 12:13], item_f[:, 12:13], float(NE), None, ALU.add))
                own(nc.vector.memset(item_pos[:, :, 11:12], -1.0))
                tell(nc.vector.memset(item_gate[:, :, 11:12], 0.0), m_lo)
                for r in range(MAX_ITEMS - NE):
                    own(nc.vector.tensor_scalar(rt[:, R_IND, :], rt[:, R_RANK, :], float(r), None, ALU.is_equal))
                    own(nc.vector.tensor_tensor(rt[:, R_IND, :], rt[:, R_IND, :], cnt, ALU.mult))
                    ind = rt[:, R_IND, :].unsqueeze(1).broadcast_to((P, NT, NE))
                    own(nc.vector.tensor_tensor(rt[:, R_TMP, :], rt[:, R_IND, :], C("iota")[:, 0:NE], ALU.mult))
                    own(nc.vector.tensor_reduce(item_f[:, NE + r:NE + r + 1], rt[:, R_TMP, :], AX, ALU.add))
                    for src, off, dst in ((item_pos, float(P), item_pos), (item_gate, 0.0, item_gate)):
                        own(nc.vector.tensor_tensor(rt[:, R_TMP:R_TMP + 2, :], src[:, :, 0:NE], ind, ALU.mult))
                        own(nc.vector.tensor_reduce(rt[:, R_MAX, 4:6], rt[:, R_TMP:R_TMP + 2, :], AX, ALU.add))
                        own(nc.vector.tensor_scalar(dst[:, :, NE + r], rt[:, R_MAX, 4:6], off, None, ALU.subtract))
                tell(nc.vector.tensor_copy(item_i[:, :], item_f[:, :]), items_ready)
                tell(nc.vector.memset(y_s[:, :, :], 0.0), m_y)
                tell(nc.vector.memset(spread[:, :, :], 0.0), m_read)

                def choose(item, done):
                    for tt in range(NT):
                        done(nc.vector.tensor_scalar(pick[:, tt, :], C("iota"), item_pos[:, tt, item], None,
                                                     ALU.is_equal))
                    for tt in range(NT):
                        done(nc.vector.tensor_scalar(pick_gate[:, tt, :], pick[:, tt, :], item_gate[:, tt, item], None,
                                                     ALU.mult))

                choose(slice(0, 1), lambda ins: tell(ins, picked0))
                for half in range(2):
                    b = batch(("gather", half))
                    high()
                    tell(nc.vector.tensor_tensor(xT2[:, 4 * half:4 * half + 4, 0:P],
                                                 b[:, :].rearrange("p (a b) -> p a b", a=4),
                                                 xT1[:, 4 * half:4 * half + 4, 0:P].bitcast(F32), ALU.subtract),
                         tp_free["D"])

                def split(j, i):
                    dve.wait_ge(m_hi, i * MT + (j + 1))
                    nc.vector.tensor_tensor(w_lo[:, j % SPL, :], raw[:, j % RAW, :], w_hi[:, j % SPL, :],
                                            ALU.subtract).then_inc(m_lo, 1)

                for j in range(SPL):
                    split(j, 0)
                n = n_items(dve)
                with dve.Fori(0, n) as i:
                    at_ = [SPL]
                    reads = [0]

                    def split_until(j):
                        for k in range(at_[0], j):
                            split(k, i)
                        at_[0] = max(at_[0], j)

                    def read(ins):
                        reads[0] += 1
                        ins.then_inc(m_read, 1)
                        dve.wait_ge(m_read, i * M_READS + (reads[0] + 1))

                    def turned(f):
                        bi = TURN + f if f < 6 else TURN6
                        dve.wait_ge(m_turned, i * 9 + (f + 1 if f < 6 else 9))
                        cols = slice(4 * f * P, 4 * (f + 1) * P)
                        read(nc.vector.tensor_tensor(hidden2[:, cols], tp[bi % 4][:, :], hidden1[:, cols].bitcast(F32),
                                                     ALU.subtract))

                    def scattered(bi, c):
                        for tt in range(NT):
                            dve.wait_ge(m_tp, i * M_BANKS + (bi + tt + 1))
                            hh = h[:, tt, c * CB:c * CB + CB]
                            read(nc.vector.tensor_tensor(hh, tp[(bi + tt) % 4][:, :], hh, ALU.add))

                    for f in range(FB):
                        split_until(4 * f + 2 + SPL - 1)
                        if f == 0:
                            scattered(SC1, 1)
                        else:
                            turned(f - 1)
                        split_until(4 * f + 4 + SPL - 1)
                        dve.wait_ge(m_used, i * MT + (4 * f + 4))
                        dve.wait_ge(m_gate, i * FB + (f + 1))
                        if f > 1:
                            dve.wait_ge(m_tp, i * M_BANKS + (TURN + f - 1))
                        nc.vector.tensor_tensor(hnat[:, f % 2, :], acc[2 * (f % 2) + 1][:, :], gate_s[:, f % 2, :],
                                                ALU.mult).then_inc(m_up, 1)
                        if f == FB - 2:
                            picks = [0]

                            def done(ins):
                                picks[0] += 1
                                ins.then_inc(m_pick, 1)
                                dve.wait_ge(m_pick, i * 4 + picks[0])

                            choose(bass.ds(i + 1, 1), done)
                    for half in range(2):
                        bi = GATHER + half
                        dve.wait_ge(m_turned, i * 9 + (7 + half))
                        read(nc.vector.tensor_tensor(xT2[:, 4 * half:4 * half + 4, 0:P],
                                                     tp[bi % 4][:, :].rearrange("p (a b) -> p a b", a=4),
                                                     xT1[:, 4 * half:4 * half + 4, 0:P].bitcast(F32), ALU.subtract))
                    split_until(4 * FB + 1 + SPL - 1)
                    turned(FB - 1)
                    split_until(5 * FB + 2 + SPL - 1)
                    scattered(SC0, 0)
                    split_until(MT + SPL)
                    assert reads[0] == M_READS
                for tt in range(NT):
                    dve.wait_ge(m_tp, n * M_BANKS + (tt + 1))
                    hh = h[:, tt, CB:D]
                    ins = nc.vector.tensor_tensor(hh, tp[tt][:, :], hh, ALU.add)
                    if tt:
                        tell(ins, moe_done)
                    else:
                        own(ins)

            def second_block():
                state["limit"] = len(stream)
                normed(mem_in)
                norm_turn("mm", "mem2")

                def headed(name):
                    dst, size, gain = HEADED[name]
                    if size:
                        q = NORMED.index(name)
                        n = NT * CB // size
                        dve.wait_ge(h_square, 2 * (q + 1))
                        own(nc.vector.tensor_reduce(hs[:, 0, 0:n], head_sq[:, :, :].rearrange(
                            "p t (a b) -> p (t a) b", b=size), AX, ALU.add))
                        tell(nc.vector.tensor_scalar(hs[:, 0, 0:n], hs[:, 0, 0:n], 1.0 / size, EPS, ALU.mult, ALU.add),
                             h_sq_v)
                        dve.wait_ge(h_rs, q + 1)
                        newton(hs[:, 1, 0:n], hs[:, 0, 0:n], hs[:, 2, 0:n])
                        if name in ("fxq", "mq"):
                            own(nc.vector.tensor_scalar(hs[:, 1, 0:n], hs[:, 1, 0:n], float(size) ** -0.5, None, ALU.mult))
                        x = xn[:, STAGE[name], :].rearrange("p (a b) -> p a b", b=size)
                        tell(nc.vector.tensor_tensor(x, x, hs[:, 1, 0:n].unsqueeze(2).broadcast_to((P, n, size)),
                                                     ALU.mult), h_scaled)

                def turned(name):
                    dst, size, gain = HEADED[name]
                    for j in range(2):
                        b = batch(("heads", name, j))[:, :].rearrange("p (a b) -> p a b", a=2)
                        o = dst[:, 2 * j:2 * j + 2, :]
                        tell(nc.vector.tensor_scalar(o, b, G(gain), None, ALU.mult) if size
                             else nc.vector.tensor_copy(o, b), tp_free["D"])

                split_to(group_of["b_in", "mk"][1] + SPL - 1)
                headed("mk")
                split_to(group_of["b_in", "mv"][1] + SPL - 1)
                turned("mk")
                y = rstd(0, 1.0 / D)
                for tt in range(NT):
                    tell(nc.vector.scalar_tensor_tensor(out=h[:, tt, :], in0=h[:, tt, :], scalar=y[:, tt:tt + 1],
                                                        in1=R("final"), op0=ALU.mult, op1=ALU.mult), h_done)
                normed(h)
                norm_turn("m2", "mix2")
                wide = lambda v: fx[:, v, :].rearrange("p (t h) -> p t h", t=NT)
                b = batch("forget")
                tell(nc.vector.tensor_tensor(wide(F_NLF), b[:, 0:16].rearrange("p (t h) -> p t h", t=NT),
                                             R("forget").unsqueeze(1).broadcast_to((P, NT, 8)), ALU.add), tp_free["D"])
                own(nc.vector.tensor_scalar(fx[:, F_M, :], fx[:, F_NLF, :], -1.0, 0.0, ALU.mult, ALU.max))
                own(nc.vector.tensor_scalar(fx[:, F_NLF, :], fx[:, F_NLF, :], -1.0, None, ALU.mult))
                tell(nc.vector.scalar_tensor_tensor(out=fx[:, F_E, :], in0=fx[:, F_M, :], scalar=-2.0,
                                                    in1=fx[:, F_NLF, :], op0=ALU.mult, op1=ALU.add), fox_dve)
                dve.wait_ge(fox_act, 1)
                tell(nc.vector.tensor_tensor(fx[:, F_NLF, :], fx[:, F_M, :], fx[:, F_E, :], ALU.add), fox_dve)
                for c, (name, _) in enumerate(B_IN):
                    split_to(group_of["b_in", name][1] + SPL - 1)
                    if c == 1:
                        b = batch("cumf")
                        tell(nc.vector.tensor_copy(fx[:, F_CUM, :], b[:, 0:16]), tp_free["D"])
                    if c and B_IN[c - 1][0] in HEADED:
                        turned(B_IN[c - 1][0])
                    if name in HEADED:
                        headed(name)
                turned("mq")
                mask = C("before")
                for pair in range(4):
                    hd = (2 * pair, 2 * pair + 1)
                    for hh in hd:
                        dve.wait_ge(sb_l, hh + 1)
                        z, sp_, l = xn[:, hh % 2, 0:3 * P], xn[:, hh % 2, 3 * P:6 * P], third[:, hh % 2, :]
                        own(nc.vector.scalar_tensor_tensor(out=sp_, in0=z, scalar=0.0, in1=l, op0=ALU.max, op1=ALU.add))
                        own(nc.vector.tensor_tensor(sp_[:, 0:P], sp_[:, 0:P], mask, ALU.mult))
                        tell(nc.vector.tensor_tensor(sp_[:, 2 * P:3 * P], sp_[:, 2 * P:3 * P], mask, ALU.mult), sb_sp)
                    for hh in hd:
                        z = xn[:, hh % 2, 0:3 * P]
                        tell(nc.vector.tensor_tensor(z, z, batch(("sb_cum", hh))[:, 0:3 * P], ALU.subtract), tp_free["D"])
                        tell(nc.vector.tensor_scalar(z, z, 0.0, None, ALU.min), sb_a)
                    for hh in hd:
                        dve.wait_ge(sb_wx, hh + 1)
                        w = xn[:, hh % 2, 0:3 * P]
                        own(nc.vector.tensor_tensor(w[:, 0:P], w[:, 0:P], mask, ALU.mult))
                        tell(nc.vector.tensor_tensor(w[:, 2 * P:3 * P], w[:, 2 * P:3 * P], mask, ALU.mult), sb_w)
                    tell(nc.vector.tensor_copy(o_sb[:, :, pair * P:pair * P + P],
                                               batch(("sb_o", pair))[:, 0:S].rearrange("p (t c) -> p t c", t=NT)),
                         tp_free["D"])

                def maxima(hh, parts):
                    for tt, cols in enumerate(parts):
                        mx = st[:, hh % 2 * 2 + tt, 0:1]
                        own(nc.vector.tensor_reduce(mx, xn[:, hh % 2, cols], AX, ALU.max))
                        tell(nc.vector.tensor_scalar(mx, mx, -1.0, None, ALU.mult), sm_z if tt else d_own)

                def divide(name, n, hd, o, width):
                    b = batch(name)
                    for k, hh in enumerate(hd):
                        for tt in range(NT):
                            q = st[:, hh % 2 * 2 + tt, 1:2]
                            own(nc.vector.reciprocal(q, q))
                            c0 = tt * 2 * width + k * width
                            tell(nc.vector.tensor_scalar(o[:, tt, hh * width:hh * width + width], b[:, c0:c0 + width],
                                                         q, None, ALU.mult),
                                 tp_free["D"] if k and tt else d_own)

                for pair in range(4):
                    hd = (2 * pair, 2 * pair + 1)
                    for hh in hd:
                        b = batch(("fx_z", hh))
                        x = xn[:, hh % 2, :]
                        c0, c1 = fx[:, F_CUM, hh:hh + 1], fx[:, F_CUM, 8 + hh:9 + hh]
                        own(nc.vector.scalar_tensor_tensor(out=x[:, 0:P], in0=b[:, 0:P], scalar=c0, in1=C("future"),
                                                           op0=ALU.subtract, op1=ALU.add))
                        own(nc.vector.tensor_scalar(x[:, P:S], b[:, P:S], c1, None, ALU.subtract))
                        tell(nc.vector.scalar_tensor_tensor(out=x[:, S:3 * P], in0=b[:, S:3 * P], scalar=c1,
                                                            in1=C("future"), op0=ALU.subtract, op1=ALU.add), tp_free["D"])
                        maxima(hh, (slice(0, P), slice(P, 3 * P)))
                    divide(("fx_o", pair), hh, hd, o_fox, 64)
                for pair in range(2):
                    hd = (2 * pair, 2 * pair + 1)
                    for hh in hd:
                        b = batch(("mm_z", hh))
                        tell(nc.vector.tensor_copy(xn[:, hh % 2, 0:2 * S], b[:, :]), tp_free["D"])
                        maxima(hh, (slice(0, S), slice(S, 2 * S)))
                    divide(("mm_o", pair), 8 + hh, hd, o_mem, P)
                for br in range(3):
                    for j in range(2):
                        b = batch(("oT", br, j))
                        high()
                        tell(nc.vector.tensor_tensor(oT2[br][:, 2 * j:2 * j + 2, :],
                                                     b[:, :].rearrange("p (a b) -> p a b", a=2),
                                                     oT1[br][:, 2 * j:2 * j + 2, :].bitcast(F32), ALU.subtract),
                             tp_free["D"])
                for c in range(2):
                    for br in range(3):
                        banks = after(("branch", br, c))
                        dve.wait_ge(acc_free["A"], group_of["b_gate", br, c][3])
                        m = [xn[:, tt, c * CB:c * CB + CB] for tt in range(NT)]
                        for tt in range(NT):
                            o = gate2[:, tt, :] if br else m[tt]
                            tell(nc.vector.tensor_tensor(o, banks[tt][:, :], gate2[:, tt, :], ALU.mult),
                                 acc_free["D"] if tt else d_own)
                        if br:
                            for tt in range(NT):
                                tell(nc.vector.tensor_tensor(m[tt], m[tt], gate2[:, tt, :], ALU.add),
                                     d_own if tt == 0 else xn_done if br == 2 else d_own)
                        tell(nc.vector.memset(small[:, 250:251], 0.0), merged)
                norm_turn("mg", None)
                for c in range(2):
                    add_to_h(("b_out", c), c)
                normed(h)
                norm_turn("m3", "mlp2")
                for hf in range(2):
                    def hidden(b):
                        for tt in range(NT):
                            bk = batch((("fhid", hf, b), tt))
                            high()
                            tell(nc.vector.tensor_tensor(hid2[:, 4 * b:4 * b + 4, tt * P:tt * P + P],
                                                         bk[:, :].rearrange("p (k c) -> p k c", k=4),
                                                         hid1[:, 4 * b:4 * b + 4, tt * P:tt * P + P].bitcast(F32),
                                                         ALU.subtract), tp_free["D"])

                    for b in range(4):
                        split_to(group_of["f_up", hf, b][1] + SPL - 1)
                        dve.wait_ge(acc_free["A"], group_of["f_up", hf, b][3])
                        if b:
                            hidden(b - 1)
                        for tt in range(NT):
                            tell(nc.vector.tensor_tensor(hnat[:, tt, :], gate_s[:, tt, :], gate_s[:, tt, :], ALU.mult),
                                 relu_sq)
                    split_to(cbs["f_down", hf, 0][0] + 1 + SPL)
                    hidden(3)
                    for c in range(2):
                        add_to_h(("f_down", hf, c), c)

            def add_to_h(name, c):
                banks = after(name)
                for tt in range(NT):
                    hh = h[:, tt, c * CB:c * CB + CB]
                    tell(nc.vector.tensor_tensor(hh, banks[tt][:, :], hh, ALU.add), acc_free["D"] if tt else d_own)

            normed(h)
            split_to(SPL)
            norm_turn("n0", "mix0")
            split_to(cbs["pool_in", 1][1] + SPL - 1)
            for g in range(4):
                b = batch_of["pool", g][0]
                high()
                tell(nc.vector.tensor_tensor(xT2[:, 2 * g:2 * g + 2, :], b[:, :].rearrange("p (a b) -> p a b", a=2),
                                             xT1[:, 2 * g:2 * g + 2, :].bitcast(F32), ALU.subtract), tp_free["D"])
            for c in range(2):
                banks = after(("pool_out", c))
                for tt in range(NT):
                    tell(nc.vector.tensor_tensor(pool_t[:, tt, :], banks[tt][:, :], R("scale")[:, c * CB:c * CB + CB],
                                                 ALU.mult), acc_free["D"] if tt else d_own)
                for tt in range(NT):
                    hh = h[:, tt, c * CB:c * CB + CB]
                    tell(nc.vector.tensor_tensor(hh, hh, pool_t[:, tt, :], ALU.add), h_done)
            split_to(cbs["pool_out", 1][1] + SPL)
            normed(h)
            norm_turn("n1", "ffn0")
            for hf, (f0, blocks) in enumerate(FF_HALVES):
                nb = len(blocks)

                def hidden(b):
                    for tt in range(NT):
                        bk = batch_of[("hid", hf, b), tt][0]
                        n = cbs["up", hf, b][2] // P
                        high()
                        tell(nc.vector.tensor_tensor(hid2[:, 4 * b:4 * b + n, tt * P:tt * P + P],
                                                     bk[:, 0:n * P].rearrange("p (k c) -> p k c", k=n),
                                                     hid1[:, 4 * b:4 * b + n, tt * P:tt * P + P].bitcast(F32),
                                                     ALU.subtract), tp_free["D"])

                for b in range(nb):
                    if b:
                        split_to(group_of["gate", hf, b][1] + SPL - 1)
                        hidden(b - 1)
                    banks = after(("up", hf, b))
                    n = cbs["up", hf, b][2]
                    dve.wait_ge(acc_free["A"], group_of["gate", hf, b][3])
                    for tt in range(NT if b or hf else 0):
                        dve.wait_ge(tp_done, batch_of[("hid",) + before(hf, b), tt][1])
                    for tt in range(NT):
                        tell(nc.vector.tensor_tensor(hnat[:, tt, 0:n], banks[tt][:, 0:n], gate_s[:, tt, 0:n], ALU.mult),
                             acc_free["D"] if tt else d_own)
                split_to(cbs["down", hf, 0][0] + 1 + SPL)
                hidden(nb - 1)
                for c in range(2):
                    banks = after(("down", hf, c))
                    for tt in range(NT):
                        hh = h[:, tt, c * CB:c * CB + CB]
                        tell(nc.vector.tensor_tensor(hh, banks[tt][:, :], hh, ALU.add), acc_free["D"] if tt else d_own)
            normed(h)
            norm_turn("n2", "mix1")
            deltanet()
            experts()
            second_block()
            nc.vector.memset(small[:, 250:251], 0.0).then_inc(out_done, 1)


def layout(**x):
    a = {k: np.asarray(v) for k, v in x.items()}

    def columns(v):
        return np.asarray(v, np.float32).reshape(-1, P).T

    cols = [columns(a["norm_mix_g"][0]), columns(a["norm_ffn_g"][0]), columns(a["norm_mix_g"][1]),
            columns(a["norm_ffn_g"][1]), columns(a["g_mix_norm_2"][0]), columns(a["g_mem_norm_2"][0]),
            columns(a["g_mlp_norm_2"][0]),
            a["dn_conv_w"][0].reshape(CONV, 24, P).transpose(2, 1, 0).reshape(P, 96),
            columns(a["dn_norm_g"][0]), columns(a["g_mem_q_2"][0]), columns(a["g_mem_k_2"][0]),
            columns(np.concatenate([a["g_fox_q_2"][0]] * 2)), columns(np.concatenate([a["g_fox_k_2"][0]] * 2))]
    rows = [a["pool_scale"][0], a["final_norm_g"], a["dn_dt_bias"][0], a["dn_a_log"][0], a["moe_router_b"][0],
            a["b_forget_2"][0]]
    consts, pool = shape_constants()
    given = {"rows2": a["norm_ffn_g"][1][None, :], "consts": consts, "pool_mix": pool, "cols": np.concatenate(cols, axis=1),
             "rows": np.concatenate(rows)[None, :]}
    for k in STREAMED:
        given[k] = a[k]
    return given


STREAMED = ("x", "mem_2", "pool_w_in", "pool_w_group", "ffn_w_gate", "ffn_w_up", "ffn_w_down", "dn_w_in", "dn_w_out",
            "moe_router_w", "moe_w_gate", "moe_w_up", "moe_w_down", "w_in_2", "w_mem_kv_2", "w_branch_sb_2",
            "w_branch_fox_2", "w_branch_mem_2", "w_out_2", "w_ff_up_2", "w_ff_down_2")


def kernel(**inputs):
    import numpy as _np
    import concourse.bacc as _bacc
    from concourse import mybir as _mybir
    from concourse.bass_utils import run_bass_kernel_spmd as _run

    nc = _bacc.Bacc("TRN2", target_bir_lowering=False, num_devices=1)
    arrays = {f"in_{k}_dram": _np.ascontiguousarray(v) for k, v in layout(**inputs).items()}
    given = {k[3:-5]: nc.dram_tensor(k, v.shape, _mybir.dt.from_np(v.dtype), kind="ExternalInput").ap()
             for k, v in arrays.items()}
    out = nc.dram_tensor("out_0_dram", (1, S, D), _mybir.dt.float32, kind="ExternalOutput").ap()
    build(nc, given, out)
    r = _run(nc, [arrays], core_ids=[0])
    return r.results[0]["out_0_dram"]
```

```python
from contextlib import ExitStack

import numpy as np

import concourse.bass as bass
from concourse import mybir

F32 = mybir.dt.float32
FR = mybir.dt.float32r
I32 = mybir.dt.int32
ALU = mybir.AluOpType
ACT = mybir.ActivationFunctionType
AX = mybir.AxisListType.X

P = 128
D = 1024
S = 256
NT = S // P
KD = D // P
CB = 512
KC = 4
EPS = 1e-6
RAW = 7
SPL = 3
TOP_K = 2
NEG = -1e30

POOL_WINDOWS = (2, 4, 8, 16)
DENSE_FF = 2816
NE = 8
EXPERT_FF = 3584
HEADS = 8
CONV = 4
SB_HD = 64
MEM_HD = 128
MEM_HEADS = 4
FF2 = 4096
MAX_ITEMS = NE + 3

LEVELS = (1, 2, 4, 8, 16, 32, 64)
CONST_AT = {}
_at = 0
for _name, _n in (("ident", P), ("ones", P), ("upto", P), ("before", P), ("from_", P), ("future", P),
                  ("iota", P), ("levels", P * len(LEVELS)), ("jlt", NE * NE), ("one_at", 4 * HEADS - 1)):
    CONST_AT[_name] = (_at, _at + _n)
    _at += _n
N_CONST = _at
COL_AT = {}
_at = 0
for _name, _n in (("mix0", 8), ("ffn0", 8), ("mix1", 8), ("ffn1", 8), ("mix2", 8), ("mem2", 8), ("mlp2", 8),
                  ("conv", 96), ("dn_norm", 1), ("mem_q", 1), ("mem_k", 1), ("fox_q", 1), ("fox_k", 1)):
    COL_AT[_name] = (_at, _at + _n)
    _at += _n
N_COL = _at
ROW_AT = {}
_at = 0
for _name, _n in (("scale", D), ("final", D), ("dt", 8), ("alog", 8), ("router_b", 8), ("forget", 8)):
    ROW_AT[_name] = (_at, _at + _n)
    _at += _n
N_ROW = _at


def shape_constants():
    c = np.zeros((P, N_CONST), np.float32)
    i, j = np.arange(P)[:, None], np.arange(P)[None, :]

    def put(name, a):
        c[:, CONST_AT[name][0]:CONST_AT[name][1]] = a

    put("ident", i == j)
    put("ones", np.ones((P, P)))
    put("upto", i <= j)
    put("before", i < j)
    put("from_", i >= j)
    put("future", np.where(j > i, NEG, 0.0))
    put("iota", np.broadcast_to(j, (P, P)))
    put("levels", np.concatenate([(i // (2 * s) == j // (2 * s)) & (i // s % 2 == 0) & (j // s % 2 == 1)
                                  for s in LEVELS], axis=1))
    put("one_at", np.broadcast_to(np.arange(4 * HEADS - 1)[None, :] == 2 * HEADS - 1, (P, 4 * HEADS - 1)))
    put("jlt", np.broadcast_to((np.arange(NE)[None, :] < np.arange(NE)[:, None]).reshape(1, -1), (P, NE * NE)))
    pool = np.zeros((P, 2, len(POOL_WINDOWS), S), np.float32)
    t, s = np.arange(S)[None, :], np.arange(S)[:, None]
    for g, w in enumerate(POOL_WINDOWS):
        a = ((s <= t) & (s > t - w)) / np.minimum(t + 1, w) - (s == t)
        pool[:, :, g, :] = a.reshape(2, P, S).transpose(1, 0, 2)
    return c, pool.reshape(P, -1)


def build(nc, t, out):
    with ExitStack() as ctx:
        def sb(name, shape, dt=F32):
            return ctx.enter_context(nc.sbuf_tensor(name, shape, dt))

        def sem(name):
            return ctx.enter_context(nc.semaphore(name))

        raw = sb("raw", [P, RAW, KC * CB])
        w_hi = sb("w_hi", [P, SPL, KC * CB], FR)
        low_parts = nc.sbuf_base
        w_lo = sb("w_lo", [P, SPL, KC * CB], FR)
        heads_in = nc.alloc_sbuf_tensor_at("heads_in", [P, 8, 6 * P], F32, offset=low_parts)
        cst = sb("cst", [P, N_CONST])
        col = sb("col", [P, N_COL])
        row = sb("row", [P, N_ROW])
        narrow_hi = sb("narrow_hi", [P, KD, 32], FR)
        narrow_lo = sb("narrow_lo", [P, KD, 32], FR)
        BA, ROUTER, FORGET = slice(0, 16), slice(16, 24), slice(24, 32)
        h = sb("h", [P, NT, D])
        xn = sb("xn", [P, NT, D])
        small = sb("small", [P, 336])
        xT1 = sb("xT1", [P, KD, S], FR)
        xT2 = sb("xT2", [P, KD, S], FR)
        area = nc.sbuf_base
        sb("room", [P, 13312])

        def at(name, shape, off, dt=F32):
            return nc.alloc_sbuf_tensor_at(name, shape, dt, offset=area + int(off * 1024))

        hid1 = at("hid1", [P, 16, S], 0, FR)
        hid2 = at("hid2", [P, 16, S], 16, FR)
        gate_s = at("gate_s", [P, NT, CB], 32)
        hnat = at("hnat", [P, NT, CB], 36)
        narrow = at("narrow", [P, KD, 32], 44)
        narrow_T = at("narrow_T", [32, S], 51)
        pool_m = at("pool_m", [P, 2, 4, S], 0)
        pool_u = at("pool_u", [P, NT, D], 8)
        pool_t = at("pool_t", [P, NT, CB], 16)

        qkvT = [at(n, [P, HEADS, S], o) for n, o in (("qT", 0), ("kT", 8), ("vT", 16))]
        qT, kT, vT = qkvT
        z_s = at("z_s", [P, NT, D], 24)
        kn = at("kn", [P, NT, HEADS, P], 32)
        vn = at("vn", [P, NT, HEADS, P], 40)
        memory_s = at("memory_s", [P, HEADS, P], 48)
        squares = at("squares", [P, 16, S], 32)
        o_sq = [at("o_sq0", [P, D], 32), at("o_sq1", [P, D], 0)]
        buf = {}
        for _h, offs in enumerate(((-16, -14, -12, -10, -8, -6), (-4, -2, 16, 18, 20, 22))):
            for _i, (_n, _o) in enumerate(zip(("dec", "A", "T", "TT", "X", "qk"), offs)):
                buf[_n, 0, _h] = at(f"{_n}0{_h}", [P, 4, P], _o)
                buf[_n, 1, _h] = nc.alloc_sbuf_tensor_at(f"{_n}1{_h}", [P, 4, P], F32,
                                                         offset=low_parts + 2048 * (6 * _h + _i))
        hidden1 = hid1[:, :, :].rearrange("p a b -> p (a b)")
        hidden2 = hid2[:, :, :].rearrange("p a b -> p (a b)")
        y_s = at("y_s", [P, 2, CB], 40)
        pick = at("pick", [P, NT, P], 44)
        pick_gate = at("pick_gate", [P, NT, P], 45)
        spread = at("spread", [P, NT, P], 46)
        rt = at("rt", [P, 64, 8], 48)
        item_pos = at("item_pos", [P, NT, 12], 50)
        item_gate = at("item_gate", [P, NT, 12], 50.25)
        item_f = at("item_f", [P, 16], 50.5)
        item_i = at("item_i", [P, 16], 50.75, I32)
        mem_in = [at(f"mem_in{tt}", [P, KD, S], 8 * tt - 16)[:, :, P:S] for tt in range(NT)]
        mem_sq = at("mem_sq", [P, D], 0)
        h_sq = at("h_sq", [P, D], 16)
        o_sb = at("o_sb", [P, NT, CB], 0)
        o_fox = at("o_fox", [P, NT, CB], 4)
        o_mem = at("o_mem", [P, NT, CB], 44)
        v_mem = at("v_mem", [P, NT, CB], 8)
        k_memT = at("k_memT", [P, 4, S], 12)
        q_sbT = at("q_sbT", [P, 4, S], 16)
        k_sbT = at("k_sbT", [P, 4, S], 20)
        v_sb = at("v_sb", [P, NT, CB], 24)
        q_foxT = at("q_foxT", [P, 4, S], 28)
        k_foxT = at("k_foxT", [P, 4, S], 32)
        v_fox = at("v_fox", [P, NT, CB], 36)
        q_memT = at("q_memT", [P, 4, S], 40)
        head_sq = at("head_sq", [P, NT, CB], 44)
        oT1 = [at(f"oT1_{b}", [P, 4, S], 16 + 8 * b, FR) for b in range(3)]
        oT2 = [at(f"oT2_{b}", [P, 4, S], 20 + 8 * b, FR) for b in range(3)]
        gate2 = at("gate2", [P, NT, CB], 8)
        fx = small[:, 80:144].rearrange("p (a b) -> p a b", a=4)
        (F_NLF, F_M, F_E, F_CUM) = range(4)
        hs = small[:, 144:208].rearrange("p (a b) -> p a b", a=4)
        st = small[:, 208:272].rearrange("p (a b) -> p a b", a=16)
        dnv = small[:, 80:336].rearrange("p (a b) -> p a b", a=16)
        (V_BETA, V_X, V_M, V_E, V_G, V_GC, V_GL, V_EGC, V_EKD, V_SS, _, V_R, _, V_TMP, _, V_EA) = range(16)

        bank = [ctx.enter_context(nc.psum_tensor(f"bank{i}", [P, CB], F32)) for i in range(8)]
        acc, tp = bank[:4], bank[4:]

        def C(name):
            return cst[:, CONST_AT[name][0]:CONST_AT[name][1]]

        def G(name, k=0):
            a = COL_AT[name][0] + k
            return col[:, a:a + 1]

        def R(name):
            return row[:, ROW_AT[name][0]:ROW_AT[name][1]]

        NORMS = ("n0", "n1", "n2", "n3", "mm", "fin", "m2", "m3")

        def cells(tag, j):
            c = 8 * NORMS.index(tag) + 2 * j
            return small[:, c:c + 2]

        def root(tag, tt):
            return cells(tag, 2)[:, tt:tt + 1]

        ident = C("ident")

        stream = []
        cbs = {}

        def add_cb(name, w, c0, n, rows=None, k0=0):
            rows = w.shape[0] - k0 if rows is None else rows
            first = len(stream)
            for r in range(k0, k0 + rows, KC * P):
                kc = min(KC, (k0 + rows - r) // P)
                stream.append((w[r:r + kc * P, c0:c0 + n].rearrange("(k p) n -> p k n", p=P), kc, n))
            cbs[name] = (first, len(stream), n)

        for c in range(2):
            add_cb(("pool_in", c), t["pool_w_in"][0], c * CB, CB)
        for c in range(2):
            first = len(stream)
            stream.append((t["pool_w_group"][0, 2 * c:2 * c + 2].rearrange("g (k p) e -> p (g k) e", p=P), 4, 256))
            cbs["pool_out", c] = (first, first + 1, CB)
        FF_HALVES = ((0, (512, 512, 512)), (1536, (512, 512, 256)))
        for hf, (f0, blocks) in enumerate(FF_HALVES):
            f = f0
            for b, n in enumerate(blocks):
                if f + n > DENSE_FF:
                    n = DENSE_FF - f
                add_cb(("gate", hf, b), t["ffn_w_gate"][0], f, n)
                add_cb(("up", hf, b), t["ffn_w_up"][0], f, n)
                f += n
            for c in range(2):
                add_cb(("down", hf, c), t["ffn_w_down"][0], c * CB, CB, f - f0, f0)
        for c in range(8):
            add_cb(("dn_in", c), t["dn_w_in"][0], c * CB, CB)
        for c in range(2):
            add_cb(("dn_out", c), t["dn_w_out"][0], c * CB, CB)
        NA = len(stream)

        add_cb(("b_in", "mk"), t["w_mem_kv_2"][0], 0, CB)
        add_cb(("b_in", "mv"), t["w_mem_kv_2"][0], CB, CB)
        B_IN = (("fxq", 1536), ("fxk", 2048), ("mq", 3080), ("sbq", 0), ("sbk", 512), ("fxv", 2560), ("sbv", 1024))
        for name, c0 in B_IN:
            add_cb(("b_in", name), t["w_in_2"][0], c0, CB)
        for c in range(2):
            for b, w in enumerate(("sb", "fox", "mem")):
                add_cb(("b_gate", b, c), t["w_in_2"][0], 3592 + b * D + c * CB, CB)
                add_cb(("branch", b, c), t[f"w_branch_{w}_2"][0], c * CB, CB)
        for c in range(2):
            add_cb(("b_out", c), t["w_out_2"][0], c * CB, CB)
        for hf in range(2):
            for b in range(4):
                add_cb(("f_up", hf, b), t["w_ff_up_2"][0], (4 * hf + b) * CB, CB)
            for c in range(2):
                add_cb(("f_down", hf, c), t["w_ff_down_2"][0], c * CB, CB, 4 * CB, 4 * hf * CB)

        HEADED = {"mk": (k_memT, 128, "mem_k"), "sbq": (q_sbT, 0, None), "sbk": (k_sbT, 0, None),
                  "fxq": (q_foxT, 64, "fox_q"), "fxk": (k_foxT, 64, "fox_k"), "mq": (q_memT, 128, "mem_q")}
        KEPT = {"mv": v_mem, "sbv": v_sb, "fxv": v_fox}
        NORMED = [n for n in ("mk", "fxq", "fxk", "mq")]
        STAGE = {"mk": 1, **{n: c % 2 for c, (n, _) in enumerate(B_IN)}}

        HEADS2 = [x for hh in range(8) for x in ((("mm", hh),) if hh < MEM_HEADS else ()) + (("fx", hh), ("sb", hh))]

        def softmax_number(u):
            return sum(kind != "sb" for kind, _ in HEADS2[:u + 1])

        WIDTH = {"sb": SB_HD, "fx": SB_HD, "mm": MEM_HD}
        QUERY_TILES = {"fx": (slice(0, P), slice(P, 3 * P)), "mm": (slice(0, S), slice(S, 2 * S))}
        O_OF = {"sb": o_sb, "fx": o_fox, "mm": o_mem}

        FB = EXPERT_FF // CB
        MT = 4 * FB + 2 * FB
        m_tiles = []
        for f in range(FB):
            for w in ("moe_w_gate", "moe_w_up"):
                for k in range(2):
                    m_tiles.append((w, k * CB, f * CB))
        for c in range(2):
            for f in range(FB):
                m_tiles.append(("moe_w_down", f * CB, c * CB))
        assert len(m_tiles) == MT and MT % RAW == 0 and MT % SPL == 0

        first_in = sem("first_in")
        narrow_split = sem("narrow_split")
        setup = sem("setup")
        x_in = sem("x_in")
        landed = [sem(f"landed{i}") for i in range(RAW)]
        split_hi = sem("split_hi")
        split_lo = sem("split_lo")
        used = sem("used")
        tp_done = sem("tp_done")
        tp_free = {"A": sem("tp_free_act"), "D": sem("tp_free_dve")}
        acc_free = {"A": sem("acc_free_act"), "D": sem("acc_free_dve")}
        a_own = sem("a_own")
        d_own = sem("d_own")
        sq_done = sem("sq_done")
        rs_done = sem("rs_done")
        xn_done = sem("xn_done")
        norm_ready = sem("norm_ready")
        hi_out = sem("hi_out")
        out_done = sem("out_done")
        out_sent = sem("out_sent")
        v_done = sem("v_done")
        h_done = sem("h_done")
        silu_done = sem("silu_done")
        gain_in = sem("gain_in")
        route_act = sem("route_act")
        route_dve = sem("route_dve")
        items_ready = sem("items_ready")
        picked0 = sem("picked0")
        m_landed = [sem(f"m_landed{i}") for i in range(RAW)]
        m_hi = sem("m_hi")
        m_lo = sem("m_lo")
        m_used = sem("m_used")
        m_tp = sem("m_tp")
        m_read = sem("m_read")
        m_spread = sem("m_spread")
        m_turned = sem("m_turned")
        m_gate = sem("m_gate")
        m_up = sem("m_up")
        m_y = sem("m_y")
        m_pick = sem("m_pick")
        moe_done = sem("moe_done")
        mem_loaded = sem("mem_loaded")
        h_square = sem("h_square")
        h_sq_v = sem("h_sq_v")
        h_rs = sem("h_rs")
        h_scaled = sem("h_scaled")
        fox_dve = sem("fox_dve")
        fox_act = sem("fox_act")
        sb_l = sem("sb_l")
        sb_sp = sem("sb_sp")
        sb_a = sem("sb_a")
        sb_wx = sem("sb_wx")
        sb_w = sem("sb_w")
        sm_z = sem("sm_z")
        sm_p = sem("sm_p")
        relu_sq = sem("relu_sq")
        merged = sem("merged")
        small_act = sem("small_act")
        small_dve = sem("small_dve")
        dec_min = sem("dec_min")
        dec_exp = sem("dec_exp")
        inv_first = sem("inv_first")
        inv_level = sem("inv_level")
        rhs_done = sem("rhs_done")
        kdec_done = sem("kdec_done")
        o_done = sem("o_done")
        o_squared = sem("o_squared")
        rs_ready = sem("rs_ready")
        block = ctx.enter_context(nc.Block())

        def before(hf, b):
            return (hf, b - 1) if b else (hf - 1, len(FF_HALVES[hf - 1][1]) - 1)

        (R_LG, R_EXP, R_SEL, R_RANK, R_CNT, R_MAX, R_IND, R_TMP, R_BIG, R_TIE) = (0, 2, 4, 6, 8, 9, 10, 13, 16, 32)
        SC1, SPREAD, TURN, GATHER, TURN6, SC0, M_BANKS, M_READS = 0, 2, 3, 9, 11, 12, 14, 13

        def n_items(eng):
            return eng.value_load(item_i[0:1, 12:13], min_val=NE, max_val=MAX_ITEMS)

        batches, batch_of = [], {}
        groups, group_of = [], {}
        SETUP = 6 * 16

        @block.tensor
        def _(pe):
            def tp_bank(name, owner):
                b = len(batches)
                if b >= 4:
                    o = batches[b - 4]
                    pe.wait_ge(tp_free[o], batches[:b - 3].count(o))
                batches.append(owner)
                batch_of[name] = (tp[b % 4], b + 1, owner, batches.count(owner))
                return tp[b % 4]

            def result(name):
                _, _, owner, n = batch_of[name]
                pe.wait_ge(tp_free[owner], n)

            def gemm(name, owner, a1, a2, between=None, turned=None):
                first, end, n = cbs[name]
                g = len(groups)
                if g >= 2:
                    o = groups[g - 2]
                    pe.wait_ge(acc_free[o], groups[:g - 1].count(o))
                groups.append(owner)
                banks = acc[2 * (g % 2):2 * (g % 2) + 2]
                group_of[name] = (banks, end, owner, groups.count(owner))
                k0 = 0
                for i in range(first, end):
                    _, kc, _ = stream[i]
                    pe.wait_ge(split_lo, i + 1)
                    if turned:
                        result((turned, (k0 + kc - 1) // 2))
                    s = i % SPL
                    for tt in range(NT):
                        for k in range(kc):
                            ch = k0 + k
                            b1 = w_hi[:, s, k * n:k * n + n]
                            b2 = w_lo[:, s, k * n:k * n + n]
                            o = banks[tt][:, 0:n]
                            x1 = a1[:, ch, tt * P:tt * P + P]
                            x2 = a2[:, ch, tt * P:tt * P + P]
                            begin, end_ = i == first and k == 0, i == end - 1 and k == kc - 1
                            nc.tensor.matmul(o, x1, b2, start=begin, stop=False)
                            nc.tensor.matmul(o, x2, b1, start=False, stop=False)
                            last = nc.tensor.matmul(o, x1, b1, start=False, stop=end_)
                    last.then_inc(used, 1)
                    k0 += kc
                    if between and i == first:
                        between()

            def turn_norm(tag, src, halves=None):
                for p in range(KD // 2):
                    b = tp_bank((tag, p), "D")
                    if halves and p % 2 == 0:
                        pe.wait_ge(halves[0], halves[1 + p // 2])
                    for j in range(2):
                        for tt in range(NT):
                            ch = 2 * p + j
                            last = nc.tensor.transpose(b[:, (2 * j + tt) * P:(2 * j + tt + 1) * P],
                                                       src(tt, ch) if callable(src) else
                                                       src[:, tt, ch * P:ch * P + P], ident)
                    last.then_inc(tp_done, 1)

            def turn_hidden(tag, up):
                pe.wait_ge(acc_free["D"], group_of[up][3])
                n = cbs[up][2]
                for tt in range(NT):
                    b = tp_bank((tag, tt), "D")
                    for k in range(n // P):
                        last = nc.tensor.transpose(b[:, k * P:k * P + P], hnat[:, tt, k * P:k * P + P], ident)
                    last.then_inc(tp_done, 1)

            def small_products(name, owner, products):
                b = tp_bank(name, owner)
                for o, l, r in products(b):
                    last = nc.tensor.matmul(o, l, r, start=True, stop=True)
                last.then_inc(tp_done, 1)

            def narrow_products(name, cols):
                b = tp_bank((name, "T"), "D")
                n = cols.stop - cols.start
                for k in range(KD):
                    w1, w2 = narrow_hi[:, k, cols], narrow_lo[:, k, cols]
                    nc.tensor.matmul(b[0:n, 0:S], w2, xT1[:, k, :], start=k == 0, stop=False)
                    nc.tensor.matmul(b[0:n, 0:S], w1, xT2[:, k, :], start=False, stop=False)
                    last = nc.tensor.matmul(b[0:n, 0:S], w1, xT1[:, k, :], start=False, stop=k == KD - 1)
                last.then_inc(tp_done, 1)
                result((name, "T"))
                b = tp_bank(name, "D")
                for tt in range(NT):
                    last = nc.tensor.transpose(b[:, tt * n:tt * n + n], narrow_T[0:n, tt * P:tt * P + P],
                                               ident[0:n, 0:n])
                last.then_inc(tp_done, 1)

            def four(b):
                return [b[:, k * P:k * P + P] for k in range(4)]

            def across(v):
                return v.broadcast_to((P, P))

            def deltanet():

                def turn_conv(c):
                    pe.wait_ge(acc_free["A"], group_of["dn_in", c][3])
                    for j in range(2):
                        b = tp_bank(("conv", c, j), "D")
                        for k in range(2):
                            for tt in range(NT):
                                col0 = tt * CB + (2 * j + k) * P
                                last = nc.tensor.transpose(b[:, (2 * k + tt) * P:(2 * k + tt + 1) * P],
                                                           xn[:, c % 2, col0:col0 + P], ident)
                        last.then_inc(tp_done, 1)

                for c in range(8):
                    gemm(("dn_in", c), "A", xT1, xT2, turned=None if c else "n2")
                    if c == 0:
                        pe.wait_ge(narrow_split, 2)
                        narrow_products("ba", BA)
                    if c == 6:
                        result("ssqT")
                        b = tp_bank("ssq", "D")
                        for tt in range(NT):
                            last = nc.tensor.transpose(b[:, tt * 16:tt * 16 + 16], narrow_T[0:16, tt * P:tt * P + P],
                                                       ident[0:16, 0:16])
                        last.then_inc(tp_done, 1)
                    if 1 <= c <= 6:
                        turn_conv(c - 1)
                    if c == 2:
                        pe.wait_ge(small_dve, 2)
                        small_products("gc", "D", lambda b: [
                            (b[:, 0:16], C("upto"), dnv[:, V_G, :]), (b[:, 16:32], C("ones"), dnv[:, V_G, :])])
                    if c == 5:
                        pe.wait_ge(o_squared, 2)
                        b = tp_bank("ssqT", "D")
                        for m in range(2 * HEADS):
                            a = 2 * HEADS - 1 - m
                            last = nc.tensor.matmul(b[0:2 * HEADS, 0:S], C("one_at")[:, a:a + 2 * HEADS], squares[:, m, :],
                                                    start=m == 0, stop=m == 2 * HEADS - 1)
                        last.then_inc(tp_done, 1)
                    if c == 7:
                        pe.wait_ge(rs_ready, 1)
                        for m in range(2):
                            for p in range(4):
                                small_products(("unit", m, p), "D", lambda b: [
                                    (b[:, (2 * k + tt) * P:(2 * k + tt + 1) * P],
                                     across(dnv[:, V_R + m, tt * 8 + 2 * p + k:tt * 8 + 2 * p + k + 1]), ident)
                                    for k in range(2) for tt in range(NT)])
                pe.wait_ge(silu_done, 12)
                result(("unit", 1, 3))
                for n, src in (("vn", vT), ("kn", kT)):
                    for tt in range(NT):
                        for hg in range(2):
                            b = tp_bank((n, tt, hg), "A")
                            for k in range(4):
                                last = nc.tensor.transpose(b[:, k * P:k * P + P],
                                                           src[:, 4 * hg + k, tt * P:tt * P + P], ident)
                            last.then_inc(tp_done, 1)
                result(("kn", 1, 1))
                def heads(hg):
                    return [4 * hg + k for k in range(4)]

                GROUPS = [(tt, hg) for tt in range(NT) for hg in range(2)]
                for tt in range(NT):
                    now = slice(tt * P, tt * P + P)
                    for hg in range(2):
                        small_products(("decay", tt, hg), "D", lambda b: [
                            (o, across(dnv[:, V_G, tt * 8 + hh:tt * 8 + hh + 1]), C("upto"))
                            for o, hh in zip(four(b), heads(hg))])
                    for hg in range(2):
                        small_products(("kk", tt, hg), "D", lambda b: [
                            (o, kT[:, hh, now], kT[:, hh, now]) for o, hh in zip(four(b), heads(hg))])
                        small_products(("beta", tt, hg), "D", lambda b: [
                            (o, across(dnv[:, V_BETA, tt * 8 + hh:tt * 8 + hh + 1]), ident)
                            for o, hh in zip(four(b), heads(hg))])
                        small_products(("qk", tt, hg), "D", lambda b: [
                            (o, kT[:, hh, now], qT[:, hh, now]) for o, hh in zip(four(b), heads(hg))])
                    for hg in range(2):
                        pe.wait_ge(inv_first, 2 * tt + hg + 1)
                        b = tp_bank(("T", tt, hg), "A")
                        for k in range(4):
                            last = nc.tensor.transpose(b[:, k * P:k * P + P], buf["TT", tt, hg][:, k, :], ident)
                        last.then_inc(tp_done, 1)
                for l in range(1, len(LEVELS)):
                    for g, (tt, hg) in enumerate(GROUPS):
                        pe.wait_ge(inv_level, (l - 1) * len(GROUPS) + g + 1)
                        result(("T", tt, hg) if l == 1 else ("inv_T", tt, hg, l - 1))
                        small_products(("X", tt, hg, l), "A", lambda b: [
                            (o, buf["dec", tt, hg][:, k, :], buf["T", tt, hg][:, k, :]) for k, o in enumerate(four(b))])
                    for tt, hg in GROUPS:
                        result(("X", tt, hg, l))
                        if l > 1:
                            result(("inv_TT", tt, hg, l - 1))
                        if l < len(LEVELS) - 1:
                            small_products(("inv_T", tt, hg, l), "D", lambda b: [
                                (o, buf["TT", tt, hg][:, k, :], buf["X", tt, hg][:, k, :]) for k, o in enumerate(four(b))])
                        small_products(("inv_TT", tt, hg, l), "D", lambda b: [
                            (o, buf["X", tt, hg][:, k, :], buf["TT", tt, hg][:, k, :]) for k, o in enumerate(four(b))])
                for tt in range(NT):
                    now = slice(tt * P, tt * P + P)
                    for hg in range(2):
                        if tt:
                            result(("state", 0, hg))
                            small_products(("kS", tt, hg), "D", lambda b: [
                                (o, kT[:, hh, now], memory_s[:, hh, :]) for o, hh in zip(four(b), heads(hg))])
                            small_products(("qS", tt, hg), "D", lambda b: [
                                (o, qT[:, hh, now], memory_s[:, hh, :]) for o, hh in zip(four(b), heads(hg))])
                    for hg in range(2):
                        pe.wait_ge(rhs_done, 2 * tt + hg + 1)
                        result(("inv_TT", tt, hg, len(LEVELS) - 1))
                        small_products(("vnew", tt, hg), "A", lambda b: [
                            (o, buf["TT", tt, hg][:, k, :], buf["A", tt, hg][:, k, :]) for k, o in enumerate(four(b))])
                    for hg in range(2):
                        result(("vnew", tt, hg))
                        small_products(("o", tt, hg), "D", lambda b: [
                            (o, buf["qk", tt, hg][:, k, :], buf["X", tt, hg][:, k, :]) for k, o in enumerate(four(b))])
                        if tt == 0:
                            pe.wait_ge(kdec_done, hg + 1)
                            small_products(("state", 0, hg), "A", lambda b: [
                                (o, buf["T", tt, hg][:, k, :], buf["X", tt, hg][:, k, :]) for k, o in enumerate(four(b))])
                pe.wait_ge(xn_done, 2)
                turn_norm("o", xn)
                for c in range(2):
                    gemm(("dn_out", c), "D", xT1, xT2, turned=None if c else "o")

            def experts():
                turn_norm("n3", h, (acc_free["D"], group_of["dn_out", 0][3], group_of["dn_out", 1][3]))
                result(("n3", 3))
                narrow_products("router", ROUTER)
                pe.wait_ge(route_dve, 1)
                b = tp_bank("places", "D")
                sel = [rt[:, R_SEL + tt, :] for tt in range(NT)]
                nc.tensor.matmul(b[:, 0:8], C("before"), sel[0], start=True, stop=True)
                nc.tensor.matmul(b[:, 8:16], C("ones"), sel[0], start=True, stop=False)
                nc.tensor.matmul(b[:, 8:16], C("before"), sel[1], start=False, stop=True)
                nc.tensor.matmul(b[:, 16:24], C("ones"), sel[0], start=True, stop=False)
                nc.tensor.matmul(b[:, 16:24], C("ones"), sel[1], start=False, stop=True).then_inc(tp_done, 1)

                def gather(b, half):
                    for k in range(4):
                        ch = 4 * half + k
                        for tt in range(NT):
                            last = nc.tensor.matmul(b[:, k * P:k * P + P], xn[:, tt, ch * P:ch * P + P], pick[:, tt, :],
                                                    start=tt == 0, stop=tt == NT - 1)
                    return last

                pe.wait_ge(xn_done, 4)
                pe.wait_ge(picked0, 2)
                for half in range(2):
                    gather(tp_bank(("gather", half), "D"), half).then_inc(tp_done, 1)
                result(("gather", 1))
                pe.wait_ge(picked0, 4)
                for o in "AD":
                    pe.wait_ge(tp_free[o], batches.count(o))
                    pe.wait_ge(acc_free[o], groups.count(o))
                n = n_items(pe)
                with pe.Fori(0, n) as i:
                    def product(j, lhs, out, begin, end):
                        pe.wait_ge(m_lo, i * MT + (j + 2))
                        s = j % SPL
                        for k in range(KC):
                            a1, a2 = lhs(k)
                            b1, b2 = w_hi[:, s, k * CB:k * CB + CB], w_lo[:, s, k * CB:k * CB + CB]
                            nc.tensor.matmul(out, a1, b2, start=begin and k == 0, stop=False)
                            nc.tensor.matmul(out, a2, b1, start=False, stop=False)
                            last = nc.tensor.matmul(out, a1, b1, start=False, stop=end and k == KC - 1)
                        last.then_inc(m_used, 1)

                    def tokens(j):
                        return lambda k: (xT1[:, 4 * (j % 2) + k, 0:P], xT2[:, 4 * (j % 2) + k, 0:P])

                    def hidden(f):
                        return lambda k: (hidden1[:, (4 * f + k) * P:(4 * f + k + 1) * P],
                                          hidden2[:, (4 * f + k) * P:(4 * f + k + 1) * P])

                    def turn(f):
                        pe.wait_ge(m_up, i * FB + (f + 1))
                        bi = TURN + f if f < 6 else TURN6
                        if f < 6:
                            if f == 3:
                                pe.wait_ge(m_spread, i + 1)
                            pe.wait_ge(m_read, i * M_READS + (3 if f < 4 else f))
                        else:
                            pe.wait_ge(m_read, i * M_READS + 8)
                        b = tp[bi % 4]
                        for k in range(4):
                            last = nc.tensor.transpose(b[:, k * P:k * P + P], hnat[:, f % 2, k * P:k * P + P], ident)
                        last.then_inc(m_tp, 1)

                    def scatter(bi, c):
                        for tt in range(NT):
                            nc.tensor.matmul(tp[(bi + tt) % 4][:, :], spread[:, tt, :], y_s[:, c, :],
                                             start=True, stop=True).then_inc(m_tp, 1)

                    for f in range(FB):
                        g = acc[2 * (f % 2)][:, :]
                        u = acc[2 * (f % 2) + 1][:, :]
                        if f == 1:
                            pe.wait_ge(m_y, i * 2 + 1)
                        elif f > 1:
                            pe.wait_ge(m_gate, i * FB + (f - 1))
                        for j in (4 * f, 4 * f + 1):
                            product(j, tokens(j), g, j % 2 == 0, j % 2 == 1)
                        if f == 0:
                            pe.wait_ge(m_y, i * 2 + 1)
                            pe.wait_ge(m_read, i * M_READS + 1)
                            scatter(SC1, 1)
                        if f >= 1:
                            turn(f - 1)
                        if f >= 2:
                            pe.wait_ge(m_up, i * FB + (f - 1))
                        for j in (4 * f + 2, 4 * f + 3):
                            product(j, tokens(j), u, j % 2 == 0, j % 2 == 1)
                        if f == 0:
                            for tt in range(NT):
                                last = nc.tensor.transpose(tp[SPREAD % 4][:, tt * P:tt * P + P], pick_gate[:, tt, :], ident)
                            last.then_inc(m_tp, 1)
                    pe.wait_ge(m_pick, i * 4 + 4)
                    for half in range(2):
                        pe.wait_ge(m_read, i * M_READS + (6 + half))
                        gather(tp[(GATHER + half) % 4], half).then_inc(m_tp, 1)
                    pe.wait_ge(m_gate, i * FB + 6)
                    for j in range(4 * FB, 5 * FB):
                        if j == 4 * FB + 1:
                            turn(FB - 1)
                        f = j - 4 * FB
                        if f in (1, FB - 1):
                            pe.wait_ge(m_read, i * M_READS + (9 if f == 1 else 12))
                        product(j, hidden(f), acc[2][:, :], f == 0, f == FB - 1)
                    pe.wait_ge(m_up, i * FB + 6)
                    for j in range(5 * FB, 6 * FB):
                        f = j - 5 * FB
                        product(j, hidden(f), acc[3][:, :], f == 0, f == FB - 1)
                        if f == 1:
                            pe.wait_ge(m_y, i * 2 + 2)
                            pe.wait_ge(m_read, i * M_READS + 12)
                            scatter(SC0, 0)
                pe.wait_ge(m_y, n * 2 + 1)
                pe.wait_ge(m_read, n * M_READS + 1)
                for tt in range(NT):
                    nc.tensor.matmul(tp[tt][:, :], spread[:, tt, :], y_s[:, 1, :], start=True, stop=True)\
                        .then_inc(m_tp, 1)
                pe.wait_ge(moe_done, 1)

            def second_block():
                def turn_heads(name):
                    if HEADED[name][1]:
                        pe.wait_ge(h_scaled, NORMED.index(name) + 1)
                    else:
                        pe.wait_ge(acc_free["A"], group_of["b_in", name][3])
                    for j in range(2):
                        b = tp_bank(("heads", name, j), "D")
                        for k in range(2):
                            for tt in range(NT):
                                c0 = tt * CB + (2 * j + k) * P
                                last = nc.tensor.transpose(b[:, (2 * k + tt) * P:(2 * k + tt + 1) * P],
                                                           xn[:, STAGE[name], c0:c0 + P], ident)
                        last.then_inc(tp_done, 1)

                turn_norm("mm", lambda tt, ch: mem_in[tt][:, ch, :])
                gemm(("b_in", "mk"), "A", xT1, xT2, turned="mm")
                gemm(("b_in", "mv"), "A", xT1, xT2)
                pe.wait_ge(h_done, 6)
                turn_norm("m2", h)
                for c, (name, _) in enumerate(B_IN):
                    gemm(("b_in", name), "A", xT1, xT2, turned=None if c else "m2")
                    if c == 2:
                        pe.wait_ge(fox_dve, 2)
                        b = tp_bank("cumf", "D")
                        nc.tensor.matmul(b[:, 0:8], C("upto"), fx[:, F_NLF, 0:8], start=True, stop=True)
                        nc.tensor.matmul(b[:, 8:16], C("ones"), fx[:, F_NLF, 0:8], start=True, stop=False)
                        nc.tensor.matmul(b[:, 8:16], C("upto"), fx[:, F_NLF, 8:16], start=False, stop=True)\
                            .then_inc(tp_done, 1)
                    if c == 0:
                        turn_heads("mk")
                    elif B_IN[c - 1][0] in HEADED:
                        turn_heads(B_IN[c - 1][0])
                    if c == 1:
                        narrow_products("forget", FORGET)
                result(("heads", "sbk", 1))

                def half(x, hh, cols):
                    r = 64 * (hh % 2)
                    return x[r:r + 64, hh // 2, cols]

                t0, t1, both = slice(0, P), slice(P, S), slice(0, S)
                def scores(u):
                    kind, hh = HEADS2[u]
                    b = tp_bank(("z", u), "A" if kind == "sb" else "D")
                    if kind == "sb":
                        nc.tensor.matmul(b[:, 0:S], half(k_sbT, hh, t0), half(q_sbT, hh, both), start=True, stop=True)
                        last = nc.tensor.matmul(b[:, S:S + P], half(k_sbT, hh, t1), half(q_sbT, hh, t1),
                                                start=True, stop=True)
                    elif kind == "fx":
                        f0 = across(fx[:, F_NLF, hh:hh + 1])
                        f1 = across(fx[:, F_NLF, 8 + hh:9 + hh])
                        nc.tensor.matmul(b[:, 0:P], half(q_foxT, hh, t0), half(k_foxT, hh, t0), start=True, stop=False)
                        nc.tensor.matmul(b[:, 0:P], f0, C("upto"), start=False, stop=True)
                        nc.tensor.matmul(b[:, P:3 * P], half(q_foxT, hh, t1), half(k_foxT, hh, both), start=True, stop=False)
                        nc.tensor.matmul(b[:, P:S], f0, C("upto"), start=False, stop=False)
                        nc.tensor.matmul(b[:, S:3 * P], f0, C("ones"), start=False, stop=False)
                        last = nc.tensor.matmul(b[:, S:3 * P], f1, C("upto"), start=False, stop=True)
                    else:
                        for tt in range(NT):
                            last = nc.tensor.matmul(b[:, tt * S:tt * S + S], q_memT[:, hh, tt * P:tt * P + P],
                                                    k_memT[:, hh, :], start=True, stop=True)
                    last.then_inc(tp_done, 1)

                def second(u):
                    kind, hh = HEADS2[u]
                    x = heads_in[:, u % 8, :]
                    if kind == "sb":
                        pe.wait_ge(sb_sp, hh + 1)
                        b = tp_bank(("second", u), "D")
                        sp_ = x[:, 3 * P:6 * P]
                        nc.tensor.matmul(b[:, 0:S], C("from_"), sp_[:, 0:S], start=True, stop=False)
                        nc.tensor.matmul(b[:, P:S], C("ones"), sp_[:, S:S + P], start=False, stop=True)
                        last = nc.tensor.matmul(b[:, S:S + P], C("from_"), sp_[:, S:S + P], start=True, stop=True)
                    else:
                        pe.wait_ge(sm_p, softmax_number(u))
                        b = tp_bank(("second", u), "A")
                        for k in range(3 if kind == "fx" else 4):
                            last = nc.tensor.transpose(b[:, k * P:k * P + P], x[:, k * P:k * P + P], ident)
                    last.then_inc(tp_done, 1)

                def output(u):
                    kind, hh = HEADS2[u]
                    n = WIDTH[kind]
                    if kind == "sb":
                        pe.wait_ge(sb_w, hh + 1)
                    else:
                        result(("second", u))
                    w = heads_in[:, u % 8, 0:4 * P]
                    if u == 0:
                        pe.wait_ge(acc_free["A"], group_of["b_in", "sbv"][3])
                    b = tp_bank(("out", u), "D")
                    value = {"sb": v_sb, "fx": v_fox, "mm": v_mem}[kind]
                    v = [value[:, tt, hh * n:hh * n + n] for tt in range(NT)]
                    if kind == "mm":
                        for tt in range(NT):
                            for m in range(2):
                                last = nc.tensor.matmul(b[:, tt * n:tt * n + n], w[:, (2 * tt + m) * P:(2 * tt + m + 1) * P],
                                                        v[m], start=m == 0, stop=m == 1)
                    else:
                        nc.tensor.matmul(b[:, 0:n], w[:, 0:P], v[0], start=True, stop=True)
                        nc.tensor.matmul(b[:, n:2 * n], w[:, P:S], v[0], start=True, stop=False)
                        last = nc.tensor.matmul(b[:, n:2 * n], w[:, S:3 * P], v[1], start=False, stop=True)
                    last.then_inc(tp_done, 1)

                for u in range(len(HEADS2) + 4):
                    for do, v in ((scores, u), (second, u - 2), (output, u - 4)):
                        if 0 <= v < len(HEADS2):
                            do(v)
                gemm(("b_gate", 0, 0), "A", xT1, xT2)
                for br, (o, done) in enumerate(((o_sb, ("out", HEADS2.index(("sb", 7)))), (o_fox, ("out", HEADS2.index(("fx", 7)))),
                                                 (o_mem, ("out", HEADS2.index(("mm", 3)))))):
                    result(done)
                    for j in range(2):
                        b = tp_bank(("oT", br, j), "D")
                        for k in range(2):
                            for tt in range(NT):
                                ch = 2 * j + k
                                last = nc.tensor.transpose(b[:, (2 * k + tt) * P:(2 * k + tt + 1) * P],
                                                           o[:, tt, ch * P:ch * P + P], ident)
                        last.then_inc(tp_done, 1)
                for c in range(2):
                    for br in range(3):
                        if c or br:
                            gemm(("b_gate", br, c), "A", xT1, xT2)
                        result(("oT", br, 1))
                        gemm(("branch", br, c), "D", oT1[br], oT2[br])
                pe.wait_ge(xn_done, 6)
                turn_norm("mg", xn)
                for c in range(2):
                    gemm(("b_out", c), "D", xT1, xT2, turned=None if c else "mg")
                turn_norm("m3", h, (acc_free["D"], group_of["b_out", 0][3], group_of["b_out", 1][3]))
                for hf in range(2):
                    def turn(b):
                        pe.wait_ge(relu_sq, 2 * (4 * hf + b + 1))
                        for tt in range(NT):
                            bk = tp_bank((("fhid", hf, b), tt), "D")
                            for k in range(4):
                                last = nc.tensor.transpose(bk[:, k * P:k * P + P], hnat[:, tt, k * P:k * P + P], ident)
                            last.then_inc(tp_done, 1)

                    for b in range(4):
                        gemm(("f_up", hf, b), "A", xT1, xT2, turned=None if hf or b else "m3")
                        if b:
                            turn(b - 1)
                    result((("fhid", hf, 2), 1))
                    gemm(("f_down", hf, 0), "D", hid1, hid2,
                         between=lambda: (turn(3), result((("fhid", hf, 3), 1))))
                    gemm(("f_down", hf, 1), "D", hid1, hid2)

            pe.wait_ge(first_in, 32)
            pe.wait_ge(x_in, 16)
            turn_norm("n0", h)
            for c in range(2):
                gemm(("pool_in", c), "A", xT1, xT2, turned=None if c else "n0")
            pe.wait_ge(setup, SETUP)
            pe.wait_ge(acc_free["A"], 2)
            for g in range(4):
                b = tp_bank(("pool", g), "D")
                for j in range(2):
                    ch = 2 * g + j
                    nc.tensor.matmul(b[:, j * S:j * S + S], pool_u[:, 0, ch * P:ch * P + P], pool_m[:, 0, g, :],
                                     start=True, stop=False)
                    last = nc.tensor.matmul(b[:, j * S + P:j * S + S], pool_u[:, 1, ch * P:ch * P + P],
                                            pool_m[:, 1, g, P:S], start=False, stop=True)
                last.then_inc(tp_done, 1)
            result(("pool", 3))
            for c in range(2):
                first = cbs["pool_out", c][0]
                g = len(groups)
                o = groups[g - 2]
                pe.wait_ge(acc_free[o], groups[:g - 1].count(o))
                groups.append("D")
                banks = acc[2 * (g % 2):2 * (g % 2) + 2]
                group_of["pool_out", c] = (banks, first + 1, "D", groups.count("D"))
                pe.wait_ge(split_lo, first + 1)
                s = first % SPL
                for tt in range(NT):
                    for w in range(2):
                        for k in range(2):
                            ch = 4 * c + 2 * w + k
                            o = banks[tt][:, w * 256:w * 256 + 256]
                            b1 = w_hi[:, s, (2 * w + k) * 256:(2 * w + k + 1) * 256]
                            b2 = w_lo[:, s, (2 * w + k) * 256:(2 * w + k + 1) * 256]
                            x1, x2 = xT1[:, ch, tt * P:tt * P + P], xT2[:, ch, tt * P:tt * P + P]
                            nc.tensor.matmul(o, x1, b2, start=k == 0, stop=False)
                            nc.tensor.matmul(o, x2, b1, start=False, stop=False)
                            last = nc.tensor.matmul(o, x1, b1, start=False, stop=k == 1)
                last.then_inc(used, 1)
            turn_norm("n1", h, (h_done, 2, 4))
            for hf, (f0, blocks) in enumerate(FF_HALVES):
                nb = len(blocks)
                for b in range(nb):
                    gemm(("gate", hf, b), "A", xT1, xT2, turned=None if hf or b else "n1")
                    if b:
                        turn_hidden(("hid", hf, b - 1), ("up", hf, b - 1))
                    gemm(("up", hf, b), "D", xT1, xT2)
                result((("hid", hf, nb - 2), 1))
                gemm(("down", hf, 0), "D", hid1, hid2,
                     between=lambda: (turn_hidden(("hid", hf, nb - 1), ("up", hf, nb - 1)),
                                      result((("hid", hf, nb - 1), 1))))
                gemm(("down", hf, 1), "D", hid1, hid2)

            turn_norm("n2", h, (acc_free["D"], group_of["down", 1, 0][3], group_of["down", 1, 1][3]))
            deltanet()
            experts()
            second_block()

        @block.sync
        def _(sp):
            sp.dma_start(cst[:, 0:P], t["consts"][:, 0:P]).then_inc(first_in, 16)
            sp.dma_start(col[:], t["cols"]).then_inc(first_in, 16)
            sp.dma_start(h[:], t["x"][0].rearrange("(t p) d -> p t d", p=P)).then_inc(x_in, 16)

            def load(tiles):
                for i in tiles:
                    src, kc, n = stream[i]
                    if i >= RAW:
                        sp.wait_ge(split_lo, i - RAW + 1)
                    dst = raw[:, i % RAW, 0:kc * n].rearrange("p (k n) -> p k n", k=kc)
                    sp.dma_start(dst, src).then_inc(landed[i % RAW], 16)

            def load_expert(j, e):
                w, r, c = m_tiles[j % MT]
                sp.dma_start(raw[:, j % RAW, :].rearrange("p (k n) -> p k n", k=KC),
                             t[w][0, bass.ds(e, 1), r:r + KC * P, c:c + CB].rearrange("e (k p) n -> p (e k) n", p=P))\
                  .then_inc(m_landed[j % RAW], 16)

            load(range(NA))
            for j in range(RAW):
                sp.wait_ge(split_lo, max(i for i in range(NA) if i % RAW == j) + 1)
                load_expert(j, 0)
            sp.wait_ge(tp_free["D"], batch_of["router", "T"][3])
            for tt in range(NT):
                sp.dma_start(mem_in[tt], t["mem_2"][0, tt * P:tt * P + P].rearrange("p (k c) -> p k c", k=KD))\
                  .then_inc(mem_loaded, 16)
            sp.wait_ge(items_ready, 1)
            last = sp.value_load(item_i[0:1, 13:14], min_val=NE - 1, max_val=MAX_ITEMS - 1)

            def load_item(i, end):
                now = sp.value_load(item_i[0:1, bass.ds(i, 1)], min_val=0, max_val=NE - 1)
                after = sp.value_load(item_i[0:1, bass.ds(i + 1, 1)], min_val=0, max_val=NE - 1)
                for j in range(RAW, end):
                    if j == 4 * FB:
                        now = sp.value_load(item_i[0:1, bass.ds(i, 1)], min_val=0, max_val=NE - 1)
                    sp.wait_ge(m_lo, i * MT + (j - RAW + 2))
                    sp.wait_ge(items_ready, 1)
                    load_expert(j, now if j < MT else after)

            with sp.Fori(0, last) as i:
                load_item(i, MT + RAW)
            load_item(last, MT + SPL)
            sp.wait_ge(m_lo, last * MT + (MT + SPL + 1))
            load(range(NA, len(stream)))
            for c in range(2):
                cols = slice(c * CB, c * CB + CB)
                sp.wait_ge(out_done, c + 1)
                sp.dma_start(out[0, :, cols].rearrange("(t p) d -> p t d", p=P), h[:, :, cols]).then_inc(out_sent, 16)
            sp.wait_ge(out_sent, 32)

        @block.scalar
        def _(act):
            act.wait_ge(x_in, 16)
            act.dma_start(pool_m[:].rearrange("p a b c -> p (a b c)"), t["pool_mix"]).then_inc(setup, 16)
            act.dma_start(row[:], t["rows"].broadcast_to((P, N_ROW))).then_inc(setup, 16)
            act.dma_start(cst[:, P:N_CONST], t["consts"][:, P:N_CONST]).then_inc(setup, 16)
            act.dma_start(narrow[:, :, BA], t["dn_w_in"][0, :, 4 * D:4 * D + 16].rearrange("(k p) n -> p k n", p=P))\
               .then_inc(setup, 16)
            act.dma_start(narrow[:, :, ROUTER], t["moe_router_w"][0].rearrange("(k p) n -> p k n", p=P)).then_inc(setup, 16)
            act.dma_start(narrow[:, :, FORGET], t["w_in_2"][0, :, 3072:3080].rearrange("(k p) n -> p k n", p=P))\
               .then_inc(setup, 16)
            act.wait_ge(first_in, 32)
            told = {}
            state = {"split": 0, "limit": NA, "own": 0, "hi": 0}

            def tell(ins, signal):
                told[signal] = told.get(signal, 0) + 1
                ins.then_inc(signal, 1)
                act.wait_ge(signal, told[signal])

            def own(ins):
                tell(ins, a_own)

            def split_to(n):
                n = min(n, state["limit"])
                for i in range(state["split"], n):
                    _, kc, w = stream[i]
                    act.wait_ge(landed[i % RAW], 16 * (i // RAW + 1))
                    if i >= SPL:
                        act.wait_ge(used, i - SPL + 1)
                    nc.scalar.activation(w_hi[:, i % SPL, 0:kc * w], raw[:, i % RAW, 0:kc * w], ACT.Copy)\
                        .then_inc(split_hi, 1)
                state["split"] = max(n, state["split"])

            def after(name):
                banks, end = group_of[name][:2]
                split_to(end + SPL - 1)
                act.wait_ge(used, end)
                return banks

            def batch(name):
                b, n, _, _ = batch_of[name]
                act.wait_ge(tp_done, n)
                return b

            def whole(name):
                split_to(group_of[name][1] + SPL)
                act.wait_ge(acc_free["D"], group_of[name][3])

            def norm_root(tag, src, squares_to=None):
                for tt in range(NT):
                    tell(nc.scalar.activation(xn[:, tt, :] if squares_to is None else squares_to, src[:, tt, :], ACT.Square,
                                              accum_out=cells(tag, 0)[:, tt:tt + 1]), sq_done)
                act.wait_ge(v_done, NORMS.index(tag) + 1)
                own(nc.scalar.activation(cells(tag, 2), cells(tag, 1), ACT.Ln))
                tell(nc.scalar.activation(cells(tag, 2), cells(tag, 2), ACT.Exp, scale=-0.5), rs_done)

            def norm_used(tag):
                act.wait_ge(norm_ready, NORMS.index(tag) + 1)

            def norm_turn(tag, gain, step=1):
                for p in range(KD // 2):
                    b = batch((tag, p))
                    if gain is None:
                        tell(nc.scalar.activation(xT1[:, 2 * p:2 * p + 2, :],
                                                  b[:, :].rearrange("p (a b) -> p a b", a=2), ACT.Copy), hi_out)
                        continue
                    for j in range(2):
                        tell(nc.scalar.activation(xT1[:, 2 * p + j, :], b[:, j * S:j * S + S], ACT.Copy,
                                                  scale=G(gain, step * (2 * p + j))), hi_out)

            def result(name):
                _, _, owner, n = batch_of[name]
                act.wait_ge(tp_free[owner], n)

            def keep(name, dst):
                tell(nc.scalar.activation(dst, batch(name)[:, :].rearrange("p (a b) -> p a b", a=4), ACT.Copy),
                     tp_free["A"])

            def deltanet():
                def conv(c):
                    for j in range(2):
                        b = batch(("conv", c, j))
                        for k in range(2):
                            ch = 4 * c + 2 * j + k
                            tell(nc.scalar.activation(qkvT[ch // 8][:, ch % 8, :], b[:, k * S:k * S + S], ACT.Copy,
                                                      scale=G("conv", 4 * ch + 3)), hi_out)
                    for j in range(2):
                        result(("conv", c, j))
                        ch = 4 * c + 2 * j
                        x = qkvT[ch // 8][:, ch % 8:ch % 8 + 2, :]
                        tell(nc.scalar.activation(x, x, ACT.Silu), silu_done)

                for c in range(8):
                    if c == 0:
                        split_to(group_of["dn_in", 0][1] + SPL - 1)
                        result("ba")
                        own(nc.scalar.activation(dnv[:, V_BETA, :], dnv[:, V_BETA, :], ACT.Exp, scale=-1.0))
                        own(nc.scalar.activation(dnv[:, V_EA, 0:8], R("alog"), ACT.Exp))
                        act.wait_ge(small_dve, 1)
                        own(nc.scalar.activation(dnv[:, V_E, :], dnv[:, V_E, :], ACT.Exp))
                        tell(nc.scalar.activation(dnv[:, V_E, :], dnv[:, V_E, :], ACT.Ln, bias=1.0), small_act)
                    banks = after(("dn_in", c))
                    if c < 6:
                        if c >= 2:
                            result(("conv", c - 2, 1))
                        else:
                            result(("n2", KD // 2 - 1))
                        norm_used("n2")
                        for tt in range(NT):
                            tell(nc.scalar.activation(xn[:, c % 2, tt * CB:tt * CB + CB], banks[tt][:, :], ACT.Copy,
                                                      scale=root("n2", tt)), acc_free["A"] if tt else a_own)
                    else:
                        for tt in range(NT):
                            tell(nc.scalar.activation(z_s[:, tt, (c - 6) * CB:(c - 5) * CB], banks[tt][:, :], ACT.Silu,
                                                      scale=root("n2", tt)), acc_free["A"] if tt else a_own)
                    if 1 <= c <= 6:
                        conv(c - 1)
                    if c == 4:
                        for m in range(2):
                            tell(nc.scalar.activation(squares[:, 8 * m:8 * m + 8, :], qkvT[m][:, :, :], ACT.Square),
                                 o_squared)
                    if c == 6:
                        act.wait_ge(small_dve, 4)
                        own(nc.scalar.activation(dnv[:, V_R:V_R + 2, :], dnv[:, V_SS:V_SS + 2, :], ACT.Ln))
                        tell(nc.scalar.activation(dnv[:, V_R:V_R + 2, :], dnv[:, V_R:V_R + 2, :], ACT.Exp, scale=-0.5),
                             small_act)
                        own(nc.scalar.activation(dnv[:, V_EGC, :], dnv[:, V_GC, :], ACT.Exp))
                        tell(nc.scalar.activation(dnv[:, V_EKD, :], dnv[:, V_EKD, :], ACT.Exp), small_act)
                for n, dst in (("vn", vn), ("kn", kn)):
                    for tt in range(NT):
                        for hg in range(2):
                            keep((n, tt, hg), dst[:, tt, 4 * hg:4 * hg + 4, :])
                for tt in range(NT):
                    for hg in range(2):
                        act.wait_ge(dec_min, 2 * tt + hg + 1)
                        x = buf["dec", tt, hg][:, :, :]
                        tell(nc.scalar.activation(x, x, ACT.Exp), dec_exp)
                    for hg in range(2):
                        keep(("T", tt, hg), buf["T", tt, hg][:, :, :])
                for l in range(1, len(LEVELS)):
                    for tt in range(NT):
                        for hg in range(2):
                            keep(("X", tt, hg, l), buf["X", tt, hg][:, :, :])
                for tt in range(NT):
                    for hg in range(2):
                        keep(("vnew", tt, hg), buf["X", tt, hg][:, :, :])
                    if tt == 0:
                        for hg in range(2):
                            keep(("state", 0, hg), memory_s[:, 4 * hg:4 * hg + 4, :])
                    act.wait_ge(o_done, 2 * tt + 2)
                    tell(nc.scalar.activation(o_sq[tt][:, :], xn[:, tt, :], ACT.Square), o_squared)
                act.wait_ge(small_dve, 5)
                own(nc.scalar.activation(dnv[:, V_R, :], dnv[:, V_SS, :], ACT.Ln))
                tell(nc.scalar.activation(dnv[:, V_R, :], dnv[:, V_R, :], ACT.Exp, scale=-0.5), small_act)
                norm_turn("o", "dn_norm", 0)

            def experts():
                act.dma_start(R("scale"), t["rows2"].broadcast_to((P, D))).then_inc(gain_in, 16)
                split_to(group_of[("dn_out", 1)][1] + SPL)
                norm_turn("n3", "ffn1")
                whole(("dn_out", 1))
                norm_root("n3", h, mem_sq[:, :])
                act.wait_ge(route_dve, 2)
                tell(nc.scalar.activation(rt[:, R_EXP:R_EXP + 2, :], rt[:, R_EXP:R_EXP + 2, :], ACT.Exp), route_act)
                for half in range(2):
                    b = batch(("gather", half))
                    tell(nc.scalar.activation(xT1[:, 4 * half:4 * half + 4, 0:P],
                                              b[:, :].rearrange("p (a b) -> p a b", a=4), ACT.Copy), hi_out)
                act.wait_ge(used, NA)
                def split(j, i):
                    act.wait_ge(m_landed[j % RAW], i * (16 * MT // RAW) + 16 * (j // RAW + 1))
                    if j >= SPL:
                        act.wait_ge(m_used, i * MT + (j - SPL + 1))
                    nc.scalar.activation(w_hi[:, j % SPL, :], raw[:, j % RAW, :], ACT.Copy).then_inc(m_hi, 1)

                for j in range(SPL):
                    split(j, 0)
                act.wait_ge(mem_loaded, 32)
                for tt in range(NT):
                    tell(nc.scalar.activation(mem_sq[:, :].rearrange("p (k c) -> p k c", k=KD), mem_in[tt], ACT.Square,
                                              accum_out=cells("mm", 0)[:, tt:tt + 1]), sq_done)
                act.wait_ge(v_done, NORMS.index("mm") + 1)
                own(nc.scalar.activation(cells("mm", 2), cells("mm", 1), ACT.Ln))
                tell(nc.scalar.activation(cells("mm", 2), cells("mm", 2), ACT.Exp, scale=-0.5), rs_done)

                n = n_items(act)
                with act.Fori(0, n) as i:
                    at_ = [SPL]

                    def split_until(j):
                        for k in range(at_[0], j):
                            split(k, i)
                        at_[0] = max(at_[0], j)

                    def turned(f):
                        bi = TURN + f if f < 6 else TURN6
                        act.wait_ge(m_tp, i * M_BANKS + (bi + 1))
                        nc.scalar.activation(hidden1[:, 4 * f * P:4 * (f + 1) * P], tp[bi % 4][:, :], ACT.Copy)\
                            .then_inc(m_turned, 1)

                    for f in range(FB):
                        split_until(4 * f + 2 + SPL - 1)
                        act.wait_ge(m_used, i * MT + (4 * f + 2))
                        if f > 1:
                            act.wait_ge(m_up, i * FB + (f - 1))
                        nc.scalar.activation(gate_s[:, f % 2, :], acc[2 * (f % 2)][:, :], ACT.Silu).then_inc(m_gate, 1)
                        if f:
                            turned(f - 1)
                        else:
                            split_until(4 + SPL - 1)
                            act.wait_ge(m_tp, i * M_BANKS + (SPREAD + 1))
                            nc.scalar.activation(spread[:, :, :],
                                                 tp[SPREAD % 4][:, 0:NT * P].rearrange("p (a b) -> p a b", a=NT),
                                                 ACT.Copy).then_inc(m_spread, 1)
                    split_until(4 * FB + SPL - 1)
                    for half in range(2):
                        bi = GATHER + half
                        act.wait_ge(m_tp, i * M_BANKS + (bi + 1))
                        nc.scalar.activation(xT1[:, 4 * half:4 * half + 4, 0:P],
                                             tp[bi % 4][:, :].rearrange("p (a b) -> p a b", a=4), ACT.Copy)\
                            .then_inc(m_turned, 1)
                    split_until(4 * FB + 1 + SPL - 1)
                    turned(FB - 1)
                    for c in range(2):
                        split_until((5 + c) * FB + SPL - 1)
                        act.wait_ge(m_used, i * MT + (5 + c) * FB)
                        nc.scalar.activation(y_s[:, c, :], acc[2 + c][:, :], ACT.Copy).then_inc(m_y, 1)
                    split_until(MT + SPL)
                act.wait_ge(moe_done, 1)

            def second_block():
                state["limit"] = len(stream)
                norm_turn("mm", "mem2")
                split_to(NA + SPL)
                norm_root("fin", h)

                def headed(name):
                    banks = after(("b_in", name))
                    norm = "mm" if name in ("mk", "mv") else "m2"
                    norm_used(norm)
                    if name in KEPT:
                        for tt in range(NT):
                            tell(nc.scalar.activation(KEPT[name][:, tt, :], banks[tt][:, :], ACT.Copy,
                                                      scale=root(norm, tt)), acc_free["A"] if tt else a_own)
                        return
                    x = xn[:, STAGE[name], :]
                    for tt in range(NT):
                        tell(nc.scalar.activation(x[:, tt * CB:tt * CB + CB], banks[tt][:, :], ACT.Copy,
                                                  scale=root(norm, tt)), acc_free["A"] if tt else a_own)
                    if name != "mk":
                        head_roots(name)

                def head_roots(name):
                    x = xn[:, STAGE[name], :]
                    if name in NORMED:
                        q = NORMED.index(name)
                        if q:
                            act.wait_ge(h_sq_v, q)
                        for tt in range(NT):
                            tell(nc.scalar.activation(head_sq[:, tt, :], x[:, tt * CB:tt * CB + CB], ACT.Square), h_square)
                        act.wait_ge(h_sq_v, q + 1)
                        n = NT * CB // HEADED[name][1]
                        own(nc.scalar.activation(hs[:, 1, 0:n], hs[:, 0, 0:n], ACT.Ln))
                        tell(nc.scalar.activation(hs[:, 1, 0:n], hs[:, 1, 0:n], ACT.Exp, scale=-0.5), h_rs)

                headed("mk")
                headed("mv")
                norm_turn("m2", "mix2")
                norm_root("m2", h, h_sq[:, :])
                head_roots("mk")
                prev = {0: None, 1: "mk"}
                for c, (name, _) in enumerate(B_IN):
                    if name in HEADED and prev[c % 2]:
                        split_to(group_of["b_in", name][1] + SPL - 1)
                        result(("heads", prev[c % 2], 1))
                    if name in HEADED:
                        prev[c % 2] = name
                    if c == 1:
                        split_to(group_of["b_in", name][1] + SPL - 1)
                        act.wait_ge(fox_dve, 1)
                        own(nc.scalar.activation(fx[:, F_E, :], fx[:, F_E, :], ACT.Exp))
                        tell(nc.scalar.activation(fx[:, F_E, :], fx[:, F_E, :], ACT.Ln, bias=1.0), fox_act)
                    headed(name)
                def scores(u):
                    kind, hh = HEADS2[u]
                    x = heads_in[:, u % 8, :]
                    if kind == "sb":
                        if u >= 8:
                            result(("out", u - 8))
                        b = batch(("z", u))
                        own(nc.scalar.activation(x[:, 0:3 * P], b[:, 0:3 * P], ACT.Copy, scale=SB_HD ** -0.5))
                        l = x[:, 3 * P:6 * P]
                        tell(nc.scalar.activation(l, b[:, 0:3 * P], ACT.Abs, scale=SB_HD ** -0.5), tp_free["A"])
                        own(nc.scalar.activation(l, l, ACT.Exp, scale=-1.0))
                        tell(nc.scalar.activation(l, l, ACT.Ln, bias=1.0), sb_l)

                def softmax_exp(u):
                    kind, hh = HEADS2[u]
                    if kind != "sb":
                        x = heads_in[:, u % 8, :]
                        act.wait_ge(sm_z, softmax_number(u))
                        for tt, cols in enumerate(QUERY_TILES[kind]):
                            tell(nc.scalar.activation(x[:, cols], x[:, cols], ACT.Exp, bias=st[:, u % 8 * 2 + tt, 0:1],
                                                      accum_out=st[:, u % 8 * 2 + tt, 1:2]), sm_p if tt else a_own)

                def turned(u):
                    kind, hh = HEADS2[u]
                    if kind != "sb":
                        n = (3 if kind == "fx" else 4) * P
                        tell(nc.scalar.activation(heads_in[:, u % 8, 0:n], batch(("second", u))[:, 0:n], ACT.Copy),
                             tp_free["A"])

                def sb_exp(u):
                    kind, hh = HEADS2[u]
                    if kind == "sb":
                        act.wait_ge(sb_a, hh + 1)
                        x = heads_in[:, u % 8, 0:3 * P]
                        tell(nc.scalar.activation(x, x, ACT.Exp), sb_wx)

                for u in range(len(HEADS2) + 3):
                    for do, v in ((softmax_exp, u - 1), (sb_exp, u - 3), (scores, u), (turned, u - 2)):
                        if 0 <= v < len(HEADS2):
                            do(v)
                split_to(group_of["b_gate", 0, 0][1] + SPL - 1)
                for br in range(3):
                    for j in range(2):
                        b = batch(("oT", br, j))
                        tell(nc.scalar.activation(oT1[br][:, 2 * j:2 * j + 2, :],
                                                  b[:, :].rearrange("p (a b) -> p a b", a=2), ACT.Copy), hi_out)
                last_branch = None
                for c in range(2):
                    for br in range(3):
                        banks = after(("b_gate", br, c))
                        if last_branch:
                            act.wait_ge(acc_free["D"], group_of[last_branch][3])
                            act.wait_ge(merged, last_branch[1] + 3 * last_branch[2] + 1)
                        last_branch = ("branch", br, c)
                        for tt in range(NT):
                            tell(nc.scalar.activation(gate2[:, tt, :], banks[tt][:, :], ACT.Sigmoid,
                                                      scale=root("m2", tt)), acc_free["A"] if tt else a_own)
                split_to(group_of["branch", 2, 1][1] + SPL)
                norm_turn("mg", None)
                split_to(group_of[("b_out", 1)][1] + SPL)
                norm_turn("m3", "mlp2")
                whole(("b_out", 1))
                norm_root("m3", h)
                norm_used("m3")
                for hf in range(2):
                    def turned(b):
                        for tt in range(NT):
                            bk = batch((("fhid", hf, b), tt))
                            tell(nc.scalar.activation(hid1[:, 4 * b:4 * b + 4, tt * P:tt * P + P],
                                                      bk[:, :].rearrange("p (k c) -> p k c", k=4), ACT.Copy), hi_out)

                    for b in range(4):
                        banks = after(("f_up", hf, b))
                        if hf or b:
                            act.wait_ge(relu_sq, 2 * (4 * hf + b))
                        for tt in range(NT):
                            tell(nc.scalar.activation(gate_s[:, tt, :], banks[tt][:, :], ACT.Relu,
                                                      scale=root("m3", tt)), acc_free["A"] if tt else a_own)
                        if b:
                            turned(b - 1)
                    split_to(cbs["f_down", hf, 0][0] + SPL)
                    turned(3)
                split_to(len(stream))

            act.wait_ge(x_in, 16)
            split_to(1)
            norm_turn("n0", "mix0")
            split_to(SPL)
            norm_root("n0", h)
            norm_used("n0")
            for c in range(2):
                banks = after(("pool_in", c))
                for tt in range(NT):
                    tell(nc.scalar.activation(pool_u[:, tt, c * CB:c * CB + CB], banks[tt][:, :], ACT.Copy,
                                              scale=root("n0", tt)), acc_free["A"] if tt else a_own)
            for g in range(4):
                b = batch(("pool", g))
                tell(nc.scalar.activation(xT1[:, 2 * g:2 * g + 2, :], b[:, :].rearrange("p (a b) -> p a b", a=2),
                                          ACT.Copy), hi_out)
            act.wait_ge(setup, SETUP)
            tell(nc.scalar.activation(narrow_hi[:, :, :], narrow[:, :, :], ACT.Copy), narrow_split)
            split_to(cbs["pool_out", 1][1] + SPL)
            norm_turn("n1", "ffn0")
            act.wait_ge(h_done, 4)
            norm_root("n1", h)
            norm_used("n1")
            last_up = None
            for hf, (f0, blocks) in enumerate(FF_HALVES):
                nb = len(blocks)

                def hidden(b):
                    for tt in range(NT):
                        bk = batch((("hid", hf, b), tt))
                        n = cbs["up", hf, b][2] // P
                        tell(nc.scalar.activation(hid1[:, 4 * b:4 * b + n, tt * P:tt * P + P],
                                                  bk[:, 0:n * P].rearrange("p (k c) -> p k c", k=n), ACT.Copy), hi_out)

                for b in range(nb):
                    banks = after(("gate", hf, b))
                    n = cbs["gate", hf, b][2]
                    if last_up:
                        act.wait_ge(acc_free["D"], group_of[last_up][3])
                    last_up = ("up", hf, b)
                    for tt in range(NT):
                        tell(nc.scalar.activation(gate_s[:, tt, 0:n], banks[tt][:, 0:n], ACT.Silu, scale=root("n1", tt)),
                             acc_free["A"] if tt else a_own)
                    if b:
                        hidden(b - 1)
                split_to(cbs["down", hf, 0][0] + SPL)
                hidden(nb - 1)
            split_to(group_of[("down", 1, 1)][1] + SPL)
            norm_turn("n2", "mix1")
            whole(("down", 1, 1))
            norm_root("n2", h)
            deltanet()
            experts()
            second_block()

        @block.vector
        def _(dve):
            dve.wait_ge(first_in, 32)
            told = {}
            state = {"split": 0, "limit": NA, "own": 0, "hi": 0, "sq": 0, "rs": 0, "acc": 0}

            def tell(ins, signal):
                told[signal] = told.get(signal, 0) + 1
                ins.then_inc(signal, 1)
                dve.wait_ge(signal, told[signal])

            def own(ins):
                tell(ins, d_own)

            def split_to(n):
                n = min(n, state["limit"])
                for i in range(state["split"], n):
                    _, kc, w = stream[i]
                    dve.wait_ge(split_hi, i + 1)
                    nc.vector.tensor_tensor(w_lo[:, i % SPL, 0:kc * w], raw[:, i % RAW, 0:kc * w],
                                            w_hi[:, i % SPL, 0:kc * w], ALU.subtract).then_inc(split_lo, 1)
                state["split"] = max(n, state["split"])

            def after(name):
                banks, end = group_of[name][:2]
                split_to(end + SPL - 1)
                dve.wait_ge(used, end)
                return banks

            def high(n=1):
                state["hi"] += n
                dve.wait_ge(hi_out, state["hi"])

            def norm_root(tag):
                ss, v, y, u = (cells(tag, j) for j in range(4))
                k = NORMS.index(tag) + 1
                dve.wait_ge(sq_done, 2 * k)
                tell(nc.vector.tensor_scalar(v, ss, 1.0 / D, EPS, ALU.mult, ALU.add), v_done)
                dve.wait_ge(rs_done, k)
                own(nc.vector.tensor_tensor(u, y, y, ALU.mult))
                own(nc.vector.tensor_tensor(u, u, v, ALU.mult))
                own(nc.vector.tensor_scalar(u, u, -0.5, 1.5, ALU.mult, ALU.add))
                tell(nc.vector.tensor_tensor(y, y, u, ALU.mult), norm_ready)

            def norm_turn(tag, gain, step=1):
                for p in range(KD // 2):
                    b = batch_of[tag, p][0]
                    if gain is None:
                        high()
                        tell(nc.vector.tensor_tensor(xT2[:, 2 * p:2 * p + 2, :],
                                                     b[:, :].rearrange("p (a b) -> p a b", a=2),
                                                     xT1[:, 2 * p:2 * p + 2, :].bitcast(F32), ALU.subtract),
                             tp_free["D"])
                        continue
                    high(2)
                    for j in range(2):
                        tell(nc.vector.scalar_tensor_tensor(
                            out=xT2[:, 2 * p + j, :], in0=b[:, j * S:j * S + S], scalar=G(gain, step * (2 * p + j)),
                            in1=xT1[:, 2 * p + j, :].bitcast(F32), op0=ALU.mult, op1=ALU.subtract),
                            tp_free["D"] if j else d_own)

            def result(name):
                _, _, owner, n = batch_of[name]
                dve.wait_ge(tp_free[owner], n)

            def batch(name):
                b, n, owner, m = batch_of[name]
                assert owner == "D" and m == told.get(tp_free["D"], 0) + 1, name
                dve.wait_ge(tp_done, n)
                return b

            def narrow_batch(name, cols):
                n = cols.stop - cols.start
                tell(nc.vector.tensor_copy(narrow_T[0:n, :], batch((name, "T"))[0:n, 0:S]), tp_free["D"])
                return batch(name)

            def bank4(name):
                return batch(name)[:, :].rearrange("p (a b) -> p a b", a=4)

            def newton(y, v, u):
                own(nc.vector.tensor_tensor(u, y, y, ALU.mult))
                own(nc.vector.tensor_tensor(u, u, v, ALU.mult))
                own(nc.vector.tensor_scalar(u, u, -0.5, 1.5, ALU.mult, ALU.add))
                own(nc.vector.tensor_tensor(y, y, u, ALU.mult))

            def deltanet():
                def wide(v):
                    return dnv[:, v, :].rearrange("p (t h) -> p t h", t=NT)

                def conv(c):
                    for j in range(2):
                        b = batch(("conv", c, j))
                        high(2)
                        for back in range(1, CONV):
                            for k in range(2):
                                dve.wait_ge(d_own, told[d_own] - (back > 1))
                                ch = 4 * c + 2 * j + k
                                o = qkvT[ch // 8][:, ch % 8, back:S]
                                end = k == 1 and back == CONV - 1
                                nc.vector.scalar_tensor_tensor(
                                    out=o, in0=b[:, k * S:k * S + S - back], scalar=G("conv", 4 * ch + 3 - back),
                                    in1=o, op0=ALU.mult, op1=ALU.add).then_inc(tp_free["D"] if end else d_own, 1)
                                told[tp_free["D"] if end else d_own] += 1
                        dve.wait_ge(d_own, told[d_own])
                        dve.wait_ge(tp_free["D"], told[tp_free["D"]])

                state["limit"] = cbs["dn_in", 7][1]
                for c in range(8):
                    split_to(group_of["dn_in", c][1] + SPL - 1)
                    if c == 0:
                        b = narrow_batch("ba", BA)
                        ba = b[:, 0:32].rearrange("p (t a h) -> p t a h", t=NT, a=2)
                        roots = cells("n2", 2).unsqueeze(2).broadcast_to((P, NT, 8))
                        own(nc.vector.tensor_tensor(wide(V_X), ba[:, :, 1, :], roots, ALU.mult))
                        tell(nc.vector.tensor_tensor(wide(V_BETA), ba[:, :, 0, :], roots, ALU.mult), tp_free["D"])
                        own(nc.vector.tensor_tensor(wide(V_X), wide(V_X), R("dt").unsqueeze(1).broadcast_to((P, NT, 8)), ALU.add))
                        own(nc.vector.tensor_scalar(dnv[:, V_M, :], dnv[:, V_X, :], 0.0, None, ALU.max))
                        tell(nc.vector.scalar_tensor_tensor(out=dnv[:, V_E, :], in0=dnv[:, V_M, :], scalar=-2.0,
                                                            in1=dnv[:, V_X, :], op0=ALU.mult, op1=ALU.add), small_dve)
                        dve.wait_ge(small_act, 1)
                        own(nc.vector.tensor_scalar(dnv[:, V_BETA, :], dnv[:, V_BETA, :], 1.0, None, ALU.add))
                        own(nc.vector.reciprocal(dnv[:, V_BETA, :], dnv[:, V_BETA, :]))
                        own(nc.vector.tensor_tensor(dnv[:, V_M, :], dnv[:, V_M, :], dnv[:, V_E, :], ALU.add))
                        tell(nc.vector.scalar_tensor_tensor(out=wide(V_G), in0=wide(V_M), scalar=-1.0,
                                                            in1=dnv[:, V_EA, 0:8].unsqueeze(1).broadcast_to((P, NT, 8)),
                                                            op0=ALU.mult, op1=ALU.mult), small_dve)
                    if c == 6:
                        b = batch("ssq")
                        tell(nc.vector.tensor_scalar(dnv[:, V_SS:V_SS + 2, :].rearrange("p m (t h) -> p m t h", t=NT),
                                                     b[:, 0:32].rearrange("p (t m h) -> p m t h", t=NT, m=2),
                                                     EPS, None, ALU.add), tp_free["D"])
                        tell(nc.vector.memset(small[:, 70:71], 0.0), small_dve)
                    if 1 <= c <= 6:
                        conv(c - 1)
                    if c == 2:
                        b = batch("gc")
                        own(nc.vector.tensor_copy(dnv[:, V_GC:V_GC + 2, :], b[:, 0:32].rearrange("p (a b) -> p a b", a=2)))
                        tell(nc.vector.tensor_tensor(dnv[:, V_EKD, :], b[:, 16:32], dnv[:, V_GC, :], ALU.subtract),
                             tp_free["D"])
                        tell(nc.vector.memset(small[:, 70:71], 0.0), small_dve)
                    if c == 5:
                        tell(nc.vector.tensor_copy(narrow_T[0:2 * HEADS, :], batch("ssqT")[0:2 * HEADS, 0:S]),
                             tp_free["D"])
                    if c == 7:
                        dve.wait_ge(small_act, 2)
                        newton(dnv[:, V_R:V_R + 2, :], dnv[:, V_SS:V_SS + 2, :], dnv[:, V_TMP:V_TMP + 2, :])
                        tell(nc.vector.tensor_scalar(dnv[:, V_R, :], dnv[:, V_R, :], float(P) ** -0.5, None, ALU.mult),
                             rs_ready)
                        for m in range(2):
                            for p in range(4):
                                b = batch(("unit", m, p))
                                x = qkvT[m][:, 2 * p:2 * p + 2, :]
                                tell(nc.vector.tensor_tensor(x, b[:, :].rearrange("p (a b) -> p a b", a=2), x, ALU.mult),
                                     tp_free["D"])
                dve.wait_ge(small_act, 3)

                def by_token(v, tt, hg):
                    return dnv[:, v, tt * 8 + 4 * hg:tt * 8 + 4 * hg + 4].unsqueeze(2).broadcast_to((P, 4, P))

                def by_head(m):
                    return m.unsqueeze(1).broadcast_to((P, 4, P))

                def level(l, tt, hg):
                    tell(nc.vector.tensor_tensor(buf["dec", tt, hg][:, :, :], buf["A", tt, hg][:, :, :],
                                                 by_head(C("levels")[:, l * P:l * P + P]), ALU.mult), inv_level)

                for tt in range(NT):
                    for hg in range(2):
                        dec = buf["dec", tt, hg][:, :, :]
                        tell(nc.vector.tensor_tensor(dec, bank4(("decay", tt, hg)), by_token(V_GC, tt, hg), ALU.subtract),
                             tp_free["D"])
                        tell(nc.vector.tensor_scalar(dec, dec, 0.0, None, ALU.min), dec_min)
                    for hg in range(2):
                        dec = buf["dec", tt, hg][:, :, :]
                        dve.wait_ge(dec_exp, 2 * tt + hg + 1)
                        own(nc.vector.tensor_tensor(dec, dec, by_head(C("upto")), ALU.mult))
                        a = buf["A", tt, hg][:, :, :]
                        tell(nc.vector.tensor_tensor(a, bank4(("kk", tt, hg)), dec, ALU.mult), tp_free["D"])
                        tell(nc.vector.tensor_tensor(a, bank4(("beta", tt, hg)), a, ALU.mult), tp_free["D"])
                        tell(nc.vector.tensor_tensor(buf["qk", tt, hg][:, :, :], bank4(("qk", tt, hg)), dec, ALU.mult),
                             tp_free["D"])
                        TT = buf["TT", tt, hg][:, :, :]
                        own(nc.vector.tensor_tensor(TT, a, by_head(C("levels")[:, 0:P]), ALU.mult))
                        tell(nc.vector.tensor_tensor(TT, by_head(ident), TT, ALU.subtract), inv_first)
                        level(1, tt, hg)
                def head_sums(tt):
                    dve.wait_ge(o_squared, 3 + tt)
                    own(nc.vector.tensor_reduce(dnv[:, V_SS, 8 * tt:8 * tt + 8],
                                                o_sq[tt][:, :].rearrange("p (a b) -> p a b", a=HEADS), AX, ALU.add))

                for l in range(1, len(LEVELS)):
                    for tt in range(NT):
                        for hg in range(2):
                            T, TT = buf["T", tt, hg][:, :, :], buf["TT", tt, hg][:, :, :]
                            if l < len(LEVELS) - 1:
                                tell(nc.vector.tensor_tensor(T, T, bank4(("inv_T", tt, hg, l)), ALU.subtract), tp_free["D"])
                            tell(nc.vector.tensor_tensor(TT, TT, bank4(("inv_TT", tt, hg, l)), ALU.subtract), tp_free["D"])
                            if l < len(LEVELS) - 1:
                                level(l + 1, tt, hg)
                for tt in range(NT):
                    for hg in range(2):
                        r = buf["A", tt, hg][:, :, :]
                        v = vn[:, tt, 4 * hg:4 * hg + 4, :]
                        if tt:
                            tell(nc.vector.tensor_tensor(r, bank4(("kS", tt, hg)), by_token(V_EGC, tt, hg), ALU.mult),
                                 tp_free["D"])
                            own(nc.vector.tensor_tensor(r, v, r, ALU.subtract))
                            v = r
                            o = xn[:, tt, hg * CB:hg * CB + CB].rearrange("p (a b) -> p a b", a=4)
                            tell(nc.vector.tensor_tensor(o, bank4(("qS", tt, hg)), by_token(V_EGC, tt, hg), ALU.mult),
                                 tp_free["D"])
                        tell(nc.vector.tensor_tensor(r, v, by_token(V_BETA, tt, hg), ALU.mult), rhs_done)
                        if tt == 0:
                            tell(nc.vector.tensor_tensor(buf["T", tt, hg][:, :, :], kn[:, tt, 4 * hg:4 * hg + 4, :],
                                                         by_token(V_EKD, tt, hg), ALU.mult), kdec_done)
                    if tt:
                        head_sums(0)
                        own(nc.vector.tensor_tensor(xn[:, 0, :], xn[:, 0, :], z_s[:, 0, :], ALU.mult))
                    for hg in range(2):
                        o = xn[:, tt, hg * CB:hg * CB + CB].rearrange("p (a b) -> p a b", a=4)
                        if tt:
                            tell(nc.vector.tensor_tensor(o, bank4(("o", tt, hg)), o, ALU.add), tp_free["D"])
                        else:
                            tell(nc.vector.tensor_copy(o, bank4(("o", tt, hg))), tp_free["D"])
                        tell(nc.vector.memset(small[:, 70:71], 0.0), o_done)
                state["limit"] = NA
                head_sums(1)
                tell(nc.vector.tensor_scalar(dnv[:, V_SS, :], dnv[:, V_SS, :], 1.0 / P, EPS, ALU.mult, ALU.add), small_dve)
                own(nc.vector.tensor_tensor(xn[:, 1, :], xn[:, 1, :], z_s[:, 1, :], ALU.mult))
                dve.wait_ge(small_act, 4)
                newton(dnv[:, V_R, :], dnv[:, V_SS, :], dnv[:, V_TMP, :])
                for tt in range(NT):
                    o = xn[:, tt, :].rearrange("p (a b) -> p a b", a=HEADS)
                    tell(nc.vector.tensor_tensor(o, o, dnv[:, V_R, 8 * tt:8 * tt + 8].unsqueeze(2).broadcast_to(
                        (P, HEADS, P)), ALU.mult), xn_done)
                split_to(cbs["dn_in", 7][1] + 1)
                norm_turn("o", "dn_norm", 0)
                for c in range(2):
                    add_to_h(("dn_out", c), c)

            def experts():
                norm_turn("n3", "ffn1")
                dve.wait_ge(gain_in, 16)
                for tt in range(NT):
                    tell(nc.vector.tensor_tensor(xn[:, tt, :], h[:, tt, :], R("scale"), ALU.mult), xn_done)
                b = narrow_batch("router", ROUTER)
                norm_root("n3")
                lg = rt[:, R_LG:R_LG + 2, :]
                tell(nc.vector.tensor_tensor(lg, b[:, 0:16].rearrange("p (a b) -> p a b", a=2),
                                             cells("n3", 2).unsqueeze(2).broadcast_to((P, NT, NE)), ALU.mult),
                     tp_free["D"])
                own(nc.vector.tensor_tensor(lg, lg, R("router_b").unsqueeze(1).broadcast_to((P, NT, NE)), ALU.add))
                jlt = C("jlt").rearrange("p (a b) -> p a b", a=NE)
                jlt2 = jlt.unsqueeze(1).broadcast_to((P, NT, NE, NE))
                big, tie = (rt[:, q:q + NT * NE, :].rearrange("p (t a) b -> p t a b", t=NT) for q in (R_BIG, R_TIE))
                other = lg.unsqueeze(2).broadcast_to((P, NT, NE, NE))
                this = lg.unsqueeze(3).broadcast_to((P, NT, NE, NE))
                own(nc.vector.tensor_tensor(tie, other, this, ALU.is_equal))
                own(nc.vector.tensor_tensor(tie, tie, jlt2, ALU.mult))
                own(nc.vector.tensor_tensor(big, other, this, ALU.is_gt))
                own(nc.vector.tensor_tensor(big, big, tie, ALU.add))
                own(nc.vector.tensor_reduce(rt[:, R_RANK:R_RANK + 2, :], big, AX, ALU.add))
                sel = rt[:, R_SEL:R_SEL + 2, :]
                tell(nc.vector.tensor_scalar(sel, rt[:, R_RANK:R_RANK + 2, :], TOP_K - 0.5, None, ALU.is_lt), route_dve)
                own(nc.vector.tensor_reduce(rt[:, R_MAX, 0:2], lg, AX, ALU.max))
                tell(nc.vector.tensor_tensor(rt[:, R_EXP:R_EXP + 2, :], lg,
                                             rt[:, R_MAX, 0:2].unsqueeze(2).broadcast_to((P, NT, NE)), ALU.subtract),
                     route_dve)
                b = batch("places")
                place = item_pos[:, :, 0:NE]
                cnt = rt[:, R_CNT, :]
                own(nc.vector.tensor_scalar(cnt, b[:, 16:24], P + 0.5, None, ALU.is_gt))
                tell(nc.vector.scalar_tensor_tensor(out=rt[:, R_LG:R_LG + 2, :],
                                                    in0=b[:, 0:16].rearrange("p (a b) -> p a b", a=2), scalar=1.0,
                                                    in1=sel, op0=ALU.add, op1=ALU.mult), tp_free["D"])
                own(nc.vector.tensor_scalar(place, lg, 1.0, None, ALU.subtract))

                def choose(item, done, what=(0, 1)):
                    for dst, value in ((pick, lambda tt: root("n3", tt)), (pick_gate, lambda tt: item_gate[:, tt, item])):
                        for tt in range(NT):
                            if (dst is pick_gate) in what:
                                done(nc.vector.tensor_scalar(dst[:, tt, :], C("iota"), item_pos[:, tt, item], value(tt),
                                                             ALU.is_equal, ALU.mult))

                choose(slice(0, 1), lambda ins: tell(ins, picked0), (0,))
                dve.wait_ge(route_act, 1)
                gate = rt[:, R_EXP:R_EXP + 2, :]
                own(nc.vector.tensor_tensor(gate, gate, sel, ALU.mult))
                own(nc.vector.tensor_reduce(rt[:, R_MAX, 2:4], gate, AX, ALU.add))
                own(nc.vector.reciprocal(rt[:, R_MAX, 2:4], rt[:, R_MAX, 2:4]))
                own(nc.vector.tensor_tensor(item_gate[:, :, 0:NE], gate,
                                            rt[:, R_MAX, 2:4].unsqueeze(2).broadcast_to((P, NT, NE)), ALU.mult))
                choose(slice(0, 1), lambda ins: tell(ins, picked0), (1,))
                more = MAX_ITEMS - NE
                own(nc.vector.tensor_tensor(tie[:, 0], cnt.unsqueeze(1).broadcast_to((P, NE, NE)), jlt, ALU.mult))
                own(nc.vector.tensor_reduce(rt[:, R_RANK, :], tie[:, 0], AX, ALU.add))
                own(nc.vector.memset(item_f[:, :], 0.0))
                own(nc.vector.tensor_copy(item_f[:, 0:NE], C("iota")[:, 0:NE]))
                own(nc.vector.tensor_reduce(item_f[:, 12:13], cnt, AX, ALU.add))
                own(nc.vector.tensor_scalar(item_f[:, 12:13], item_f[:, 12:13], float(NE), None, ALU.add))
                own(nc.vector.tensor_scalar(item_f[:, 13:14], item_f[:, 12:13], 1.0, None, ALU.subtract))
                own(nc.vector.memset(item_pos[:, :, 11:12], -1.0))
                ind = rt[:, R_IND:R_IND + more, :]
                own(nc.vector.tensor_tensor(ind, C("iota")[:, 0:more].unsqueeze(2).broadcast_to((P, more, NE)),
                                            rt[:, R_RANK, :].unsqueeze(1).broadcast_to((P, more, NE)), ALU.is_equal))
                own(nc.vector.tensor_tensor(ind, ind, cnt.unsqueeze(1).broadcast_to((P, more, NE)), ALU.mult))
                own(nc.vector.tensor_tensor(rt[:, R_TMP:R_TMP + more, :], ind,
                                            C("iota")[:, 0:NE].unsqueeze(1).broadcast_to((P, more, NE)), ALU.mult))
                own(nc.vector.tensor_reduce(item_f[:, NE:NE + more], rt[:, R_TMP:R_TMP + more, :], AX, ALU.add))
                tell(nc.vector.tensor_copy(item_i[:, :], item_f[:, :]), items_ready)
                for q, table in ((R_BIG, item_pos), (R_TIE, item_gate)):
                    x = rt[:, q:q + NT * more, :].rearrange("p (t r) e -> p t r e", t=NT)
                    own(nc.vector.tensor_tensor(x, table[:, :, 0:NE].unsqueeze(2).broadcast_to((P, NT, more, NE)),
                                                ind.unsqueeze(1).broadcast_to((P, NT, more, NE)), ALU.mult))
                    own(nc.vector.tensor_reduce(table[:, :, NE:NE + more], x, AX, ALU.add))
                own(nc.vector.tensor_scalar(item_pos[:, :, NE:NE + more], item_pos[:, :, NE:NE + more], float(P), None,
                                            ALU.subtract))
                tell(nc.vector.memset(item_gate[:, :, 11:12], 0.0), m_lo)
                tell(nc.vector.memset(y_s[:, :, :], 0.0), m_y)
                tell(nc.vector.memset(spread[:, :, :], 0.0), m_read)

                for half in range(2):
                    b = batch(("gather", half))
                    high()
                    tell(nc.vector.tensor_tensor(xT2[:, 4 * half:4 * half + 4, 0:P],
                                                 b[:, :].rearrange("p (a b) -> p a b", a=4),
                                                 xT1[:, 4 * half:4 * half + 4, 0:P].bitcast(F32), ALU.subtract),
                         tp_free["D"])

                def split(j, i):
                    dve.wait_ge(m_hi, i * MT + (j + 1))
                    nc.vector.tensor_tensor(w_lo[:, j % SPL, :], raw[:, j % RAW, :], w_hi[:, j % SPL, :],
                                            ALU.subtract).then_inc(m_lo, 1)

                for j in range(SPL):
                    split(j, 0)
                norm_root("mm")
                n = n_items(dve)
                with dve.Fori(0, n) as i:
                    at_ = [SPL]
                    reads = [0]

                    def split_until(j):
                        for k in range(at_[0], j):
                            split(k, i)
                        at_[0] = max(at_[0], j)

                    def read(ins):
                        reads[0] += 1
                        ins.then_inc(m_read, 1)
                        dve.wait_ge(m_read, i * M_READS + (reads[0] + 1))

                    def turned(f):
                        bi = TURN + f if f < 6 else TURN6
                        dve.wait_ge(m_turned, i * 9 + (f + 1 if f < 6 else 9))
                        cols = slice(4 * f * P, 4 * (f + 1) * P)
                        read(nc.vector.tensor_tensor(hidden2[:, cols], tp[bi % 4][:, :], hidden1[:, cols].bitcast(F32),
                                                     ALU.subtract))

                    def scattered(bi, c):
                        for tt in range(NT):
                            dve.wait_ge(m_tp, i * M_BANKS + (bi + tt + 1))
                            hh = h[:, tt, c * CB:c * CB + CB]
                            read(nc.vector.tensor_tensor(hh, tp[(bi + tt) % 4][:, :], hh, ALU.add))

                    for f in range(FB):
                        split_until(4 * f + 2 + SPL - 1)
                        if f == 0:
                            scattered(SC1, 1)
                        else:
                            turned(f - 1)
                        split_until(4 * f + 4 + SPL - 1)
                        dve.wait_ge(m_used, i * MT + (4 * f + 4))
                        dve.wait_ge(m_gate, i * FB + (f + 1))
                        if f > 1:
                            dve.wait_ge(m_tp, i * M_BANKS + (TURN + f - 1))
                        nc.vector.tensor_tensor(hnat[:, f % 2, :], acc[2 * (f % 2) + 1][:, :], gate_s[:, f % 2, :],
                                                ALU.mult).then_inc(m_up, 1)
                        if f == FB - 2:
                            picks = [0]

                            def done(ins):
                                picks[0] += 1
                                ins.then_inc(m_pick, 1)
                                dve.wait_ge(m_pick, i * 4 + picks[0])

                            choose(bass.ds(i + 1, 1), done)
                    for half in range(2):
                        bi = GATHER + half
                        dve.wait_ge(m_turned, i * 9 + (7 + half))
                        read(nc.vector.tensor_tensor(xT2[:, 4 * half:4 * half + 4, 0:P],
                                                     tp[bi % 4][:, :].rearrange("p (a b) -> p a b", a=4),
                                                     xT1[:, 4 * half:4 * half + 4, 0:P].bitcast(F32), ALU.subtract))
                    split_until(4 * FB + 1 + SPL - 1)
                    turned(FB - 1)
                    split_until(5 * FB + 2 + SPL - 1)
                    scattered(SC0, 0)
                    split_until(MT + SPL)
                    assert reads[0] == M_READS
                for tt in range(NT):
                    dve.wait_ge(m_tp, n * M_BANKS + (tt + 1))
                    hh = h[:, tt, CB:D]
                    ins = nc.vector.tensor_tensor(hh, tp[tt][:, :], hh, ALU.add)
                    if tt:
                        tell(ins, moe_done)
                    else:
                        own(ins)

            def second_block():
                state["limit"] = len(stream)
                norm_turn("mm", "mem2")
                split_to(NA + SPL)
                norm_root("fin")
                for tt in range(NT):
                    tell(nc.vector.scalar_tensor_tensor(out=h[:, tt, :], in0=h[:, tt, :], scalar=root("fin", tt),
                                                        in1=R("final"), op0=ALU.mult, op1=ALU.mult), h_done)

                def headed(name):
                    dst, size, gain = HEADED[name]
                    if size:
                        q = NORMED.index(name)
                        n = NT * CB // size
                        dve.wait_ge(h_square, 2 * (q + 1))
                        own(nc.vector.tensor_reduce(hs[:, 0, 0:n], head_sq[:, :, :].rearrange(
                            "p t (a b) -> p (t a) b", b=size), AX, ALU.add))
                        tell(nc.vector.tensor_scalar(hs[:, 0, 0:n], hs[:, 0, 0:n], 1.0 / size, EPS, ALU.mult, ALU.add),
                             h_sq_v)
                        dve.wait_ge(h_rs, q + 1)
                        newton(hs[:, 1, 0:n], hs[:, 0, 0:n], hs[:, 2, 0:n])
                        if name in ("fxq", "mq"):
                            own(nc.vector.tensor_scalar(hs[:, 1, 0:n], hs[:, 1, 0:n], float(size) ** -0.5, None, ALU.mult))
                        x = xn[:, STAGE[name], :].rearrange("p (a b) -> p a b", b=size)
                        tell(nc.vector.tensor_tensor(x, x, hs[:, 1, 0:n].unsqueeze(2).broadcast_to((P, n, size)),
                                                     ALU.mult), h_scaled)

                def turned(name):
                    dst, size, gain = HEADED[name]
                    for j in range(2):
                        b = batch(("heads", name, j))[:, :].rearrange("p (a b) -> p a b", a=2)
                        o = dst[:, 2 * j:2 * j + 2, :]
                        tell(nc.vector.tensor_scalar(o, b, G(gain), None, ALU.mult) if size
                             else nc.vector.tensor_copy(o, b), tp_free["D"])

                split_to(group_of["b_in", "mv"][1] + SPL - 1)
                norm_turn("m2", "mix2")
                norm_root("m2")
                headed("mk")
                state["limit"] = cbs["b_in", B_IN[-1][0]][1]
                for c, (name, _) in enumerate(B_IN):
                    split_to(group_of["b_in", name][1] + SPL - 1)
                    if c == 2:
                        b = batch("cumf")
                        tell(nc.vector.tensor_copy(fx[:, F_CUM, :], b[:, 0:16]), tp_free["D"])
                    if c == 0:
                        turned("mk")
                    elif B_IN[c - 1][0] in HEADED:
                        turned(B_IN[c - 1][0])
                    if c == 1:
                        wide = lambda v: fx[:, v, :].rearrange("p (t h) -> p t h", t=NT)
                        b = narrow_batch("forget", FORGET)
                        tell(nc.vector.tensor_tensor(wide(F_NLF), b[:, 0:16].rearrange("p (t h) -> p t h", t=NT),
                                                     cells("m2", 2).unsqueeze(2).broadcast_to((P, NT, 8)), ALU.mult),
                             tp_free["D"])
                        own(nc.vector.tensor_tensor(wide(F_NLF), wide(F_NLF),
                                                    R("forget").unsqueeze(1).broadcast_to((P, NT, 8)), ALU.add))
                        own(nc.vector.tensor_scalar(fx[:, F_M, :], fx[:, F_NLF, :], -1.0, 0.0, ALU.mult, ALU.max))
                        own(nc.vector.tensor_scalar(fx[:, F_NLF, :], fx[:, F_NLF, :], -1.0, None, ALU.mult))
                        tell(nc.vector.scalar_tensor_tensor(out=fx[:, F_E, :], in0=fx[:, F_M, :], scalar=-2.0,
                                                            in1=fx[:, F_NLF, :], op0=ALU.mult, op1=ALU.add), fox_dve)
                        dve.wait_ge(fox_act, 1)
                        tell(nc.vector.tensor_tensor(fx[:, F_NLF, :], fx[:, F_M, :], fx[:, F_E, :], ALU.add), fox_dve)
                    if name in HEADED:
                        headed(name)
                mask = C("before")

                def scores(u):
                    kind, hh = HEADS2[u]
                    x = heads_in[:, u % 8, :]
                    if kind == "sb":
                        return
                    b = batch(("z", u))
                    if kind == "fx":
                        c0, c1 = fx[:, F_CUM, hh:hh + 1], fx[:, F_CUM, 8 + hh:9 + hh]
                        own(nc.vector.scalar_tensor_tensor(out=x[:, 0:P], in0=b[:, 0:P], scalar=c0, in1=C("future"),
                                                           op0=ALU.subtract, op1=ALU.add))
                        own(nc.vector.tensor_scalar(x[:, P:S], b[:, P:S], c1, None, ALU.subtract))
                        tell(nc.vector.scalar_tensor_tensor(out=x[:, S:3 * P], in0=b[:, S:3 * P], scalar=c1,
                                                            in1=C("future"), op0=ALU.subtract, op1=ALU.add), tp_free["D"])
                    else:
                        tell(nc.vector.tensor_copy(x[:, 0:2 * S], b[:, :]), tp_free["D"])
                    for tt, cols in enumerate(QUERY_TILES[kind]):
                        mx = st[:, u % 8 * 2 + tt, 0:1]
                        own(nc.vector.tensor_reduce(mx, x[:, cols], AX, ALU.max))
                        tell(nc.vector.tensor_scalar(mx, mx, -1.0, None, ALU.mult), sm_z if tt else d_own)

                def second(u):
                    kind, hh = HEADS2[u]
                    if kind == "sb":
                        z = heads_in[:, u % 8, 0:3 * P]
                        tell(nc.vector.tensor_tensor(z, z, batch(("second", u))[:, 0:3 * P], ALU.subtract), tp_free["D"])
                        tell(nc.vector.tensor_scalar(z, z, 0.0, None, ALU.min), sb_a)

                def softplus(u):
                    kind, hh = HEADS2[u]
                    if kind == "sb":
                        dve.wait_ge(sb_l, hh + 1)
                        z, sp_ = heads_in[:, u % 8, 0:3 * P], heads_in[:, u % 8, 3 * P:6 * P]
                        own(nc.vector.scalar_tensor_tensor(out=sp_, in0=z, scalar=0.0, in1=sp_, op0=ALU.max, op1=ALU.add))
                        own(nc.vector.tensor_tensor(sp_[:, 0:P], sp_[:, 0:P], mask, ALU.mult))
                        tell(nc.vector.tensor_tensor(sp_[:, 2 * P:3 * P], sp_[:, 2 * P:3 * P], mask, ALU.mult), sb_sp)

                def weights(u):
                    kind, hh = HEADS2[u]
                    if kind == "sb":
                        dve.wait_ge(sb_wx, hh + 1)
                        w = heads_in[:, u % 8, 0:3 * P]
                        own(nc.vector.tensor_tensor(w[:, 0:P], w[:, 0:P], mask, ALU.mult))
                        tell(nc.vector.tensor_tensor(w[:, 2 * P:3 * P], w[:, 2 * P:3 * P], mask, ALU.mult), sb_w)

                def output(u):
                    kind, hh = HEADS2[u]
                    n = WIDTH[kind]
                    b = batch(("out", u))
                    if kind == "sb":
                        tell(nc.vector.tensor_copy(o_sb[:, :, hh * n:hh * n + n],
                                                   b[:, 0:2 * n].rearrange("p (t c) -> p t c", t=NT)), tp_free["D"])
                        return
                    q = st[:, u % 8 * 2:u % 8 * 2 + 2, 1:2]
                    own(nc.vector.reciprocal(q, q))
                    for tt in range(NT):
                        tell(nc.vector.tensor_scalar(O_OF[kind][:, tt, hh * n:hh * n + n], b[:, tt * n:tt * n + n],
                                                     st[:, u % 8 * 2 + tt, 1:2], None, ALU.mult),
                             tp_free["D"] if tt else d_own)

                for u in range(len(HEADS2) + 5):
                    for do, v in ((weights, u - 4), (output, u - 5), (scores, u), (softplus, u - 1), (second, u - 2)):
                        if 0 <= v < len(HEADS2):
                            do(v)
                state["limit"] = len(stream)
                split_to(group_of["b_gate", 0, 0][1] + SPL - 1)
                for br in range(3):
                    for j in range(2):
                        b = batch(("oT", br, j))
                        high()
                        tell(nc.vector.tensor_tensor(oT2[br][:, 2 * j:2 * j + 2, :],
                                                     b[:, :].rearrange("p (a b) -> p a b", a=2),
                                                     oT1[br][:, 2 * j:2 * j + 2, :].bitcast(F32), ALU.subtract),
                             tp_free["D"])
                for c in range(2):
                    for br in range(3):
                        banks = after(("branch", br, c))
                        dve.wait_ge(acc_free["A"], group_of["b_gate", br, c][3])
                        m = [xn[:, tt, c * CB:c * CB + CB] for tt in range(NT)]
                        for tt in range(NT):
                            o = gate2[:, tt, :] if br else m[tt]
                            tell(nc.vector.tensor_tensor(o, banks[tt][:, :], gate2[:, tt, :], ALU.mult),
                                 acc_free["D"] if tt else d_own)
                        if br:
                            for tt in range(NT):
                                tell(nc.vector.tensor_tensor(m[tt], m[tt], gate2[:, tt, :], ALU.add),
                                     d_own if tt == 0 else xn_done if br == 2 else d_own)
                        tell(nc.vector.memset(small[:, 70:71], 0.0), merged)
                norm_turn("mg", None)
                for c in range(2):
                    add_to_h(("b_out", c), c)
                norm_turn("m3", "mlp2")
                norm_root("m3")
                for hf in range(2):
                    def hidden(b):
                        for tt in range(NT):
                            bk = batch((("fhid", hf, b), tt))
                            high()
                            tell(nc.vector.tensor_tensor(hid2[:, 4 * b:4 * b + 4, tt * P:tt * P + P],
                                                         bk[:, :].rearrange("p (k c) -> p k c", k=4),
                                                         hid1[:, 4 * b:4 * b + 4, tt * P:tt * P + P].bitcast(F32),
                                                         ALU.subtract), tp_free["D"])

                    for b in range(4):
                        split_to(group_of["f_up", hf, b][1] + SPL - 1)
                        dve.wait_ge(acc_free["A"], group_of["f_up", hf, b][3])
                        if b:
                            hidden(b - 1)
                        for tt in range(NT):
                            tell(nc.vector.tensor_tensor(hnat[:, tt, :], gate_s[:, tt, :], gate_s[:, tt, :], ALU.mult),
                                 relu_sq)
                    split_to(cbs["f_down", hf, 0][0] + SPL)
                    hidden(3)
                    for c in range(2):
                        add_to_h(("f_down", hf, c), c)
                        if hf:
                            tell(nc.vector.memset(small[:, 70:71], 0.0), out_done)

            def add_to_h(name, c):
                banks = after(name)
                for tt in range(NT):
                    hh = h[:, tt, c * CB:c * CB + CB]
                    tell(nc.vector.tensor_tensor(hh, banks[tt][:, :], hh, ALU.add), acc_free["D"] if tt else d_own)

            split_to(1)
            norm_turn("n0", "mix0")
            split_to(SPL)
            norm_root("n0")
            split_to(cbs["pool_in", 1][1] + SPL - 1)
            for g in range(4):
                b = batch_of["pool", g][0]
                high()
                tell(nc.vector.tensor_tensor(xT2[:, 2 * g:2 * g + 2, :], b[:, :].rearrange("p (a b) -> p a b", a=2),
                                             xT1[:, 2 * g:2 * g + 2, :].bitcast(F32), ALU.subtract), tp_free["D"])
            dve.wait_ge(setup, SETUP)
            dve.wait_ge(narrow_split, 1)
            nc.vector.tensor_tensor(narrow_lo[:, :, :], narrow[:, :, :], narrow_hi[:, :, :], ALU.subtract)\
                .then_inc(narrow_split, 1)
            for c in range(2):
                banks = after(("pool_out", c))
                for tt in range(NT):
                    tell(nc.vector.tensor_tensor(pool_t[:, tt, :], banks[tt][:, :], R("scale")[:, c * CB:c * CB + CB],
                                                 ALU.mult), acc_free["D"] if tt else d_own)
                for tt in range(NT):
                    hh = h[:, tt, c * CB:c * CB + CB]
                    tell(nc.vector.tensor_tensor(hh, hh, pool_t[:, tt, :], ALU.add), h_done)
            split_to(cbs["pool_out", 1][1] + SPL)
            norm_turn("n1", "ffn0")
            norm_root("n1")
            for hf, (f0, blocks) in enumerate(FF_HALVES):
                nb = len(blocks)

                def hidden(b):
                    for tt in range(NT):
                        bk = batch_of[("hid", hf, b), tt][0]
                        n = cbs["up", hf, b][2] // P
                        high()
                        tell(nc.vector.tensor_tensor(hid2[:, 4 * b:4 * b + n, tt * P:tt * P + P],
                                                     bk[:, 0:n * P].rearrange("p (k c) -> p k c", k=n),
                                                     hid1[:, 4 * b:4 * b + n, tt * P:tt * P + P].bitcast(F32),
                                                     ALU.subtract), tp_free["D"])

                for b in range(nb):
                    if b:
                        split_to(group_of["gate", hf, b][1] + SPL - 1)
                        hidden(b - 1)
                    banks = after(("up", hf, b))
                    n = cbs["up", hf, b][2]
                    dve.wait_ge(acc_free["A"], group_of["gate", hf, b][3])
                    for tt in range(NT if b or hf else 0):
                        dve.wait_ge(tp_done, batch_of[("hid",) + before(hf, b), tt][1])
                    for tt in range(NT):
                        tell(nc.vector.scalar_tensor_tensor(out=hnat[:, tt, 0:n], in0=banks[tt][:, 0:n],
                                                            scalar=root("n1", tt), in1=gate_s[:, tt, 0:n],
                                                            op0=ALU.mult, op1=ALU.mult), acc_free["D"] if tt else d_own)
                split_to(cbs["down", hf, 0][0] + SPL)
                hidden(nb - 1)
                for c in range(2):
                    banks = after(("down", hf, c))
                    for tt in range(NT):
                        hh = h[:, tt, c * CB:c * CB + CB]
                        tell(nc.vector.tensor_tensor(hh, banks[tt][:, :], hh, ALU.add), acc_free["D"] if tt else d_own)
            norm_turn("n2", "mix1")
            norm_root("n2")
            deltanet()
            experts()
            second_block()


def layout(**x):
    a = {k: np.asarray(v) for k, v in x.items()}

    def columns(v):
        return np.asarray(v, np.float32).reshape(-1, P).T

    cols = [columns(a["norm_mix_g"][0]), columns(a["norm_ffn_g"][0]), columns(a["norm_mix_g"][1]),
            columns(a["norm_ffn_g"][1]), columns(a["g_mix_norm_2"][0]), columns(a["g_mem_norm_2"][0]),
            columns(a["g_mlp_norm_2"][0]),
            a["dn_conv_w"][0].reshape(CONV, 24, P).transpose(2, 1, 0).reshape(P, 96),
            columns(a["dn_norm_g"][0]), columns(a["g_mem_q_2"][0]), columns(a["g_mem_k_2"][0]),
            columns(np.concatenate([a["g_fox_q_2"][0]] * 2)), columns(np.concatenate([a["g_fox_k_2"][0]] * 2))]
    rows = [a["pool_scale"][0], a["final_norm_g"], a["dn_dt_bias"][0], a["dn_a_log"][0], a["moe_router_b"][0],
            a["b_forget_2"][0]]
    consts, pool = shape_constants()
    given = {"rows2": a["norm_ffn_g"][1][None, :], "consts": consts, "pool_mix": pool, "cols": np.concatenate(cols, axis=1),
             "rows": np.concatenate(rows)[None, :]}
    for k in STREAMED:
        given[k] = a[k]
    return given


STREAMED = ("x", "mem_2", "pool_w_in", "pool_w_group", "ffn_w_gate", "ffn_w_up", "ffn_w_down", "dn_w_in", "dn_w_out",
            "moe_router_w", "moe_w_gate", "moe_w_up", "moe_w_down", "w_in_2", "w_mem_kv_2", "w_branch_sb_2",
            "w_branch_fox_2", "w_branch_mem_2", "w_out_2", "w_ff_up_2", "w_ff_down_2")


def kernel(**inputs):
    import numpy as _np
    import concourse.bacc as _bacc
    from concourse import mybir as _mybir
    from concourse.bass_utils import run_bass_kernel_spmd as _run

    nc = _bacc.Bacc("TRN2", target_bir_lowering=False, num_devices=1)
    arrays = {f"in_{k}_dram": _np.ascontiguousarray(v) for k, v in layout(**inputs).items()}
    given = {k[3:-5]: nc.dram_tensor(k, v.shape, _mybir.dt.from_np(v.dtype), kind="ExternalInput").ap()
             for k, v in arrays.items()}
    out = nc.dram_tensor("out_0_dram", (1, S, D), _mybir.dt.float32, kind="ExternalOutput").ap()
    build(nc, given, out)
    r = _run(nc, [arrays], core_ids=[0])
    return r.results[0]["out_0_dram"]
```
